# Optimizing a Trainium2 kernel written in Bass

```python
import math
import jax, jax.numpy as jnp
from jax import lax
import numpy as np

D_MODEL = 1024
BATCH = 1
SEQ = 1024
DEPTH = 1

PLE_DIM = 256
EPS = 1e-6

GLA_HEADS = 4
GLA_DK = 64
GLA_DV = 128
GLA_RANK = 16
GLA_TAU = 16.0
GLA_CHUNK = 64
GLA_WIDTH = GLA_HEADS * GLA_DV

NSA_HEADS = 8
NSA_KV_HEADS = 2
NSA_GROUP = NSA_HEADS // NSA_KV_HEADS
NSA_DH = 64
NSA_WIDTH = NSA_HEADS * NSA_DH
NSA_KVW = NSA_KV_HEADS * NSA_DH
CMP_LEN = 32
CMP_STRIDE = 16
CMP_HIDDEN = 2 * NSA_DH
SLC_BLOCK = 64
SLC_TOPN = 16
WINDOW = 512
Q_BLOCK = 128
N_BRANCH = 3

ROPE_THETA = 500000.0
ROPE_DIM = NSA_DH // 4

MIX_WIDTH = GLA_WIDTH + NSA_WIDTH
SPLIT_SIZES = [
    GLA_HEADS * GLA_DK,
    GLA_HEADS * GLA_DK,
    GLA_WIDTH,
    GLA_RANK,
    GLA_WIDTH,
    NSA_WIDTH,
    NSA_KVW, NSA_KVW,
    NSA_KVW, NSA_KVW,
    NSA_KVW, NSA_KVW,
    NSA_HEADS * N_BRANCH,
    NSA_WIDTH,
]
IN_WIDTH = int(sum(SPLIT_SIZES))
SPLIT_POINTS = [int(v) for v in np.cumsum(SPLIT_SIZES)[:-1]]

kernel_name = "hymba_gla_nsa_sandwich_ple"

def rms_norm(x, gain):
    xf = x.astype(jnp.float32)
    y = xf * lax.rsqrt(jnp.mean(xf * xf, axis=-1, keepdims=True) + EPS)
    return (y * gain.astype(jnp.float32)).astype(x.dtype)

def rope_partial(x, pos):
    half = ROPE_DIM // 2
    inv = ROPE_THETA ** (-(jnp.arange(half, dtype=jnp.float32) * 2.0) / ROPE_DIM)
    ang = pos.astype(jnp.float32)[:, None] * inv[None, :]
    cos = jnp.cos(ang)[:, None, :]
    sin = jnp.sin(ang)[:, None, :]
    xr = x[..., :ROPE_DIM].astype(jnp.float32)
    x1, x2 = xr[..., :half], xr[..., half:]
    rot = jnp.concatenate([x1 * cos - x2 * sin, x2 * cos + x1 * sin], axis=-1)
    return jnp.concatenate([rot.astype(x.dtype), x[..., ROPE_DIM:]], axis=-1)

def gla_mixer(q, k, v, log_a):
    B, T = q.shape[0], q.shape[1]
    n = T // GLA_CHUNK

    def to_chunks(t):
        return t.astype(jnp.float32).reshape(B, n, GLA_CHUNK, *t.shape[2:]).swapaxes(0, 1)

    qc, kc, vc, gc = (to_chunks(t) for t in (q * (GLA_DK ** -0.5), k, v, log_a))
    causal = jnp.tril(jnp.ones((GLA_CHUNK, GLA_CHUNK), dtype=bool))[None, :, :, None, None]

    def step(S, inp):
        q_, k_, v_, g_ = inp
        b = jnp.cumsum(g_, axis=1)
        o_inter = jnp.einsum('bchk,bhkv->bchv', q_ * jnp.exp(b), S)
        diff = b[:, :, None] - b[:, None, :]
        decay = jnp.exp(jnp.where(causal, diff, -jnp.inf))
        att = jnp.einsum('bihk,bjhk,bijhk->bhij', q_, k_, decay)
        o_intra = jnp.einsum('bhij,bjhv->bihv', att, v_)
        b_last = b[:, -1]
        S = jnp.exp(b_last)[..., None] * S + jnp.einsum(
            'bjhk,bjhv->bhkv', k_ * jnp.exp(b_last[:, None] - b), v_)
        return S, o_inter + o_intra

    S0 = jnp.zeros((B, GLA_HEADS, GLA_DK, GLA_DV), jnp.float32)
    _, o = lax.scan(step, S0, (qc, kc, vc, gc))
    return o.swapaxes(0, 1).reshape(B, T, GLA_HEADS, GLA_DV)

def _take_blocks(kb, ix):
    return kb[ix]

_gather_blocks = jax.vmap(jax.vmap(_take_blocks))

def nsa_mixer(q, k_cmp, v_cmp, k_slc, v_slc, k_win, v_win, gates,
              cmp_pos_k, cmp_w1_k, cmp_w2_k, cmp_pos_v, cmp_w1_v, cmp_w2_v):
    B, T = q.shape[0], q.shape[1]
    f32 = jnp.float32
    pos = jnp.arange(T)
    q = rope_partial(q, pos) * (NSA_DH ** -0.5)
    k_slc = rope_partial(k_slc, pos)
    k_win = rope_partial(k_win, pos)

    n_cmp = (T - CMP_LEN) // CMP_STRIDE + 1
    blk_idx = np.arange(n_cmp)[:, None] * CMP_STRIDE + np.arange(CMP_LEN)[None, :]

    def compress(t, pos_emb, w1, w2):
        blocks = t[:, blk_idx] + pos_emb[None, None, :, None, :]
        flat = blocks.transpose(0, 1, 3, 2, 4).reshape(B, n_cmp, NSA_KV_HEADS, CMP_LEN * NSA_DH)
        return jax.nn.silu(flat @ w1) @ w2

    cmp_end_np = np.arange(n_cmp) * CMP_STRIDE + CMP_LEN - 1
    cmp_end = jnp.asarray(cmp_end_np)
    kc = rope_partial(compress(k_cmp, cmp_pos_k, cmp_w1_k, cmp_w2_k), cmp_end).astype(f32)
    vc = compress(v_cmp, cmp_pos_v, cmp_w1_v, cmp_w2_v).astype(f32)

    n_slc = T // SLC_BLOCK
    n_sel = min(SLC_TOPN, n_slc)
    cs = np.arange(n_cmp) * CMP_STRIDE
    ss = np.arange(n_slc) * SLC_BLOCK
    cmp_to_slc = jnp.asarray(((cs[:, None] < ss[None, :] + SLC_BLOCK) &
                              (cs[:, None] + CMP_LEN > ss[None, :])).astype(np.float32))
    ks_blk = k_slc.reshape(B, n_slc, SLC_BLOCK, NSA_KV_HEADS, NSA_DH).transpose(0, 3, 1, 2, 4)
    vs_blk = v_slc.reshape(B, n_slc, SLC_BLOCK, NSA_KV_HEADS, NSA_DH).transpose(0, 3, 1, 2, 4)

    kw_pad = jnp.pad(k_win, ((0, 0), (WINDOW, 0), (0, 0), (0, 0)))
    vw_pad = jnp.pad(v_win, ((0, 0), (WINDOW, 0), (0, 0), (0, 0)))
    slc_ids = jnp.arange(n_slc)

    def block(qb):
        q0 = qb * Q_BLOCK
        t = q0 + jnp.arange(Q_BLOCK)
        qblk = lax.dynamic_slice_in_dim(q, q0, Q_BLOCK, 1).astype(f32).reshape(
            B, Q_BLOCK, NSA_KV_HEADS, NSA_GROUP, NSA_DH)

        s = jnp.einsum('bqhgd,bihd->bhgqi', qblk, kc)
        valid = cmp_end[None, :] <= t[:, None]
        p_cmp = jax.nn.softmax(jnp.where(valid, s, -1e30), axis=-1) * valid
        o_cmp = jnp.einsum('bhgqi,bihd->bqhgd', p_cmp, vc)

        imp = jnp.einsum('bhgqi,ij->bhqj', p_cmp, cmp_to_slc)
        cur = t // SLC_BLOCK
        forced = (slc_ids[None, :] == 0) | (slc_ids[None, :] == cur[:, None]) | \
                 (slc_ids[None, :] == cur[:, None] - 1)
        imp = jnp.where(forced, 1e3, jnp.where(slc_ids[None, :] <= cur[:, None], imp, -1.0))
        _, sel = lax.top_k(imp, n_sel)
        k_g = _gather_blocks(ks_blk, sel).astype(f32)
        v_g = _gather_blocks(vs_blk, sel).astype(f32)
        s = jnp.einsum('bqhgd,bhqnld->bhgqnl', qblk, k_g)
        kpos = sel[..., None] * SLC_BLOCK + jnp.arange(SLC_BLOCK)
        m = (kpos <= t[None, None, :, None, None])[:, :, None]
        s = jnp.where(m, s, -1e30)
        p_slc = jax.nn.softmax(s.reshape(*s.shape[:4], n_sel * SLC_BLOCK), axis=-1).reshape(s.shape)
        o_slc = jnp.einsum('bhgqnl,bhqnld->bqhgd', p_slc, v_g)

        kw = lax.dynamic_slice_in_dim(kw_pad, q0, WINDOW + Q_BLOCK, 1).astype(f32)
        vw = lax.dynamic_slice_in_dim(vw_pad, q0, WINDOW + Q_BLOCK, 1).astype(f32)
        kpos_w = q0 - WINDOW + jnp.arange(WINDOW + Q_BLOCK)
        dist = t[:, None] - kpos_w[None, :]
        mw = (kpos_w[None, :] >= 0) & (dist >= 0) & (dist < WINDOW)
        s = jnp.einsum('bqhgd,bkhd->bhgqk', qblk, kw)
        p_win = jax.nn.softmax(jnp.where(mw, s, -1e30), axis=-1)
        o_win = jnp.einsum('bhgqk,bkhd->bqhgd', p_win, vw)

        g = lax.dynamic_slice_in_dim(gates, q0, Q_BLOCK, 1).astype(f32).reshape(
            B, Q_BLOCK, NSA_KV_HEADS, NSA_GROUP, N_BRANCH)
        o = g[..., 0:1] * o_cmp + g[..., 1:2] * o_slc + g[..., 2:3] * o_win
        return o.reshape(B, Q_BLOCK, NSA_WIDTH)

    out = lax.map(block, jnp.arange(T // Q_BLOCK))
    return out.transpose(1, 0, 2, 3).reshape(B, T, NSA_WIDTH)

def setup_inputs(seed: int = 0) -> dict:
    key = jax.random.key(seed)
    ks = jax.random.split(key, 24)
    f32 = jnp.float32

    def nrm(k, shape, scale):
        return jax.random.normal(k, shape, f32) * scale

    def gain(k, shape):
        return 1.0 + 0.01 * jax.random.normal(k, shape, f32)

    L = DEPTH
    return {
        "x": nrm(ks[0], (BATCH, SEQ, D_MODEL), 1.0),
        "p": nrm(ks[1], (DEPTH, BATCH, SEQ, PLE_DIM), 1.0),
        "pre_norm": gain(ks[2], (L, D_MODEL)),
        "w_in": nrm(ks[3], (L, D_MODEL, IN_WIDTH), D_MODEL ** -0.5),
        "gla_a_up": nrm(ks[4], (L, GLA_RANK, GLA_HEADS * GLA_DK), GLA_RANK ** -0.5),
        "gla_a_bias": nrm(ks[5], (L, GLA_HEADS * GLA_DK), 0.1),
        "gla_out_norm": gain(ks[6], (L, GLA_DV)),
        "cmp_pos_k": nrm(ks[7], (L, CMP_LEN, NSA_DH), 0.02),
        "cmp_w1_k": nrm(ks[8], (L, CMP_LEN * NSA_DH, CMP_HIDDEN), (CMP_LEN * NSA_DH) ** -0.5),
        "cmp_w2_k": nrm(ks[9], (L, CMP_HIDDEN, NSA_DH), CMP_HIDDEN ** -0.5),
        "cmp_pos_v": nrm(ks[10], (L, CMP_LEN, NSA_DH), 0.02),
        "cmp_w1_v": nrm(ks[11], (L, CMP_LEN * NSA_DH, CMP_HIDDEN), (CMP_LEN * NSA_DH) ** -0.5),
        "cmp_w2_v": nrm(ks[12], (L, CMP_HIDDEN, NSA_DH), CMP_HIDDEN ** -0.5),
        "w_out": nrm(ks[13], (L, MIX_WIDTH, D_MODEL), MIX_WIDTH ** -0.5),
        "post_norm": gain(ks[14], (L, D_MODEL)),
        "ple_proj": nrm(ks[15], (L, PLE_DIM, D_MODEL), PLE_DIM ** -0.5),
        "ple_gate": nrm(ks[16], (L, D_MODEL, D_MODEL), D_MODEL ** -0.5),
        "ple_norm": gain(ks[17], (L, D_MODEL)),
    }

def reference(x, p, pre_norm, w_in, gla_a_up, gla_a_bias, gla_out_norm,
              cmp_pos_k, cmp_w1_k, cmp_w2_k, cmp_pos_v, cmp_w1_v, cmp_w2_v,
              w_out, post_norm, ple_proj, ple_gate, ple_norm):
    B, T, _ = x.shape
    h = x
    for i in range(DEPTH):
        xn = rms_norm(h, pre_norm[i])
        proj = xn @ w_in[i]
        (g_q, g_k, g_v, g_a, g_z, n_q, n_kc, n_vc, n_ks, n_vs, n_kw, n_vw, n_g, n_z) = \
            jnp.split(proj, SPLIT_POINTS, axis=-1)

        log_a = jax.nn.log_sigmoid((g_a @ gla_a_up[i] + gla_a_bias[i]).astype(jnp.float32)) / GLA_TAU
        o_gla = gla_mixer(g_q.reshape(B, T, GLA_HEADS, GLA_DK),
                          g_k.reshape(B, T, GLA_HEADS, GLA_DK),
                          g_v.reshape(B, T, GLA_HEADS, GLA_DV),
                          log_a.reshape(B, T, GLA_HEADS, GLA_DK))
        o_gla = rms_norm(o_gla, gla_out_norm[i]).reshape(B, T, GLA_WIDTH)
        o_gla = (o_gla * jax.nn.silu(g_z.astype(jnp.float32))).astype(x.dtype)

        kv = lambda t: t.reshape(B, T, NSA_KV_HEADS, NSA_DH)
        gates = jax.nn.sigmoid(n_g.astype(jnp.float32)).reshape(B, T, NSA_HEADS, N_BRANCH)
        o_nsa = nsa_mixer(n_q.reshape(B, T, NSA_HEADS, NSA_DH), kv(n_kc), kv(n_vc), kv(n_ks), kv(n_vs),
                          kv(n_kw), kv(n_vw), gates,
                          cmp_pos_k[i], cmp_w1_k[i], cmp_w2_k[i], cmp_pos_v[i], cmp_w1_v[i], cmp_w2_v[i])
        o_nsa = (o_nsa * jax.nn.silu(n_z.astype(jnp.float32))).astype(x.dtype)

        mixed = jnp.concatenate([o_gla, o_nsa], axis=-1) @ w_out[i]
        h = h + rms_norm(mixed, post_norm[i])

        gate = jax.nn.sigmoid((h @ ple_gate[i]).astype(jnp.float32))
        e = (p[i] @ ple_proj[i]).astype(jnp.float32) * gate
        h = h + rms_norm(e.astype(x.dtype), ple_norm[i])
    return h


_drawn_inputs = setup_inputs


def setup_inputs(seed=0):
    import zlib

    import numpy as np

    out = dict(_drawn_inputs(seed))
    spreads = {}
    factors = {'pre_norm': 4.432,
     'gla_out_norm': 46.924,
     'cmp_pos_k': 90.107,
     'cmp_pos_v': 157.159,
     'post_norm': 124.55,
     'ple_norm': 200.0,
     'gla_a_bias': 2.776}
    for name, (base, spread) in spreads.items():
        noise = np.random.default_rng([zlib.crc32(name.encode()), seed]).standard_normal(out[name].shape)
        drawn = base * np.exp(spread * noise) if base else spread * noise
        out[name] = __import__('jax').numpy.asarray(drawn.astype(out[name].dtype))
    for name, factor in factors.items():
        out[name] = (out[name] * factor).astype(out[name].dtype)
    return out
```

```python
from contextlib import ExitStack

import numpy as np

import concourse.bass as bass
from concourse import mybir

F32 = mybir.dt.float32
F32R = mybir.dt.float32r
BF16 = mybir.dt.bfloat16
U16 = mybir.dt.uint16
U32 = mybir.dt.uint32
ALU = mybir.AluOpType
ACT = mybir.ActivationFunctionType

P = 128
SEQ, DM = 1024, 1024
NT = SEQ // P
KD = DM // P
EPS = 1e-6
GH, GDK, GDV, RANK = 4, 64, 128, 16
NH, NKV, DH = 8, 2, 64
GRP = NH // NKV
CLEN, CSTR = 32, 16
NCMP = (SEQ - CLEN) // CSTR + 1
CROWS = SEQ // CSTR + NCMP
WINDOW = 512
WT = WINDOW // P + 1
ROT = DH // 4 // 2
THETA = 500000.0
PLE = 256
GQ, GK, GV_, GA, GZ_ = 0, 256, 512, 1024, 1040
NQ_, NKC, NKS, NG_, NZ_ = 1552, 2064, 2320, 2832, 2856
LEVELS = (2, 4, 8, 16, 32, 64, 128)

C_ID, C_COS, C_SIN, C_CCOS, C_CSIN, C_V31, C_HALF = 0, 128, 192, 256, 264, 272, 273
C_END = 274
M_SLC, M_WIN, M_CMP = 0, SEQ, SEQ + WT * P
M_END = M_CMP + NCMP + 7 * 8 + 1


def shape_constants():
    c = np.zeros((P, C_END), np.float32)
    c[:, C_ID:C_ID + P] = np.eye(P, dtype=np.float32)
    inv = THETA ** (-(np.arange(ROT, dtype=np.float32) * 2.0) / (2 * ROT))
    pos = np.arange(SEQ, dtype=np.float32).reshape(NT, P).T
    ang = (pos[:, :, None] * inv.astype(np.float32)).astype(np.float32)
    c[:, C_COS:C_COS + NT * ROT] = np.cos(ang).reshape(P, -1)
    c[:, C_SIN:C_SIN + NT * ROT] = np.sin(ang).reshape(P, -1)
    end = np.arange(P, dtype=np.float32) * CSTR + CLEN - 1
    angc = (end[:, None] * inv.astype(np.float32)).astype(np.float32)
    c[:, C_CCOS:C_CCOS + ROT] = np.cos(angc)
    c[:, C_CSIN:C_CSIN + ROT] = np.sin(angc)
    c[:, C_V31] = np.arange(P) >= CLEN - 1
    c[:, C_HALF] = -0.5
    q = np.arange(P)[:, None]
    k = np.arange(P)[None, :]
    low = 0xF14A
    m = np.zeros((P, M_END), np.uint16)
    m[:, SEQ - P:SEQ] = np.where(k <= q, 0, low)
    m[:, M_WIN:M_WIN + P] = np.where(k > q, 0, low)
    m[:, M_WIN + (WT - 1) * P:M_WIN + WT * P] = np.where(k <= q, 0, low)
    i = np.arange(M_END - M_CMP)[None, :] - 7 * 8
    m[:, M_CMP:] = np.where(i * CSTR + CLEN - 1 <= q, 0, low)
    j, t = np.arange(P)[:, None], np.arange(P)[None, :]
    g = np.zeros((P, len(LEVELS) + 1, P), np.float32)
    g[:, 0] = j == t
    for n, z in enumerate(LEVELS):
        g[:, n + 1] = (j // z == t // z) & (j % z < z // 2) & (t % z >= z // 2)
    return c, m, g.reshape(P, -1)


def chunk_plan():
    return [("gqk", True, KD, 8, 512), ("gv", False, KD, 8, 512), ("kv3", False, KD, 8, 512),
            ("nq", False, KD, 8, 512), ("ag", True, KD, 6, 304), ("gz", False, KD, 8, 512),
            ("nz", True, KD, 8, 512),
            ("wo0", False, KD, 8, 512), ("wo1", False, KD, 8, 512),
            ("pg0", False, KD, 8, 512), ("pg1", False, KD, 8, 512),
            ("pp0", False, PLE // P, 8, 512), ("pp1", False, PLE // P, 8, 512)]


def build_program(nc, a):
    chunks = chunk_plan()
    cidx = {c[0]: i for i, c in enumerate(chunks)}
    piece0 = [sum(c[2] for c in chunks[:i]) for i in range(len(chunks) + 1)]
    bank0 = [sum(c[3] for c in chunks[:i]) for i in range(len(chunks) + 1)]
    RAW, SPLIT = 3, 3

    ctx = ExitStack()
    base = (nc.sbuf_base + 31) // 32 * 32
    used = [base]

    def region(kb):
        at = used[0]
        used[0] += int(kb * 1024)
        return at

    def sb(name, shape, dt, at):
        return nc.alloc_sbuf_tensor_at(name, shape, dt, offset=at)

    R1 = region(64)
    R2 = region(18)
    R3 = region(32)
    R4 = region(22)
    R5 = region(16)
    R6 = region(32)
    R7 = region(16)
    R8 = region(7.8)

    XTh = sb("xT_hi", [P, KD, SEQ], F32R, R1)
    XTl = sb("xT_lo", [P, KD, SEQ], F32R, R1 + 32768)
    raw = sb("w_raw", [P, RAW, 512], F32, R2)
    Wh = sb("w_hi", [P, SPLIT, 512], F32R, R2 + 6144)
    Wl = sb("w_lo", [P, SPLIT, 512], F32R, R2 + 12288)
    GQK = sb("gla_qkT", [P, 4, SEQ], F32, R3)
    GV = sb("gla_v", [P, NT, 512], F32, R3 + 16384)
    KSW = sb("rot_keys", [P, NT, 4, DH], F32, R4)
    AG = sb("gate_rank_T", [P, SEQ], F32, R4 + 8192)
    SG = sb("sigmoid_tmp", [P, 2, 512], F32, R4 + 12288)
    RT = sb("rot_tmp", [P, 3, 512], F32, R4 + 16384)
    VS = sb("v_hi_lo", [P, NT, 2, NKV, P], F32R, R5)
    XN = sb("x_tok", [P, NT, DM], F32, R6)
    NQ = sb("nsa_q", [P, NT, NH, DH], F32, R6)
    DC = sb("cmp_in", [P, 2, NKV, SEQ], F32, R6 + 16384)
    NZ = sb("nsa_zT", [P, 4, SEQ], F32, R6 + 16384)
    W1 = sb("cmp_w1", [P, 2, 16, P], F32, R7)
    GZ = sb("gla_z", [P, NT, 512], F32, R7)
    small = [R8]

    def sm(name, shape, dt=F32, size=4):
        n = size
        for s in shape[1:]:
            n *= s
        at = small[0]
        small[0] += (n + 31) // 32 * 32
        assert small[0] <= R8 + int(7.8 * 1024)
        return sb(name, shape, dt, at)

    CT = sm("consts", [P, C_END])
    gpre = sm("pre_gain", [P, KD])
    st = sm("stats", [P, 3, 8])
    GT = sm("gates", [P, NT, NH, 3])
    VC = sm("vc_hi_lo", [P, NKV, P], F32R)
    KCN = sm("kc_tok", [P, NKV, DH])
    NM = sm("neg_max", [P, 4 * 48])
    SU = sm("exp_sum", [P, 4 * 48])
    RG = sm("gate_over_sum", [P, 4 * 48])
    ident = CT[:, C_ID:C_ID + P]
    W2 = sm("cmp_w2", [P, 2, DH])
    PB = sm("cmp_pos", [P, 2, 16])
    HC = sb("cmp_h", [P, 2, P], F32, R6 + 16384)
    HCT = sb("cmp_hT", [P, 2, 128], F32, R6 + 17408)
    SC = sb("cmp_sig", [P, 2, P], F32, R6 + 18432 + 0)
    GAU = sb("gla_a_up", [P, 256], F32, R4 + 20480)
    GGN = sb("gla_gain", [P, GDV], F32, R4 + 21504)
    GBI = sb("gla_bias", [P, 2], F32, R4 + 22016)
    XB = sb("gla_x", [P, 2, 2, SEQ], F32, R1)
    GB = sb("gla_b", [P, 2, SEQ], F32, R1 + 16384)
    QTI = sb("gla_q_dec", [P, 2, SEQ], F32, R1 + 24576)
    KTI = sb("gla_k_dec", [P, 2, SEQ], F32, R1 + 32768)
    KTN = sb("gla_k_dec_tok", [P, NT, 256], F32, R1 + 40960)
    ATT = sb("gla_att", [P, NT, GH, P], F32, R1 + 49152)
    OG = sb("gla_o", [P, NT, 512], F32, R1)
    GM = sb("gla_masks", [P, 8, P], F32, R2)
    ONE = sb("gla_ones", [P, P], F32, R2 + 4096)
    GS = sb("gla_state", [P, 2, 2, P], F32, R2 + 4608)
    GBL = sb("gla_decay_last", [P, 2, NT], F32, R2 + 6656)
    GSS = sb("gla_ss", [P, 3, NT * GH], F32, R2 + 6784)
    GSQ = sb("gla_sq", [P, GH, P], F32, R2 + 8192)
    QS = sb("qT_hi_lo", [P, NH, SEQ], F32R, R1)
    K1 = sb("kT_hi_hi", [P, 4, SEQ], F32R, R1 + 32768)
    K2 = sb("kT_lo_lo", [P, 4, SEQ], F32R, R1 + 49152)
    PSL = sb("p_slc", [P, 2, GRP, SEQ], F32, R3)
    PWN = sb("p_win", [P, 2, GRP, WT * P], F32, R4)
    PCM = sb("p_cmp", [P, 2, GRP, 64], F32, R4 + 20480)
    PTh = sb("pT_hi", [P, 4, 512], F32R, R2)
    PTl = sb("pT_lo", [P, 4, 512], F32R, R2 + 8192)
    KC1 = sb("kcT_hi_hi", [P, NKV, 64], F32R, R2 + 16384)
    KC2 = sb("kcT_lo_lo", [P, NKV, 64], F32R, R2 + 16896)
    MK = sb("masks", [P, M_END], U16, R6)
    OB = sb("o_low_half", [64, 512], F32, R6 + 4096)
    OT = sb("o_sum", [P, 2, P], F32, R6 + 6144)
    MGh = sb("mix_glaT_hi", [P, 4, SEQ], F32R, R1)
    MGl = sb("mix_glaT_lo", [P, 4, SEQ], F32R, R1 + 16384)
    MNh = sb("mix_nsaT_hi", [P, 4, SEQ], F32R, R6)
    MNl = sb("mix_nsaT_lo", [P, 4, SEQ], F32R, R6 + 16384)
    H = sb("h_tok", [P, NT, DM], F32, R1 + 32768)
    MIX = sb("mixed", [P, NT, DM], F32, R3)
    GPO = sb("post_gain", [P, DM], F32, R4)
    GPL = sb("ple_gain", [P, DM], F32, R4 + 4096)
    TMP = sb("out_tmp", [P, 2, DM], F32, R4 + 8192)
    HTh = sb("hT_hi", [P, KD, SEQ], F32R, R1)
    HTl = sb("hT_lo", [P, KD, SEQ], F32R, R6)
    GATE = sb("ple_gate_e", [P, NT, DM], F32, R3)
    PR = sb("p_tok", [P, NT, PLE], F32, R5)
    pTh = sb("pT_ple_hi", [P, 2, SEQ], F32R, R7)
    pTl = sb("pT_ple_lo", [P, 2, SEQ], F32R, R7 + 8192)

    PSUM = ctx.enter_context(nc.psum_tensor("psum", [P, 8, 512], F32))

    def bank(i):
        return PSUM[:, i, :]

    def sem(name):
        return ctx.enter_context(nc.semaphore(name))

    s_const = sem("const_in")
    s_small = sem("small_in")
    s_x = [sem(f"x_in{t}") for t in range(NT)]
    s_ssq_a, s_ssq_d, s_rms = sem("x_sumsq_act"), sem("x_sumsq_dve"), sem("x_rms")
    s_xn, s_xtr, s_xhi, s_xlo = sem("x_scaled"), sem("x_turned"), sem("xT_hi_made"), sem("xT_lo_made")
    s_raw = [sem(f"w_raw_in{i}") for i in range(RAW)]
    s_whi, s_wlo, s_wused = sem("w_hi_made"), sem("w_lo_made"), sem("w_used")
    s_bank = sem("bank_done")
    s_eva, s_evd = sem("bank_read_act"), sem("bank_read_dve")
    s_sig, s_vhi, s_gain = sem("sigmoid_made"), sem("v_hi_made"), sem("gla_z_gained")
    s_d, s_p, s_a = sem("dve_chain"), sem("pool_chain"), sem("act_chain")
    s_cmp, s_csig, s_ch, s_cht, s_chc, s_cout, s_cvh, s_cend = (
        sem("cmp_hidden"), sem("cmp_sigmoid"), sem("cmp_silu"), sem("cmp_turned"),
        sem("cmp_hT"), sem("cmp_out"), sem("cmp_v_hi"), sem("cmp_end"))
    s_pow = sem("pool_mean")
    s_gm, s_mk, s_h, s_pin, s_gn = sem("gla_masks_in"), sem("masks_in"), sem("x_again_in"), sem("p_in"), sem("gains_in")
    s_la, s_z, s_sp, s_b = sem("gla_rank_up"), sem("gla_z_made"), sem("gla_softplus"), sem("gla_b_made")
    s_dec_d, s_dec_e, s_dec_x = sem("decay_diff"), sem("decay_exp"), sem("decay_mul")
    s_lv, s_cp = sem("level_scores"), sem("level_taken")
    s_kt, s_ktn, s_ds, s_st, s_o, s_og = (
        sem("k_turned"), sem("k_tok"), sem("state_add"), sem("state_new"), sem("gla_out"), sem("gla_out_read"))
    s_oss, s_orms, s_gend = sem("gla_sumsq"), sem("gla_rms"), sem("gla_end")
    s_qtr, s_qhi, s_qlo = sem("qk_turned"), sem("qk_hi"), sem("qk_lo")
    s_qk, s_ttr, s_exp, s_rg, s_norm = (
        sem("scores"), sem("scores_masked"), sem("probs"), sem("gate_over_sum"), sem("probs_scaled"))
    s_normd = sem("probs_scaled_dve")
    s_pt, s_phi, s_plo, s_pv = sem("probs_turned"), sem("pT_hi_made"), sem("pT_lo_made"), sem("pv_done")
    s_ob, s_oev, s_nend = sem("o_half_copied"), sem("o_read"), sem("nsa_tile_end")
    s_mtr, s_mhi, s_mlo = sem("mix_turned"), sem("mixT_hi"), sem("mixT_lo")
    s_nhi, s_nlo = sem("nsaT_hi"), sem("nsaT_lo")
    s_hss, s_hr, s_hm, s_hh = sem("mix_sumsq"), sem("mix_rms"), sem("mix_scaled"), sem("h_made")
    s_htr, s_hhi, s_hlo = sem("h_turned"), sem("hT_hi_made"), sem("hT_lo_made")
    s_ptr, s_pphi, s_pplo = sem("p_turned"), sem("p_hi_made"), sem("p_lo_made")
    s_ess, s_er, s_em, s_eo, s_out = sem("e_sumsq"), sem("e_rms"), sem("e_scaled"), sem("out_made"), sem("out_stored")

    plain = {"gqk", "gv", "nq", "wo0", "wo1"}

    def reader(c, b):
        name = chunks[c][0]
        if name in plain:
            return "A" if b % 2 == 0 else "D"
        if name == "ag":
            return "A" if b in (0, 1, 2, 4) else "D"
        return "A" if name in ("pg0", "pg1") else "D"

    order = [(c, b) for c in range(len(chunks)) for b in range(chunks[c][3])]
    read_count = {}
    n_read = {"A": 0, "D": 0}
    for c, b in order:
        e = reader(c, b)
        n_read[e] += 1
        read_count[c, b] = n_read[e]

    def wait_read(eng, c, b):
        eng.wait_ge(s_eva if reader(c, b) == "A" else s_evd, read_count[c, b])

    def wait_chunk_read(eng, c, upto=None):
        last = {reader(c, b): b for b in range(chunks[c][3])}
        for b in last.values():
            wait_read(eng, c, b)

    piece = [(c, k) for c in range(len(chunks)) for k in range(chunks[c][2])]
    used_count = []
    for c, k in piece:
        used_count.append((used_count[-1] if used_count else 0) + (k < chunks[c][2] - 1))

    def wait_used(eng, i):
        c, k = piece[i]
        if k < chunks[c][2] - 1:
            eng.wait_ge(s_wused, used_count[i])
        else:
            eng.wait_ge(s_bank, bank0[c + 1])

    def raw_count(i):
        return sum(16 * (3 if chunks[piece[j][0]][0] == "ag" else 1) for j in range(i % RAW, i + 1, RAW))

    def halves(ap, z, first):
        v = ap.rearrange("p c (n z) -> p (c n) z", z=z)
        return v[:, :, 0:z // 2] if first else v[:, :, z // 2:z]

    steps = [(kv, qt, br) for kv in range(NKV) for qt in range(NT) for br in range(3)]

    def span(qt, br):
        if br == 0:
            return 0, NCMP
        n = qt + 1 if br == 1 else min(qt + 1, WT)
        return (qt + 1 - n) * P, n * P

    units = []
    first_unit = []
    for s, (kv, qt, br) in enumerate(steps):
        first_unit.append(len(units))
        units += [(s, i) for i in range(-(-span(qt, br)[1] // P))]
    first_unit.append(len(units))

    jobs = []
    for s in range(len(steps) + 2):
        q = [("score", 4 * s + g) for g in range(GRP)] if s < len(steps) else []
        u = [("tile", n) for n in range(first_unit[s - 2], first_unit[s - 1])] if s >= 2 else []
        a_, b_ = len(q), len(u)
        merged = sorted([((i + 0.5) / max(a_, 1), 0, x) for i, x in enumerate(q)]
                        + [((i + 0.6) / max(b_, 1), 1, x) for i, x in enumerate(u)])
        jobs.append([x for _, _, x in merged])

    def probs(s):
        kv, qt, br = steps[s]
        return (PCM, PSL, PWN)[br][:, (s // 3) % 2]

    def spread(copy, b):
        n, half = divmod(b - 2, 2)
        ps, t0 = bank(b), half * 512
        for kv in range(NKV):
            src = ps[64 * kv:64 * kv + 64]
            copy(DC[0:64, n, kv, t0:t0 + 512], src)
            ins = copy(DC[64:128, n, kv, t0:t0 + 511], src[:, 1:512]) if t0 == 0 else \
                copy(DC[64:128, n, kv, t0 - 1:t0 + 511], src)
        return ins

    block = ctx.enter_context(nc.Block())

    @block.sync
    def _(sp):
        sp.dma_start(CT[:], a["consts"]).then_inc(s_const, 16)
        sp.dma_start(gpre[:], a["pre_norm"][0].rearrange("(k p) -> p k", p=P),
                     allow_slow_non_contiguous=True).then_inc(s_const, 16)
        for t in range(NT):
            sp.dma_start(XN[:, t], a["x"][0, t * P:(t + 1) * P, :]).then_inc(s_x[t], 16)

        def load_piece(i):
            c, k = piece[i]
            name = chunks[c][0]
            if i >= RAW:
                sp.wait_ge(s_wlo, i - RAW + 1)
            dst, s_in = raw[:, i % RAW], s_raw[i % RAW]
            rows = slice(k * P, (k + 1) * P)
            w = a["w_in"][0]
            if name == "ag":
                sp.dma_start(dst[:, 0:24], w[rows, NG_:NG_ + 24]).then_inc(s_in, 16)
                sp.dma_start(dst[:, 32:48], w[rows, GA:GA + RANK]).then_inc(s_in, 16)
                sp.dma_start(dst[:, 48:304], w[rows, NKC:NKC + 256]).then_inc(s_in, 16)
                return
            if name[:2] in ("wo", "pg", "pp"):
                w = {"wo": a["w_out"], "pg": a["ple_gate"], "pp": a["ple_proj"]}[name[:2]][0]
                col = 512 * int(name[2])
            else:
                col = {"gqk": GQ, "gv": GV_, "kv3": NKS, "nq": NQ_, "gz": GZ_, "nz": NZ_}[name]
            sp.dma_start(dst, w[rows, col:col + 512]).then_inc(s_in, 16)

        for i in range(piece0[1]):
            load_piece(i)
        for n, (w1, w2, pe) in enumerate((("cmp_w1_k", "cmp_w2_k", "cmp_pos_k"),
                                          ("cmp_w1_v", "cmp_w2_v", "cmp_pos_v"))):
            for l in range(16):
                sp.dma_start(W1[:, n, l], a[w1][0, l * P:(l + 1) * P, :]).then_inc(s_small, 16)
            sp.dma_start(W2[:, n], a[w2][0]).then_inc(s_small, 16)
            sp.dma_start(PB[:, n], a[pe][0].rearrange("(l a) d -> (a d) l", a=2),
                         allow_slow_non_contiguous=True).then_inc(s_small, 16)
        sp.dma_start(GAU[32:32 + RANK, :], a["gla_a_up"][0]).then_inc(s_small, 16)
        sp.dma_start(GBI[:], a["gla_a_bias"][0].rearrange("(c p) -> p c", p=P),
                     allow_slow_non_contiguous=True).then_inc(s_small, 16)
        sp.dma_start(GGN[:], a["gla_out_norm"][0].partition_broadcast(P)).then_inc(s_small, 16)
        for i in range(piece0[1], piece0[cidx["wo0"]]):
            load_piece(i)

        wait_used(sp, piece0[cidx["wo0"]] - 1)
        sp.dma_start(GM[:], a["gla_masks"].rearrange("p (l j) -> p l j", l=8)).then_inc(s_gm, 16)

        sp.wait_ge(s_qtr, 8)
        sp.dma_start(MK[:], a["masks"]).then_inc(s_mk, 16)

        sp.wait_ge(s_pv, len(units))
        for i in range(piece0[cidx["wo0"]], piece0[cidx["wo0"]] + RAW):
            load_piece(i)
        for t in range(NT):
            sp.dma_start(H[:, t], a["x"][0, t * P:(t + 1) * P, :]).then_inc(s_h, 16)
        sp.dma_start(GPO[:], a["post_norm"][0].partition_broadcast(P)).then_inc(s_gn, 16)
        sp.dma_start(GPL[:], a["ple_norm"][0].partition_broadcast(P)).then_inc(s_gn, 16)
        sp.dma_start(PR[:], a["p"][0, 0].rearrange("(t p) d -> p t d", p=P)).then_inc(s_pin, 16)
        for i in range(piece0[cidx["wo0"]] + RAW, len(piece)):
            load_piece(i)

        for t in range(NT):
            sp.wait_ge(s_eo, t + 1)
            sp.dma_start(a["out"][0, t * P:(t + 1) * P, :], H[:, t]).then_inc(s_out, 16)
        sp.wait_ge(s_out, 16 * NT)

    @block.tensor
    def _(pe):
        pe.wait_ge(s_const, 32)
        for half in range(2):
            pe.wait_ge(s_xn, 4 * half + 4)
            for k in range(KD):
                u = half * KD + k
                if u >= 8:
                    pe.wait_ge(s_xlo, u - 7)
                for t in range(4):
                    mm = pe.transpose(bank(u % 8)[:, t * P:(t + 1) * P],
                                      XN[:, 4 * half + t, k * P:(k + 1) * P], ident)
                mm.then_inc(s_xtr, 1)
        pe.wait_ge(s_xlo, 2 * KD)

        def project(name, tokens):
            c = cidx[name]
            _, moving, kt, banks, _ = chunks[c]
            cuts = [(0, 48), (48, 176), (176, 304)] if name == "ag" else \
                [(m * P, (m + 1) * P) for m in range(4)]
            for k in range(kt):
                i = piece0[c] + k
                pe.wait_ge(s_wlo, i + 1)
                wh, wl = Wh[:, i % SPLIT], Wl[:, i % SPLIT]
                xh, xl = tokens(k)
                for b in range(banks):
                    if k == 0 and c > 0:
                        prev = c - 1
                        if b < chunks[prev][3] and name != "wo0":
                            wait_read(pe, prev, b)
                    if moving:
                        lo, hi = cuts[b // 2]
                        ts = slice(b % 2 * 512, b % 2 * 512 + 512)
                        ops = ((wh[:, lo:hi], xh[:, ts]), (wh[:, lo:hi], xl[:, ts]), (wl[:, lo:hi], xh[:, ts]))
                        out = bank(b)[0:hi - lo, :]
                    else:
                        ts = slice(b * P, b * P + P)
                        ops = ((xh[:, ts], wh), (xh[:, ts], wl), (xl[:, ts], wh))
                        out = bank(b)
                    for n, (lhs, rhs) in enumerate(ops):
                        mm = pe.matmul(out, lhs, rhs, start=(k == 0 and n == 0),
                                       stop=(k == kt - 1 and n == 2))
                    if k == kt - 1:
                        mm.then_inc(s_bank, 1)
                if k < kt - 1:
                    mm.then_inc(s_wused, 1)

        def xt(k):
            return XTh[:, k], XTl[:, k]

        for name in ("gqk", "gv", "kv3", "nq", "ag"):
            project(name, xt)

        wait_chunk_read(pe, cidx["nq"])
        wait_chunk_read(pe, cidx["ag"])
        pe.wait_ge(s_small, 16 * 39)
        for n in range(2):
            out = bank(6 + n)[0:CROWS, 0:P]
            for l in range(16):
                flat = DC[:, n].rearrange("p c t -> p (c t)")
                blocks = flat[:, 2 * l:2 * l + CSTR * (CROWS - 1) + 1:CSTR]
                pe.matmul(out, blocks, W1[:, n, l], start=(l == 0), stop=False)
            for l in range(16):
                mm = pe.matmul(out, PB[:, n, l:l + 1].to_broadcast([P, CROWS]), W1[:, n, l],
                               start=False, stop=(l == 15))
        mm.then_inc(s_cmp, 1)
        for t in range(NT):
            mm = pe.transpose(bank(5)[:, t * 24:t * 24 + 24], AG[0:24, t * P:(t + 1) * P], ident[0:24, 0:24])
        mm.then_inc(s_cmp, 1)
        pe.wait_ge(s_ch, 1)
        for n in range(2):
            mm = pe.transpose(bank(6 + n)[:, 0:CROWS], HC[0:CROWS, n, :], ident[0:CROWS, 0:CROWS])
        mm.then_inc(s_cht, 1)
        pe.wait_ge(s_chc, 1)
        for n in range(2):
            for kv in range(NKV):
                mm = pe.matmul(bank(6 + n)[0:NCMP, kv * DH:(kv + 1) * DH],
                               HCT[:, n, kv * 64:kv * 64 + NCMP], W2[:, n], start=True, stop=True)
        mm.then_inc(s_cout, 1)
        pe.wait_ge(s_cend, 1)

        project("gz", xt)
        project("nz", xt)

        wait_chunk_read(pe, cidx["nz"])
        for ct in range(2):
            for half in range(2):
                pe.matmul(bank(ct * 2 + half), GAU[32:32 + RANK, ct * P:(ct + 1) * P],
                          AG[32:32 + RANK, half * 512:half * 512 + 512],
                          start=True, stop=True).then_inc(s_la, 1)
        for lev in range(8):
            for t in range(NT):
                u = lev * NT + t
                if u == 0:
                    pe.wait_ge(s_z, 4)
                if u >= 4:
                    pe.wait_ge(s_cp, u - 3)
                if t == 0 and lev >= 1:
                    pe.wait_ge(s_dec_x, 2 * lev)
                for h in range(GH):
                    r = slice(64 * (h % 2), 64 * (h % 2) + 64)
                    ct, ts = h // 2, slice(t * P, (t + 1) * P)
                    if lev == 0:
                        lhs, rhs = GQK[r, 2 + ct, ts], GQK[r, ct, ts]
                    else:
                        lhs = rhs = XB[r, (lev - 1) % 2, ct, ts]
                    mm = pe.matmul(bank(u % 4 * 2 + h % 2)[:, ct * P:(ct + 1) * P], lhs, rhs,
                                   start=True, stop=True)
                mm.then_inc(s_lv, 1)
        pe.wait_ge(s_cp, 64)
        pe.wait_ge(s_p, 2)
        for w in range(4):
            for i in range(4):
                t, ct = 2 * w + i // 2, i % 2
                mm = pe.transpose(bank(w)[:, i * P:(i + 1) * P], KTI[:, ct, t * P:(t + 1) * P], ident)
            mm.then_inc(s_kt, 1)
        pe.wait_ge(s_ktn, 4)
        for t in range(NT):
            if t < NT - 1:
                if t >= 2:
                    pe.wait_ge(s_st, t - 1)
                for ct in range(2):
                    mm = pe.matmul(bank(2 * (t % 2) + ct)[:, 0:256], KTN[:, t, ct * P:(ct + 1) * P],
                                   GV[:, t, ct * 256:ct * 256 + 256], start=True, stop=True)
                mm.then_inc(s_ds, 1)
            if t >= 2:
                pe.wait_ge(s_og, t - 1)
            if t >= 1:
                pe.wait_ge(s_st, t)
            for h in range(GH):
                ct, par = h // 2, h % 2
                r = slice(64 * par, 64 * par + 64)
                out = bank(4 + 2 * (t % 2) + par)[:, ct * P:(ct + 1) * P]
                mm = pe.matmul(out, ATT[:, t, par * 2 + ct], GV[:, t, h * P:(h + 1) * P],
                               start=True, stop=(t == 0))
                if t:
                    mm = pe.matmul(out, QTI[r, ct, t * P:(t + 1) * P], GS[r, t % 2, ct],
                                   start=False, stop=True)
            mm.then_inc(s_o, 1)
        pe.wait_ge(s_og, NT)

        pe.wait_ge(s_gend, NT)
        for u in range(13):
            if u >= 8:
                pe.wait_ge(s_qlo, u - 7)
            for i in range(4):
                t = 4 * (u % 2) + i
                if u < 8:
                    src = NQ[:, t, u // 2 * 2:u // 2 * 2 + 2].rearrange("p h d -> p (h d)")
                elif u < 12:
                    k = (u - 8) // 2 * 2
                    src = KSW[:, t, k:k + 2].rearrange("p h d -> p (h d)")
                if u < 12:
                    mm = pe.transpose(bank(u % 8)[:, i * P:(i + 1) * P], src, ident)
            if u == 12:
                mm = pe.transpose(bank(u % 8)[:, 0:NCMP], KCN[0:NCMP].rearrange("p h d -> p (h d)"),
                                  ident[0:NCMP, 0:NCMP])
            mm.then_inc(s_qtr, 1)
        pe.wait_ge(s_qlo, 13)

        def scores(n):
            s, g = divmod(n, GRP)
            kv, qt, br = steps[s]
            k0, nk = span(qt, br)
            if n >= 2:
                pe.wait_ge(s_ttr, n - 1)
            lhs = QS[:, kv * GRP + g, qt * P:(qt + 1) * P]
            for c0 in range(0, nk, 512):
                w = min(512, nk - c0) if br else NCMP + 1
                out = bank(n % 2 * 2 + c0 // 512)[:, 0:w]
                if br == 0:
                    kk = [KC1[:, kv], KC2[:, kv]]
                else:
                    ks = slice(k0 + c0, k0 + c0 + w)
                    kk = [K1[:, (br - 1) * NKV + kv, ks], K2[:, (br - 1) * NKV + kv, ks]]
                pe.matmul(out, lhs, kk[0], start=True, stop=False)
                mm = pe.matmul(out, lhs, kk[1], start=False, stop=True)
            mm.then_inc(s_qk, 1)

        def turn(u):
            s, i = units[u]
            kv, qt, br = steps[s]
            if i == 0:
                pe.wait_ge(s_normd, s + 1)
                pe.wait_ge(s_norm, s + 1)
            if u >= 3:
                pe.wait_ge(s_plo, u - 2)
            n = min(P, span(qt, br)[1])
            for g in range(GRP):
                mm = pe.transpose(bank(4 + u % 3)[0:n, g * P:(g + 1) * P],
                                  probs(s)[:, g, i * P:i * P + n], ident)
            mm.then_inc(s_pt, 1)

        def values(u):
            s, i = units[u]
            kv, qt, br = steps[s]
            first = br == 0
            last = u + 1 == len(units) or (units[u + 1][0] // 3 != s // 3)
            if first and s >= 3:
                pe.wait_ge(s_oev, s // 3)
            pe.wait_ge(s_plo, u + 1)
            n = NCMP if br == 0 else P
            v = VC[0:n, kv] if br == 0 else VS[:, span(qt, br)[0] // P + i, br - 1, kv]
            pe.matmul(bank(7), v, PTh[0:n, u % 4], start=first, stop=False)
            pe.matmul(bank(7), v, PTl[0:n, u % 4], start=False, stop=last).then_inc(s_pv, 1)

        for s, todo in enumerate(jobs):
            for kind, n in todo:
                if kind == "score":
                    scores(n)
                else:
                    turn(n)
                    if n >= 2:
                        values(n - 2)
        values(len(units) - 2)
        values(len(units) - 1)

        pe.wait_ge(s_oev, 2 * NT)
        for u in range(8):
            for i in range(4):
                t = 4 * (u % 2) + i
                mm = pe.transpose(bank(u)[:, i * P:(i + 1) * P], GZ[:, t, (u // 2) * P:(u // 2 + 1) * P], ident)
            mm.then_inc(s_mtr, 1)
        pe.wait_ge(s_mlo, 8)
        pe.wait_ge(s_nlo, 4)

        def mixed(k):
            return (MGh[:, k], MGl[:, k]) if k < 4 else (MNh[:, k - 4], MNl[:, k - 4])

        project("wo0", mixed)
        project("wo1", mixed)
        wait_chunk_read(pe, cidx["wo1"])
        pe.wait_ge(s_pin, 16)
        for u in range(4):
            for i in range(4):
                t = 4 * (u % 2) + i
                mm = pe.transpose(bank(u)[:, i * P:(i + 1) * P], PR[:, t, (u // 2) * P:(u // 2 + 1) * P], ident)
            mm.then_inc(s_ptr, 1)
        for u in range(2 * KD):
            half, k = divmod(u, KD)
            pe.wait_ge(s_hh, 4 * half + 4)
            if u >= 4:
                pe.wait_ge(s_hlo, u - 3)
            for i in range(4):
                mm = pe.transpose(bank(4 + u % 4)[:, i * P:(i + 1) * P],
                                  H[:, 4 * half + i, k * P:(k + 1) * P], ident)
            mm.then_inc(s_htr, 1)
        pe.wait_ge(s_pplo, 4)
        pe.wait_ge(s_hlo, 2 * KD)
        for name in ("pg0", "pg1"):
            project(name, lambda k: (HTh[:, k], HTl[:, k]))
        for name in ("pp0", "pp1"):
            project(name, lambda k: (pTh[:, k], pTl[:, k]))

    @block.scalar
    def _(act):
        chain = [0]

        def link(ins):
            chain[0] += 1
            ins.then_inc(s_a, 1)
            act.wait_ge(s_a, chain[0])

        act.wait_ge(s_const, 32)
        for t in range(0, NT, 2):
            act.wait_ge(s_x[t], 16)
            link(act.activation(GQK[:, 0], XN[:, t], ACT.Square, accum_out=st[:, 0, t:t + 1]))

        def split_hi(i):
            c, k = piece[i]
            w = chunks[c][4]
            act.wait_ge(s_raw[i % RAW], raw_count(i))
            if i >= SPLIT:
                wait_used(act, i - SPLIT)
            act.activation(Wh[:, i % SPLIT, 0:w], raw[:, i % RAW, 0:w], ACT.Copy).then_inc(s_whi, 1)

        for u in range(2 * KD):
            half, k = divmod(u, KD)
            if u == 8:
                for i in range(2):
                    split_hi(i)
            act.wait_ge(s_xtr, u + 1)
            act.activation(XTh[:, k, half * 512:half * 512 + 512], bank(u % 8), ACT.Copy,
                           scale=gpre[:, k:k + 1]).then_inc(s_xhi, 1)

        def read_out(c):
            name = chunks[c][0]
            for b in range(chunks[c][3]):
                ps, done = bank(b), bank0[c] + b + 1
                mine = reader(c, b) == "A"
                out = None
                if name in plain and mine:
                    act.wait_ge(s_bank, done)
                    scale = 1.0
                    if name == "gqk":
                        out = GQK[:, b // 2, b % 2 * 512:b % 2 * 512 + 512]
                        scale = GDK ** -0.5 if b < 4 else 1.0
                    elif name == "gv":
                        out = GV[:, b]
                    elif name == "nq":
                        out = NQ[:, b].rearrange("p h d -> p (h d)")
                    else:
                        out = MIX[:, b, 512 * int(name[2]):512 * int(name[2]) + 512]
                    act.activation(out, ps, ACT.Copy, scale=scale).then_inc(s_eva, 1)
                elif name == "kv3":
                    act.wait_ge(s_bank, done)
                    v = ps.rearrange("p (r w c) -> p r w c", r=2, w=2)
                    act.activation(KSW[:, b].rearrange("p (r c) d -> p r (c d)", r=2), v[:, :, 0], ACT.Copy)
                    act.activation(VS[:, b, :, :, 0:DH], v[:, :, 1].rearrange("p r (c d) -> p r c d", c=2),
                                   ACT.Copy).then_inc(s_vhi, 1)
                elif name == "ag" and mine:
                    act.wait_ge(s_bank, done)
                    if b < 2:
                        cols = slice(b * 512, b * 512 + 512)
                        act.activation(AG[0:24, cols], ps[0:24], ACT.Sigmoid)
                        act.activation(AG[32:48, cols], ps[32:48], ACT.Copy).then_inc(s_eva, 1)
                    else:
                        spread(lambda o, i_: act.activation(o, i_, ACT.Copy), b).then_inc(s_eva, 1)
                elif name in ("gz", "nz"):
                    act.wait_ge(s_bank, done)
                    if b >= 2:
                        wait_read(act, c, b - 2)
                    elif name == "nz":
                        wait_read(act, cidx["gz"], 6 + b)
                    act.activation(SG[:, b % 2], ps, ACT.Sigmoid).then_inc(s_sig, 1)
                elif name in ("pg0", "pg1"):
                    act.wait_ge(s_bank, done)
                    col = 512 * int(name[2])
                    act.activation(GATE[:, b, col:col + 512], ps, ACT.Sigmoid).then_inc(s_eva, 1)

        def chunk_work(c, start):
            for k in range(start, chunks[c][2]):
                split_hi(piece0[c] + k)
                if k == 1 and c > 0 and chunks[c - 1][0] not in ("ag", "nz"):
                    read_out(c - 1)

        for c in range(cidx["wo0"]):
            chunk_work(c, 2 if c == 0 else 0)
            if chunks[c][0] == "ag":
                read_out(c)
                act.wait_ge(s_cmp, 1)
                for n in range(2):
                    ins = act.activation(SC[0:CROWS, n], bank(6 + n)[0:CROWS, 0:P], ACT.Sigmoid)
                ins.then_inc(s_csig, 1)
                act.wait_ge(s_cout, 1)
                act.activation(VC[0:NCMP, :, 0:DH], bank(7)[0:NCMP, 0:P].rearrange("p (c d) -> p c d", c=2),
                               ACT.Copy).then_inc(s_cvh, 1)
        read_out(cidx["nz"])

        act.wait_ge(s_z, 4)
        link(act.activation(XB[:, 0], GB[:], ACT.Abs))
        link(act.activation(XB[:, 0], XB[:, 0], ACT.Exp, scale=-1.0))
        act.activation(XB[:, 0], XB[:, 0], ACT.Ln, bias=1.0).then_inc(s_sp, 1)
        act.wait_ge(s_b, 1)
        act.activation(QTI[:], GB[:], ACT.Exp, scale=1.0 / 16).then_inc(s_dec_e, 1)
        act.activation(GBL[:], GB[:].rearrange("p c (t j) -> p c t j", j=P)[:, :, :, P - 1], ACT.Exp,
                       scale=1.0 / 16)
        act.wait_ge(s_dec_d, 1)
        act.activation(KTI[:], KTI[:], ACT.Exp, scale=1.0 / 16).then_inc(s_dec_e, 1)
        for lev, z in enumerate(LEVELS):
            x = XB[:, lev % 2]
            act.wait_ge(s_dec_d, lev + 2)
            act.activation(halves(x, z, True), halves(x, z, True), ACT.Exp, scale=-1.0 / 16)
            act.activation(halves(x, z, False), halves(x, z, False), ACT.Exp, scale=1.0 / 16).then_inc(s_dec_e, 1)
        for w in range(4):
            act.wait_ge(s_kt, w + 1)
            act.activation(KTN[:, 2 * w:2 * w + 2].rearrange("p t c -> p (t c)"), bank(w),
                           ACT.Copy).then_inc(s_ktn, 1)
        for t in range(NT):
            act.wait_ge(s_o, t + 1)
            b = 4 + 2 * (t % 2)
            link(act.activation(OG[:, t].rearrange("p (c r d) -> p r c d", c=2, r=2),
                                PSUM[:, b:b + 2, 0:256].rearrange("p r (c d) -> p r c d", c=2), ACT.Copy))
            for h in range(GH):
                ins = act.activation(GSQ[:, h], OG[:, t, h * P:(h + 1) * P], ACT.Square,
                                     accum_out=GSS[:, 0, t * GH + h:t * GH + h + 1])
            ins.then_inc(s_og, 1)

        for u in range(13):
            act.wait_ge(s_qtr, u + 1)
            cols = slice(u % 2 * 512, u % 2 * 512 + 512)
            for par in range(2):
                ps = bank(u % 8)[64 * par:64 * par + 64]
                if u < 8:
                    ins = act.activation(QS[0:64, u // 2 * 2 + par, cols], ps, ACT.Copy)
                    continue
                for r in (slice(0, 64), slice(64, 128)):
                    if u < 12:
                        ins = act.activation(K1[r, (u - 8) // 2 * 2 + par, cols], ps, ACT.Copy)
                    else:
                        ins = act.activation(KC1[r, par, 0:NCMP], ps[:, 0:NCMP], ACT.Copy)
            ins.then_inc(s_qhi, 1)

        def exponent(n):
            s, g = divmod(n, GRP)
            kv, qt, br = steps[s]
            nk = span(qt, br)[1]
            act.wait_ge(s_ttr, n + 1)
            act.activation(probs(s)[:, g, 0:nk], probs(s)[:, g, 0:nk], ACT.Exp, bias=NM[:, n:n + 1],
                           scale=-1.0, accum_out=SU[:, n:n + 1]).then_inc(s_exp, 1)

        def tile_hi(u):
            s, i = units[u]
            n = min(P, span(*steps[s][1:])[1])
            act.wait_ge(s_pt, u + 1)
            if u >= 4:
                act.wait_ge(s_pv, u - 3)
            act.activation(PTh[0:n, u % 4], bank(4 + u % 3)[0:n], ACT.Copy).then_inc(s_phi, 1)

        def output_half(j):
            act.wait_ge(s_pv, first_unit[3 * (j + 1)])
            if j:
                act.wait_ge(s_oev, j)
            act.activation(OB[:], bank(7)[64:128], ACT.Copy).then_inc(s_ob, 1)

        late = []
        for s, todo in enumerate(jobs):
            for kind, n in todo:
                if kind == "score":
                    late.append(n)
                    if len(late) > 1:
                        exponent(late.pop(0))
                else:
                    tile_hi(n)
            if late and s >= len(steps) - 1:
                exponent(late.pop(0))
            if s >= 5 and (s - 5) % 3 == 0:
                output_half((s - 5) // 3)
        for j in range((len(jobs) - 1 - 5) // 3 + 1, 2 * NT):
            output_half(j)

        for u in range(8):
            act.wait_ge(s_mtr, u + 1)
            act.activation(MGh[:, u // 2, u % 2 * 512:u % 2 * 512 + 512], bank(u), ACT.Copy).then_inc(s_mhi, 1)
        act.wait_ge(s_nend, 2 * NT)
        for m in range(4):
            act.activation(MNh[:, m], NZ[:, m], ACT.Copy).then_inc(s_nhi, 1)
        chunk_work(cidx["wo0"], 0)
        chunk_work(cidx["wo1"], 0)
        split_hi(piece0[cidx["pg0"]])
        split_hi(piece0[cidx["pg0"]] + 1)
        read_out(cidx["wo1"])
        for u in range(4):
            act.wait_ge(s_ptr, u + 1)
            act.activation(pTh[:, u // 2, u % 2 * 512:u % 2 * 512 + 512], bank(u), ACT.Copy).then_inc(s_pphi, 1)
        for u in range(2 * KD):
            half, k = divmod(u, KD)
            act.wait_ge(s_htr, u + 1)
            act.activation(HTh[:, k, half * 512:half * 512 + 512], bank(4 + u % 4), ACT.Copy).then_inc(s_hhi, 1)
        for k in range(2, KD):
            split_hi(piece0[cidx["pg0"]] + k)
        chunk_work(cidx["pg1"], 0)
        chunk_work(cidx["pp0"], 0)
        chunk_work(cidx["pp1"], 0)

    @block.gpsimd
    def _(pool):
        chain = [0]

        def link(ins):
            chain[0] += 1
            ins.then_inc(s_p, 1)
            pool.wait_ge(s_p, chain[0])

        def inverse_rms(mean_eps, out, total, n, width, done):
            pool.tensor_scalar(mean_eps, total, 1.0 / n, EPS, ALU.mult, ALU.add).then_inc(s_pow, 1)
            pow_count[0] += 1
            pool.wait_ge(s_pow, pow_count[0])
            pool.tensor_tensor(out, mean_eps, CT[:, C_HALF:C_HALF + 1].to_broadcast([P, width]),
                               ALU.pow).then_inc(done, 1)

        pow_count = [0]
        pool.wait_ge(s_const, 32)
        pool.wait_ge(s_a, NT // 2)
        pool.wait_ge(s_ssq_d, 4)
        inverse_rms(st[:, 1], st[:, 2], st[:, 0], DM, NT, s_rms)

        def split_lo(i):
            c, k = piece[i]
            w = chunks[c][4]
            pool.wait_ge(s_whi, i + 1)
            pool.tensor_tensor(Wl[:, i % SPLIT, 0:w], raw[:, i % RAW, 0:w],
                               Wh[:, i % SPLIT, 0:w].bitcast(F32), ALU.subtract).then_inc(s_wlo, 1)

        for i in range(piece0[cidx["nz"]] + 2):
            split_lo(i)
        pool.wait_ge(s_small, 16 * 39)
        for t in range(NT):
            wait_read(pool, cidx["gz"], t)
            pool.tensor_tensor(GZ[:, t].rearrange("p (h d) -> p h d", h=GH),
                               GZ[:, t].rearrange("p (h d) -> p h d", h=GH),
                               GGN[:].unsqueeze(1).to_broadcast([P, GH, GDV]), ALU.mult).then_inc(s_gain, 1)
            if t < 6:
                split_lo(piece0[cidx["nz"]] + 2 + t)
        pool.wait_ge(s_dec_e, 1)
        pool.tensor_tensor(QTI[:], QTI[:], GQK[:, 0:2], ALU.mult).then_inc(s_p, 1)
        pool.wait_ge(s_dec_e, 2)
        pool.tensor_tensor(KTI[:], KTI[:], GQK[:, 2:4], ALU.mult).then_inc(s_p, 1)
        chain[0] += 2
        for lev, z in enumerate(LEVELS):
            x = XB[:, lev % 2]
            pool.wait_ge(s_dec_e, lev + 3)
            for first, src in ((True, GQK[:, 2:4]), (False, GQK[:, 0:2])):
                pool.tensor_tensor(halves(x, z, first), halves(x, z, first), halves(src, z, first),
                                   ALU.mult).then_inc(s_dec_x, 1)
        pool.wait_ge(s_og, NT)
        inverse_rms(GSS[:, 1], GSS[:, 2], GSS[:, 0], GDV, NT * GH, s_orms)

        for n in range(GRP - 1, GRP * len(steps), GRP):
            s, g = divmod(n, GRP)
            nk = span(*steps[s][1:])[1]
            pool.wait_ge(s_rg, s + 1)
            pool.tensor_scalar(probs(s)[:, g, 0:nk], probs(s)[:, g, 0:nk], RG[:, n:n + 1], None,
                               ALU.mult).then_inc(s_norm, 1)

        for i in range(piece0[cidx["wo0"]], piece0[cidx["pg0"]] + 2):
            split_lo(i)
        pool.wait_ge(s_hss, NT)
        inverse_rms(st[:, 1], st[:, 2], st[:, 0], DM, NT, s_hr)
        for t in range(NT):
            pool.wait_ge(s_hm, t + 1)
            pool.wait_ge(s_h, 16 * NT)
            pool.tensor_tensor(H[:, t], H[:, t], TMP[:, t % 2], ALU.add).then_inc(s_hh, 1)
        for i in range(piece0[cidx["pg0"]] + 2, len(piece)):
            split_lo(i)
        pool.wait_ge(s_ess, NT)
        inverse_rms(st[:, 1], st[:, 2], st[:, 0], DM, NT, s_er)
        for t in range(NT):
            pool.wait_ge(s_em, t + 1)
            pool.tensor_tensor(H[:, t], H[:, t], TMP[:, t % 2], ALU.add).then_inc(s_eo, 1)

    @block.vector
    def _(dve):
        chain = [0]

        def link(ins):
            chain[0] += 1
            ins.then_inc(s_d, 1)
            dve.wait_ge(s_d, chain[0])

        dve.wait_ge(s_const, 32)
        for t in range(1, NT, 2):
            dve.wait_ge(s_x[t], 16)
            if t > 1:
                dve.wait_ge(s_ssq_d, t // 2)
            dve.tensor_tensor_reduce(GV[:, 0:2].rearrange("p a b -> p (a b)"), XN[:, t], XN[:, t], 1.0, 0.0,
                                     ALU.mult, ALU.add, st[:, 0, t:t + 1]).then_inc(s_ssq_d, 1)
        dve.wait_ge(s_rms, 1)
        for t in range(NT):
            dve.wait_ge(s_x[t], 16)
            dve.tensor_scalar(XN[:, t], XN[:, t], st[:, 2, t:t + 1], None, ALU.mult).then_inc(s_xn, 1)
        for u in range(2 * KD):
            half, k = divmod(u, KD)
            cols = slice(half * 512, half * 512 + 512)
            dve.wait_ge(s_xhi, u + 1)
            dve.scalar_tensor_tensor(XTl[:, k, cols], bank(u % 8), gpre[:, k:k + 1],
                                     XTh[:, k, cols].bitcast(F32), ALU.mult, ALU.subtract).then_inc(s_xlo, 1)

        def read_out(c):
            name = chunks[c][0]
            for b in range(chunks[c][3]):
                ps, done = bank(b), bank0[c] + b + 1
                mine = reader(c, b) == "D"
                if not mine:
                    continue
                if name in plain:
                    dve.wait_ge(s_bank, done)
                    if name == "gqk":
                        out = GQK[:, b // 2, b % 2 * 512:b % 2 * 512 + 512]
                        if b < 4:
                            dve.tensor_scalar(out, ps, GDK ** -0.5, None, ALU.mult).then_inc(s_evd, 1)
                            continue
                    elif name == "gv":
                        out = GV[:, b]
                    elif name == "nq":
                        out = NQ[:, b].rearrange("p h d -> p (h d)")
                    else:
                        out = MIX[:, b, 512 * int(name[2]):512 * int(name[2]) + 512]
                    dve.tensor_copy(out, ps).then_inc(s_evd, 1)
                elif name == "kv3":
                    dve.wait_ge(s_vhi, b + 1)
                    v = ps.rearrange("p (r w c) -> p r w c", r=2, w=2)[:, :, 1]
                    dve.tensor_tensor(VS[:, b, :, :, DH:P], v.rearrange("p r (c d) -> p r c d", c=2),
                                      VS[:, b, :, :, 0:DH].bitcast(F32), ALU.subtract).then_inc(s_evd, 1)
                elif name == "ag":
                    dve.wait_ge(s_bank, done)
                    spread(lambda o, i_: dve.tensor_copy(o, i_), b).then_inc(s_evd, 1)
                elif name in ("gz", "nz"):
                    dve.wait_ge(s_sig, b + 1 + (8 if name == "nz" else 0))
                    out = GZ[:, b] if name == "gz" else NZ[:, b // 2, b % 2 * 512:b % 2 * 512 + 512]
                    dve.tensor_tensor(out, ps, SG[:, b % 2], ALU.mult).then_inc(s_evd, 1)
                elif name in ("pp0", "pp1"):
                    dve.wait_ge(s_bank, done)
                    col = 512 * int(name[2])
                    g = GATE[:, b, col:col + 512]
                    dve.tensor_tensor(g, ps, g, ALU.mult).then_inc(s_evd, 1)

        def rotate(x, cos, sin, n):
            x1, x2 = x[..., 0:ROT], x[..., ROT:2 * ROT]
            t1, t2 = RT[0:n, 0], RT[0:n, 1]
            sh = list(x1.shape)

            def like(t):
                size = 1
                for d in sh[1:]:
                    size *= d
                t = t[:, 0:size]
                return t.rearrange("p (a b c) -> p a b c", a=sh[1], b=sh[2]) if len(sh) == 4 \
                    else t.rearrange("p (a c) -> p a c", a=sh[1])

            t1, t2 = like(t1), like(t2)
            dve.tensor_tensor(t1, x1, sin, ALU.mult)
            link(dve.tensor_tensor(t2, x2, sin, ALU.mult))
            dve.tensor_tensor(x1, x1, cos, ALU.mult)
            link(dve.tensor_tensor(x2, x2, cos, ALU.mult))
            dve.tensor_tensor(x1, x1, t2, ALU.subtract)
            link(dve.tensor_tensor(x2, x2, t1, ALU.add))

        def tables(w):
            sh = [P, NT, w, ROT]
            cos = CT[:, C_COS:C_COS + NT * ROT].rearrange("p (t r) -> p t r", t=NT)
            sin = CT[:, C_SIN:C_SIN + NT * ROT].rearrange("p (t r) -> p t r", t=NT)
            return cos.unsqueeze(2).to_broadcast(sh), sin.unsqueeze(2).to_broadcast(sh)

        for c in range(cidx["wo0"]):
            read_out(c)
            name = chunks[c][0]
            if name == "kv3":
                rotate(KSW[:], *tables(4), P)
            elif name == "nq":
                wait_chunk_read(dve, c)
                rotate(NQ[:], *tables(NH), P)
            elif name == "ag":
                dve.wait_ge(s_csig, 1)
                dve.wait_ge(s_cmp, 2)
                for n in range(2):
                    dve.tensor_tensor(HC[0:CROWS, n], bank(6 + n)[0:CROWS, 0:P], SC[0:CROWS, n],
                                      ALU.mult)
                link(dve.tensor_copy(GT[:].rearrange("p t h b -> p (t h b)"), bank(5)[:, 0:NT * 24]))
                dve.tensor_scalar(GT[:, 0, :, 0], GT[:, 0, :, 0], CT[:, C_V31:C_V31 + 1], None,
                                  ALU.mult).then_inc(s_ch, 1)
                dve.wait_ge(s_cht, 1)
                for n in range(2):
                    ins = dve.tensor_copy(HCT[:, n, 0:CROWS], bank(6 + n)[:, 0:CROWS])
                ins.then_inc(s_chc, 1)
                dve.wait_ge(s_cout, 1)
                link(dve.tensor_copy(KCN[0:NCMP].rearrange("p c d -> p (c d)"), bank(6)[0:NCMP, 0:P]))
                dve.wait_ge(s_cvh, 1)
                dve.tensor_tensor(VC[0:NCMP, :, DH:P], bank(7)[0:NCMP, 0:P].rearrange("p (c d) -> p c d", c=2),
                                  VC[0:NCMP, :, 0:DH].bitcast(F32), ALU.subtract).then_inc(s_cend, 1)
                sh = [NCMP, NKV, ROT]
                rotate(KCN[0:NCMP], CT[0:NCMP, C_CCOS:C_CCOS + ROT].unsqueeze(1).to_broadcast(sh),
                       CT[0:NCMP, C_CSIN:C_CSIN + ROT].unsqueeze(1).to_broadcast(sh), NCMP)

        wait_used(dve, piece0[cidx["wo0"]] - 1)
        dve.memset(ATT[:].rearrange("p t h q -> p (t h q)"), 0.0)
        dve.memset(ONE[:], 1.0)
        for i in range(4):
            ct, half = divmod(i, 2)
            dve.wait_ge(s_la, i + 1)
            dve.tensor_scalar(GB[:, ct, half * 512:half * 512 + 512], bank(i), GBI[:, ct:ct + 1], None,
                              ALU.add).then_inc(s_z, 1)
        dve.wait_ge(s_sp, 1)
        link(dve.scalar_tensor_tensor(XB[:, 1], GB[:], 0.0, XB[:, 0], ALU.min, ALU.subtract))
        for ct in range(2):
            for t in range(NT):
                ts = slice(t * P, (t + 1) * P)
                ins = dve.tensor_tensor_scan(GB[:, ct, ts], ONE[:], XB[:, 1, ct, ts], 0.0, ALU.mult, ALU.add)
        ins.then_inc(s_b, 1)
        dve.wait_ge(s_b, 1)
        b3 = GB[:].rearrange("p c (t j) -> p (c t) j", j=P)
        dve.tensor_tensor(KTI[:].rearrange("p c (t j) -> p (c t) j", j=P),
                          b3[:, :, P - 1:P].to_broadcast([P, 2 * NT, P]), b3, ALU.subtract).then_inc(s_dec_d, 1)

        def level_diff(lev):
            z = LEVELS[lev]
            if lev >= 2:
                dve.wait_ge(s_lv, NT * lev)
            b2 = GB[:].rearrange("p c (n z) -> p (c n) z", z=z)
            dve.tensor_tensor(XB[:, lev % 2].rearrange("p c (n z) -> p (c n) z", z=z), b2,
                              b2[:, :, z // 2 - 1:z // 2].to_broadcast([P, 2 * SEQ // z, z]),
                              ALU.subtract).then_inc(s_dec_d, 1)

        dve.wait_ge(s_gm, 16)
        level_diff(0)
        level_diff(1)
        for lev in range(8):
            for t in range(NT):
                u = lev * NT + t
                dve.wait_ge(s_lv, u + 1)
                b = u % 4 * 2
                for par in range(2):
                    ins = dve.copy_predicated(
                        ATT[:, t, 2 * par:2 * par + 2],
                        GM[:, lev].bitcast(U32).unsqueeze(1).to_broadcast([P, 2, P]),
                        PSUM[:, b + par, 0:256].rearrange("p (c q) -> p c q", c=2))
                ins.then_inc(s_cp, 1)
            if 1 <= lev < 6:
                level_diff(lev + 1)
        for t in range(NT - 1):
            dve.wait_ge(s_ds, t + 1)
            if t:
                dve.wait_ge(s_o, t)
                dve.wait_ge(s_st, t)
            for ct in range(2):
                for par in range(2):
                    r = slice(64 * par, 64 * par + 64)
                    new, add = GS[r, (t + 1) % 2, ct], bank(2 * (t % 2) + ct)[r, par * P:(par + 1) * P]
                    if t == 0:
                        ins = dve.tensor_copy(new, add)
                    else:
                        ins = dve.scalar_tensor_tensor(new, GS[r, t % 2, ct], GBL[r, ct, t:t + 1], add,
                                                       ALU.mult, ALU.add)
            ins.then_inc(s_st, 1)
        dve.wait_ge(s_orms, 1)
        for t in range(NT):
            dve.wait_ge(s_gain, t + 1)
            dve.wait_ge(s_og, t + 1)
            for h in range(GH):
                hs = slice(h * P, (h + 1) * P)
                i = t * GH + h
                ins = dve.scalar_tensor_tensor(GZ[:, t, hs], OG[:, t, hs], GSS[:, 2, i:i + 1], GZ[:, t, hs],
                                               ALU.mult, ALU.mult)
            ins.then_inc(s_gend, 1)

        for kc in (KC1, KC2):
            dve.memset(kc[:, :, NCMP:NCMP + 1].bitcast(F32), 0.0)
        for u in range(13):
            dve.wait_ge(s_qhi, u + 1)
            cols = slice(u % 2 * 512, u % 2 * 512 + 512)
            for par in range(2):
                ps = bank(u % 8)[64 * par:64 * par + 64]
                if u < 8:
                    h = u // 2 * 2 + par
                    ins = dve.tensor_tensor(QS[64:128, h, cols], ps, QS[0:64, h, cols].bitcast(F32),
                                            ALU.subtract)
                    continue
                for r in (slice(0, 64), slice(64, 128)):
                    if u < 12:
                        k = (u - 8) // 2 * 2 + par
                        ins = dve.tensor_tensor(K2[r, k, cols], ps, K1[r, k, cols].bitcast(F32), ALU.subtract)
                    else:
                        ins = dve.tensor_tensor(KC2[r, par, 0:NCMP], ps[:, 0:NCMP],
                                                KC1[r, par, 0:NCMP].bitcast(F32), ALU.subtract)
            ins.then_inc(s_qlo, 1)
        dve.wait_ge(s_mk, 16)

        def mask_max(n):
            s, g = divmod(n, GRP)
            kv, qt, br = steps[s]
            nk = span(qt, br)[1]
            m0 = {0: M_CMP + 7 * 8 - 8 * qt, 1: SEQ - nk, 2: M_WIN + WT * P - nk}[br]
            dve.wait_ge(s_qk, n + 1)
            ps = PSUM[:, n % 2 * 2:n % 2 * 2 + 2].rearrange("p a b -> p (a b)")[:, 0:nk]
            dve.tensor_tensor_reduce(probs(s)[:, g, 0:nk], ps, MK[:, m0:m0 + nk].bitcast(BF16),
                                     -(DH ** -0.5), 3.0e38, ALU.add, ALU.min,
                                     NM[:, n:n + 1]).then_inc(s_ttr, 1)

        def gate_over_sum(s):
            kv, qt, br = steps[s]
            n = slice(GRP * s, GRP * s + GRP)
            dve.wait_ge(s_exp, GRP * (s + 1))
            link(dve.reciprocal(RG[:, n], SU[:, n]))
            dve.tensor_tensor(RG[:, n], RG[:, n], GT[:, qt, kv * GRP:(kv + 1) * GRP, br],
                              ALU.mult).then_inc(s_rg, 1)
            dve.wait_ge(s_rg, s + 1)
            nk = span(qt, br)[1]
            for g in range(GRP - 1):
                x = probs(s)[:, g, 0:nk]
                ins = dve.tensor_scalar(x, x, RG[:, GRP * s + g:GRP * s + g + 1], None, ALU.mult)
            ins.then_inc(s_normd, 1)

        def tile_lo(u):
            s, i = units[u]
            n = min(P, span(*steps[s][1:])[1])
            dve.wait_ge(s_phi, u + 1)
            dve.tensor_tensor(PTl[0:n, u % 4], bank(4 + u % 3)[0:n], PTh[0:n, u % 4].bitcast(F32),
                              ALU.subtract).then_inc(s_plo, 1)

        def output_tile(j):
            kv, qt = divmod(j, NT)
            dve.wait_ge(s_ob, j + 1)
            o = bank(7)[0:64].rearrange("p (a r q) -> p a r q", a=2, r=2)
            ob = OB[:].rearrange("p (a r q) -> p a r q", a=2, r=2)
            for par in range(2):
                ins = dve.tensor_tensor(OT[64 * par:64 * par + 64], o[:, :, par], ob[:, :, par], ALU.add)
            ins.then_inc(s_oev, 1)
            dve.wait_ge(s_oev, j + 1)
            z = NZ[:, 2 * kv:2 * kv + 2, qt * P:(qt + 1) * P]
            dve.tensor_tensor(z, z, OT[:], ALU.mult).then_inc(s_nend, 1)

        late = []
        for s, todo in enumerate(jobs):
            for m, (kind, n) in enumerate(todo):
                if kind == "score":
                    mask_max(n)
                else:
                    late.append(n)
                    if len(late) > 1:
                        tile_lo(late.pop(0))
                if m == 1 and 1 <= s <= len(steps):
                    gate_over_sum(s - 1)
            if s == len(jobs) - 1:
                tile_lo(late.pop(0))
            if s >= 5 and (s - 5) % 3 == 0:
                output_tile((s - 5) // 3)
        for j in range((len(jobs) - 1 - 5) // 3 + 1, 2 * NT):
            output_tile(j)

        for u in range(8):
            cols = slice(u % 2 * 512, u % 2 * 512 + 512)
            dve.wait_ge(s_mhi, u + 1)
            dve.tensor_tensor(MGl[:, u // 2, cols], bank(u), MGh[:, u // 2, cols].bitcast(F32),
                              ALU.subtract).then_inc(s_mlo, 1)
        for m in range(4):
            dve.wait_ge(s_nhi, m + 1)
            dve.tensor_tensor(MNl[:, m], NZ[:, m], MNh[:, m].bitcast(F32), ALU.subtract).then_inc(s_nlo, 1)
        read_out(cidx["wo0"])
        read_out(cidx["wo1"])
        wait_chunk_read(dve, cidx["wo1"])

        def sum_squares(x, t, done):
            if t >= 2:
                dve.wait_ge(done, t - 1)
            dve.tensor_tensor_reduce(TMP[:, t % 2], x, x, 1.0, 0.0, ALU.mult, ALU.add,
                                     st[:, 0, t:t + 1]).then_inc(done, 1)

        for t in range(NT):
            sum_squares(MIX[:, t], t, s_hss)
        dve.wait_ge(s_gn, 32)
        dve.wait_ge(s_hr, 1)
        for t in range(NT):
            if t >= 2:
                dve.wait_ge(s_hh, t - 1)
            dve.scalar_tensor_tensor(TMP[:, t % 2], MIX[:, t], st[:, 2, t:t + 1], GPO[:],
                                     ALU.mult, ALU.mult).then_inc(s_hm, 1)
        for u in range(4):
            cols = slice(u % 2 * 512, u % 2 * 512 + 512)
            dve.wait_ge(s_pphi, u + 1)
            dve.tensor_tensor(pTl[:, u // 2, cols], bank(u), pTh[:, u // 2, cols].bitcast(F32),
                              ALU.subtract).then_inc(s_pplo, 1)
        for u in range(2 * KD):
            half, k = divmod(u, KD)
            cols = slice(half * 512, half * 512 + 512)
            dve.wait_ge(s_hhi, u + 1)
            dve.tensor_tensor(HTl[:, k, cols], bank(4 + u % 4), HTh[:, k, cols].bitcast(F32),
                              ALU.subtract).then_inc(s_hlo, 1)
        for name in ("pg0", "pg1", "pp0", "pp1"):
            read_out(cidx[name])
        for t in range(NT):
            wait_read(dve, cidx["pp1"], t)
            sum_squares(GATE[:, t], t, s_ess)
        dve.wait_ge(s_er, 1)
        for t in range(NT):
            if t >= 2:
                dve.wait_ge(s_eo, t - 1)
            dve.scalar_tensor_tensor(TMP[:, t % 2], GATE[:, t], st[:, 2, t:t + 1], GPL[:],
                                     ALU.mult, ALU.mult).then_inc(s_em, 1)

    ctx.close()


_INS = ["x", "p", "pre_norm", "w_in", "gla_a_up", "gla_a_bias", "gla_out_norm", "cmp_pos_k", "cmp_w1_k",
        "cmp_w2_k", "cmp_pos_v", "cmp_w1_v", "cmp_w2_v", "w_out", "post_norm", "ple_proj", "ple_gate",
        "ple_norm"]


def kernel(**inputs):
    import numpy as _np
    import concourse.bacc as _bacc
    from concourse import mybir as _mybir
    from concourse.bass_utils import run_bass_kernel_spmd as _run

    nc = _bacc.Bacc("TRN2", target_bir_lowering=False, num_devices=1)
    arrays, aps = {}, {}
    named = {n: _np.ascontiguousarray(inputs[n]) for n in _INS}
    named["consts"], named["masks"], named["gla_masks"] = shape_constants()
    for n, v in named.items():
        arrays[f"in_{n}"] = v
        aps[n] = nc.dram_tensor(f"in_{n}", v.shape, _mybir.dt.from_np(v.dtype), kind="ExternalInput").ap()
    aps["out"] = nc.dram_tensor("out_0", (1, SEQ, DM), _mybir.dt.float32, kind="ExternalOutput").ap()
    build_program(nc, aps)
    r = _run(nc, [arrays], core_ids=[0])
    return r.results[0]["out_0"]
```

```python
from contextlib import ExitStack

import numpy as np

import concourse.bass as bass
from concourse import mybir

F32 = mybir.dt.float32
F32R = mybir.dt.float32r
BF16 = mybir.dt.bfloat16
U16 = mybir.dt.uint16
U32 = mybir.dt.uint32
ALU = mybir.AluOpType
ACT = mybir.ActivationFunctionType

P = 128
SEQ, DM = 1024, 1024
NT = SEQ // P
KD = DM // P
EPS = 1e-6
GH, GDK, GDV, RANK = 4, 64, 128, 16
NH, NKV, DH = 8, 2, 64
GRP = NH // NKV
CLEN, CSTR = 32, 16
NCMP = (SEQ - CLEN) // CSTR + 1
CROWS = SEQ // CSTR + NCMP
WINDOW = 512
WT = WINDOW // P + 1
ROT = DH // 4 // 2
THETA = 500000.0
PLE = 256
GQ, GK, GV_, GA, GZ_ = 0, 256, 512, 1024, 1040
NQ_, NKC, NKS, NG_, NZ_ = 1552, 2064, 2320, 2832, 2856
LEVELS = (2, 4, 8, 16, 32, 64, 128)

C_ID, C_COS, C_SIN, C_CCOS, C_CSIN, C_V31, C_HALF = 0, 128, 192, 256, 264, 272, 273
C_END = 274
M_SLC, M_WIN, M_CMP = 0, SEQ, SEQ + WT * P
M_END = M_CMP + NCMP + 7 * 8 + 1


def shape_constants():
    c = np.zeros((P, C_END), np.float32)
    c[:, C_ID:C_ID + P] = np.eye(P, dtype=np.float32)
    inv = THETA ** (-(np.arange(ROT, dtype=np.float32) * 2.0) / (2 * ROT))
    pos = np.arange(SEQ, dtype=np.float32).reshape(NT, P).T
    ang = (pos[:, :, None] * inv.astype(np.float32)).astype(np.float32)
    c[:, C_COS:C_COS + NT * ROT] = np.cos(ang).reshape(P, -1)
    c[:, C_SIN:C_SIN + NT * ROT] = np.sin(ang).reshape(P, -1)
    end = np.arange(P, dtype=np.float32) * CSTR + CLEN - 1
    angc = (end[:, None] * inv.astype(np.float32)).astype(np.float32)
    c[:, C_CCOS:C_CCOS + ROT] = np.cos(angc)
    c[:, C_CSIN:C_CSIN + ROT] = np.sin(angc)
    c[:, C_V31] = np.arange(P) >= CLEN - 1
    c[:, C_HALF] = -0.5
    q = np.arange(P)[:, None]
    k = np.arange(P)[None, :]
    low = 0xF14A
    m = np.zeros((P, M_END), np.uint16)
    m[:, SEQ - P:SEQ] = np.where(k <= q, 0, low)
    m[:, M_WIN:M_WIN + P] = np.where(k > q, 0, low)
    m[:, M_WIN + (WT - 1) * P:M_WIN + WT * P] = np.where(k <= q, 0, low)
    i = np.arange(M_END - M_CMP)[None, :] - 7 * 8
    m[:, M_CMP:] = np.where(i * CSTR + CLEN - 1 <= q, 0, low)
    j, t = np.arange(P)[:, None], np.arange(P)[None, :]
    g = np.zeros((P, len(LEVELS), P), np.float32)
    for n, z in enumerate(LEVELS):
        g[:, n] = (j // z == t // z) & (j % z < z // 2) & (t % z >= z // 2)
    return c, m, g.reshape(P, -1)


def chunk_plan():
    return [("gqk", True, KD, 8, 512), ("gv", False, KD, 8, 512), ("kv3", False, KD, 8, 512),
            ("nq", False, KD, 8, 512), ("ag", True, KD, 6, 304), ("gz", False, KD, 8, 512),
            ("nz", True, KD, 8, 512),
            ("wo0", False, KD, 8, 512), ("wo1", False, KD, 8, 512),
            ("pg0", False, KD, 8, 512), ("pg1", False, KD, 8, 512),
            ("pp0", False, PLE // P, 8, 512), ("pp1", False, PLE // P, 8, 512)]


def build_program(nc, a):
    chunks = chunk_plan()
    cidx = {c[0]: i for i, c in enumerate(chunks)}
    piece0 = [sum(c[2] for c in chunks[:i]) for i in range(len(chunks) + 1)]
    bank0 = [sum(c[3] for c in chunks[:i]) for i in range(len(chunks) + 1)]
    RAW, SPLIT = 3, 3

    ctx = ExitStack()
    base = (nc.sbuf_base + 31) // 32 * 32
    used = [base]

    def region(kb):
        at = used[0]
        used[0] += int(kb * 1024)
        return at

    def sb(name, shape, dt, at):
        return nc.alloc_sbuf_tensor_at(name, shape, dt, offset=at)

    R1 = region(64)
    R2 = region(18)
    R3 = region(32)
    R4 = region(22)
    R5 = region(16)
    R6 = region(32)
    R7 = region(16)
    R8 = region(7.8)

    XTh = sb("xT_hi", [P, KD, SEQ], F32R, R1)
    XTl = sb("xT_lo", [P, KD, SEQ], F32R, R1 + 32768)
    raw = sb("w_raw", [P, RAW, 512], F32, R2)
    Wh = sb("w_hi", [P, SPLIT, 512], F32R, R2 + 6144)
    Wl = sb("w_lo", [P, SPLIT, 512], F32R, R2 + 12288)
    GQK = sb("gla_qkT", [P, 4, SEQ], F32, R3)
    GV = sb("gla_v", [P, NT, 512], F32, R3 + 16384)
    KSW = sb("rot_keys", [P, NT, 4, DH], F32, R4)
    AG = sb("gate_rank_T", [P, SEQ], F32, R4 + 8192)
    SG = sb("sigmoid_tmp", [P, 2, 512], F32, R4 + 12288)
    RT = sb("rot_tmp", [P, 3, 512], F32, R4 + 16384)
    VS = sb("v_hi_lo", [P, NT, 2, NKV, P], F32R, R5)
    XN = sb("x_tok", [P, NT, DM], F32, R6)
    NQ = sb("nsa_q", [P, NT, NH, DH], F32, R6)
    DC = sb("cmp_in", [P, 2, NKV, SEQ], F32, R6 + 16384)
    NZ = sb("nsa_zT", [P, 4, SEQ], F32, R6 + 16384)
    W1 = sb("cmp_w1", [P, 2, 16, P], F32, R7)
    GZ = sb("gla_z", [P, NT, 512], F32, R7)
    small = [R8]

    def sm(name, shape, dt=F32, size=4):
        n = size
        for s in shape[1:]:
            n *= s
        at = small[0]
        small[0] += (n + 31) // 32 * 32
        assert small[0] <= R8 + int(7.8 * 1024)
        return sb(name, shape, dt, at)

    CT = sm("consts", [P, C_END])
    gpre = sm("pre_gain", [P, KD])
    st = sm("stats", [P, 3, 8])
    GT = sm("gates", [P, NT, NH, 3])
    VC = sm("vc_hi_lo", [P, NKV, P], F32R)
    KCN = sm("kc_tok", [P, NKV, DH])
    NM = sm("neg_max", [P, 4 * 48])
    SU = sm("exp_sum", [P, 4 * 48])
    RG = sm("gate_over_sum", [P, 4 * 48])
    ident = CT[:, C_ID:C_ID + P]
    W2 = sm("cmp_w2", [P, 2, DH])
    PB = sm("cmp_pos", [P, 2, 16])
    HC = sb("cmp_h", [P, 2, P], F32, R6 + 16384)
    HCT = sb("cmp_hT", [P, 2, 128], F32, R6 + 17408)
    SC = sb("cmp_sig", [P, 2, P], F32, R6 + 18432 + 0)
    GAU = sb("gla_a_up", [P, 256], F32, R4 + 20480)
    GGN = sb("gla_gain", [P, GDV], F32, R4 + 21504)
    GBI = sb("gla_bias", [P, 2], F32, R4 + 22016)
    XB = sb("gla_x", [P, 2, 2, SEQ], F32, R1)
    GB = sb("gla_b", [P, 2, SEQ], F32, R1 + 16384)
    QTI = sb("gla_q_dec", [P, 2, SEQ], F32, R1 + 24576)
    KTI = sb("gla_k_dec", [P, 2, SEQ], F32, R1 + 32768)
    KTN = sb("gla_k_dec_tok", [P, NT, 256], F32, R1 + 40960)
    ATT = sb("gla_att", [P, NT, GH, P], F32, R1 + 49152)
    OG = sb("gla_o", [P, NT, 512], F32, R1)
    QP = [sb(f"gla_q_pairs{i}", [P, 2, NT, 2, P // 2], F32, at) for i, at in enumerate((R2 + 10240, R4 + 12288))]
    GM = sb("gla_masks", [P, len(LEVELS), P], F32, R2)
    HS = sb("gla_head_rows", [P, 2], F32, R2 + 9600)
    DG = sb("gla_diag", [P, NT, GH], F32, R2 + 9728)
    ONE = sb("gla_ones", [P, P], F32, R2 + 4096)
    GS = sb("gla_state", [P, 2, 2, P], F32, R2 + 4608)
    GBL = sb("gla_decay_last", [P, 2, NT], F32, R2 + 6656)
    GSS = sb("gla_ss", [P, 3, NT * GH], F32, R2 + 6784)
    GSQ = sb("gla_sq", [P, GH, P], F32, R2 + 10240)
    QS = sb("qT_hi_lo", [P, NH, SEQ], F32R, R1)
    K1 = sb("kT_hi_hi", [P, 4, SEQ], F32R, R1 + 32768)
    K2 = sb("kT_lo_lo", [P, 4, SEQ], F32R, R1 + 49152)
    PSL = sb("p_slc", [P, 2, GRP, SEQ], F32, R3)
    PWN = sb("p_win", [P, 2, GRP, WT * P], F32, R4)
    PCM = sb("p_cmp", [P, 2, GRP, 64], F32, R4 + 20480)
    PTh = sb("pT_hi", [P, 4, 512], F32R, R2)
    PTl = sb("pT_lo", [P, 4, 512], F32R, R2 + 8192)
    KC1 = sb("kcT_hi_hi", [P, NKV, 64], F32R, R2 + 16384)
    KC2 = sb("kcT_lo_lo", [P, NKV, 64], F32R, R2 + 16896)
    MK = sb("masks", [P, M_END], U16, R6)
    OB = sb("o_low_half", [64, 512], F32, R6 + 4096)
    OT = sb("o_sum", [P, 2, P], F32, R6 + 6144)
    MGh = sb("mix_glaT_hi", [P, 4, SEQ], F32R, R1)
    MGl = sb("mix_glaT_lo", [P, 4, SEQ], F32R, R1 + 16384)
    MNh = sb("mix_nsaT_hi", [P, 4, SEQ], F32R, R6)
    MNl = sb("mix_nsaT_lo", [P, 4, SEQ], F32R, R6 + 16384)
    H = sb("h_tok", [P, NT, DM], F32, R1 + 32768)
    MIX = sb("mixed", [P, NT, DM], F32, R3)
    GPO = sb("post_gain", [P, DM], F32, R4)
    GPL = sb("ple_gain", [P, DM], F32, R4 + 4096)
    TMP = sb("out_tmp", [P, 2, DM], F32, R4 + 8192)
    HTh = sb("hT_hi", [P, KD, SEQ], F32R, R1)
    HTl = sb("hT_lo", [P, KD, SEQ], F32R, R6)
    GATE = sb("ple_gate_e", [P, NT, DM], F32, R3)
    PR = sb("p_tok", [P, NT, PLE], F32, R5)
    pTh = sb("pT_ple_hi", [P, 2, SEQ], F32R, R7)
    pTl = sb("pT_ple_lo", [P, 2, SEQ], F32R, R7 + 8192)

    PSUM = ctx.enter_context(nc.psum_tensor("psum", [P, 8, 512], F32))

    def bank(i):
        return PSUM[:, i, :]

    def sem(name):
        return ctx.enter_context(nc.semaphore(name))

    s_const = sem("const_in")
    s_small = sem("small_in")
    s_x = [sem(f"x_in{t}") for t in range(NT)]
    s_ssq_a, s_ssq_d, s_rms = sem("x_sumsq_act"), sem("x_sumsq_dve"), sem("x_rms")
    s_xn, s_xtr, s_xhi, s_xlo = sem("x_scaled"), sem("x_turned"), sem("xT_hi_made"), sem("xT_lo_made")
    s_raw = [sem(f"w_raw_in{i}") for i in range(RAW)]
    s_whi, s_wlo, s_wused = sem("w_hi_made"), sem("w_lo_made"), sem("w_used")
    s_bank = sem("bank_done")
    s_eva, s_evd = sem("bank_read_act"), sem("bank_read_dve")
    s_sig, s_vhi, s_gain = sem("sigmoid_made"), sem("v_hi_made"), sem("gla_z_gained")
    s_d, s_p, s_a = sem("dve_chain"), sem("pool_chain"), sem("act_chain")
    s_cmp, s_csig, s_ch, s_cht, s_chc, s_cout, s_cvh, s_cend = (
        sem("cmp_hidden"), sem("cmp_sigmoid"), sem("cmp_silu"), sem("cmp_turned"),
        sem("cmp_hT"), sem("cmp_out"), sem("cmp_v_hi"), sem("cmp_end"))
    s_pow = sem("pool_mean")
    s_gm, s_mk, s_h, s_pin, s_gn = sem("gla_masks_in"), sem("masks_in"), sem("x_again_in"), sem("p_in"), sem("gains_in")
    s_hs, s_la, s_z, s_sp, s_b = sem("head_rows_zeroed"), sem("gla_rank_up"), sem("gla_z_made"), sem("gla_softplus"), sem("gla_b_made")
    s_dec_d, s_dec_e, s_dec_x = sem("decay_diff"), sem("decay_exp"), sem("decay_mul")
    s_qpz, s_dec_q, s_prod, s_diag = sem("q_pairs_zeroed"), sem("decay_mul_odd"), sem("qk_products"), sem("diagonal")
    s_lv, s_cp = sem("level_scores"), sem("level_taken")
    s_kt, s_ktn, s_ds, s_st, s_o, s_og = (
        sem("k_turned"), sem("k_tok"), sem("state_add"), sem("state_new"), sem("gla_out"), sem("gla_out_read"))
    s_oss, s_orms, s_gend = sem("gla_sumsq"), sem("gla_rms"), sem("gla_end")
    s_qtr, s_qhi, s_qlo = sem("qk_turned"), sem("qk_hi"), sem("qk_lo")
    s_qk, s_ttr, s_exp, s_rg, s_norm = (
        sem("scores"), sem("scores_masked"), sem("probs"), sem("gate_over_sum"), sem("probs_scaled"))
    s_normd, s_norma = sem("probs_scaled_dve"), sem("probs_scaled_act")
    s_pt, s_phi, s_plo, s_pv = sem("probs_turned"), sem("pT_hi_made"), sem("pT_lo_made"), sem("pv_done")
    s_ob, s_oev, s_nend = sem("o_half_copied"), sem("o_read"), sem("nsa_tile_end")
    s_mtr, s_mhi, s_mlo = sem("mix_turned"), sem("mixT_hi"), sem("mixT_lo")
    s_nhi, s_nlo = sem("nsaT_hi"), sem("nsaT_lo")
    s_hss, s_hr, s_hm, s_hh = sem("mix_sumsq"), sem("mix_rms"), sem("mix_scaled"), sem("h_made")
    s_htr, s_hhi, s_hlo = sem("h_turned"), sem("hT_hi_made"), sem("hT_lo_made")
    s_ptr, s_pphi, s_pplo = sem("p_turned"), sem("p_hi_made"), sem("p_lo_made")
    s_ess, s_er, s_em, s_eo, s_out = sem("e_sumsq"), sem("e_rms"), sem("e_scaled"), sem("out_made"), sem("out_stored")

    plain = {"gqk", "gv", "nq", "wo0", "wo1"}

    def reader(c, b):
        name = chunks[c][0]
        if name in plain:
            return "A" if b % 2 == 0 else "D"
        if name == "ag":
            return "A" if b in (0, 1, 2, 4) else "D"
        return "A" if name in ("pg0", "pg1") else "D"

    order = [(c, b) for c in range(len(chunks)) for b in range(chunks[c][3])]
    read_count = {}
    n_read = {"A": 0, "D": 0}
    for c, b in order:
        e = reader(c, b)
        n_read[e] += 1
        read_count[c, b] = n_read[e]

    def wait_read(eng, c, b):
        eng.wait_ge(s_eva if reader(c, b) == "A" else s_evd, read_count[c, b])

    def wait_chunk_read(eng, c, upto=None):
        last = {reader(c, b): b for b in range(chunks[c][3])}
        for b in last.values():
            wait_read(eng, c, b)

    piece = [(c, k) for c in range(len(chunks)) for k in range(chunks[c][2])]
    used_count = []
    for c, k in piece:
        used_count.append((used_count[-1] if used_count else 0) + (k < chunks[c][2] - 1))

    def wait_used(eng, i):
        c, k = piece[i]
        if k < chunks[c][2] - 1:
            eng.wait_ge(s_wused, used_count[i])
        else:
            eng.wait_ge(s_bank, bank0[c + 1])

    def raw_count(i):
        return sum(16 * (3 if chunks[piece[j][0]][0] == "ag" else 1) for j in range(i % RAW, i + 1, RAW))

    def halves(ap, z, first):
        v = ap.rearrange("p c (n z) -> p (c n) z", z=z)
        return v[:, :, 0:z // 2] if first else v[:, :, z // 2:z]

    def decay_queries(eng, lev, par):
        z, r = LEVELS[lev], slice(64 * par, 64 * par + 64)

        def second(ap):
            return ap.rearrange("p c (t n z) -> p (c t) n z", z=z, t=NT)[:, :, :, z // 2:z]

        out = QP[lev % 2][r].rearrange("p c t r (n z) -> p (c t) r n z", z=z // 2)[:, :, par]
        return eng.tensor_tensor(out, second(XB[r, lev % 2]), second(GQK[r, 0:2]), ALU.mult)

    qorder = [t for i in range(NT // 2) for t in (i, NT - 1 - i)]
    FP = 1000
    TRING, ORING = 2, 2
    steps = [(kv, qt, br) for kv in range(NKV) for qt in qorder for br in range(3)]

    def span(qt, br):
        if br == 0:
            return 0, NCMP
        n = qt + 1 if br == 1 else min(qt + 1, WT)
        return (qt + 1 - n) * P, n * P

    units = []
    first_unit = []
    for s, (kv, qt, br) in enumerate(steps):
        first_unit.append(len(units))
        units += [(s, i) for i in range(-(-span(qt, br)[1] // P))]
    first_unit.append(len(units))

    scaler = "VPAP"

    def whole(u):
        return u % FP == FP - 1

    def lows(u):
        return sum(not whole(v) for v in range(u + 1))


    def attention_timeline():
        ops, after = {}, {}
        for s, step in enumerate(steps):
            nk = span(*step[1:])[1]
            for g in range(GRP):
                n = GRP * s + g
                ops["score", n] = "P", 0.83 * nk + 60, s
                after["score", n] = [("mask_max", n - 2)]
                ops["mask_max", n] = "V", 1.04 * nk + 120, s
                after["mask_max", n] = [("score", n), ("turn", first_unit[s - 5] - 1 if s >= 6 else -1)]
                ops["exponent", n] = "A", 0.83 * nk + 250, s
                after["exponent", n] = [("mask_max", n)]
                e = scaler[g]
                ops["scale" + e, n] = e if e != "P" else "G", {"V": 0.6, "A": 0.83, "P": 3.6}[e] * nk + 150, s
                after["scale" + e, n] = [("gate", s)]
            ops["gate", s] = "V", 250, s
            after["gate", s] = [("exponent", GRP * s + GRP - 1)]
        for u, (s, i) in enumerate(units):
            j = s // 3
            ops["turn", u] = "P", 430, s
            after["turn", u] = [("scale" + scaler[g], GRP * s + g) for g in range(GRP)] \
                + [("high", u - TRING), ("low", u - TRING)]
            ops["high", u] = "A", 600, s
            after["high", u] = [("turn", u), ("values", u - 4)]
            if not whole(u):
                ops["low", u] = "V", 600, s
                after["low", u] = [("high", u)]
            ops["values", u] = "P", 860 if whole(u) else 430, s
            after["values", u] = [("high", u), ("low", u), ("output", j - ORING)]
        for j in range(2 * NT):
            ops["half", j] = "A", 600, 3 * j + 2
            after["half", j] = [("values", first_unit[3 * j + 3] - 1), ("output", j - 1)]
            ops["output", j] = "V", 900, 3 * j + 2
            after["output", j] = [("half", j)]
        kinds = ["values", "half", "output", "low", "high", "turn", "gate", "scaleV", "scaleA", "scaleP",
                 "exponent", "mask_max", "score"]
        queue = {k: sorted(n for kind, n in ops if kind == k) for k in kinds}
        free, end, line = {"P": 0, "V": 0, "A": 0, "G": 0}, {}, []
        while len(line) < len(ops):
            best = None
            for rank, kind in enumerate(kinds):
                if not queue[kind]:
                    continue
                op = kind, queue[kind][0]
                deps = [d for d in after[op] if d in ops]
                if any(d not in end for d in deps):
                    continue
                eng, dur, s = ops[op]
                start = max([free[eng]] + [end[d] + 100 for d in deps])
                key = (start, s, rank)
                if best is None or key < best[0]:
                    best = key, op
            (start, _, _), op = best
            eng, dur, _ = ops[op]
            free[eng] = end[op] = start + dur
            queue[op[0]].pop(0)
            line.append(op)
        return line

    timeline = attention_timeline()

    scaled = {"V": s_normd, "A": s_norma, "P": s_norm}

    def probs(s):
        kv, qt, br = steps[s]
        return (PCM, PSL, PWN)[br][:, (s // 3) % 2]

    def spread(copy, b):
        n, half = divmod(b - 2, 2)
        ps, t0 = bank(b), half * 512
        for kv in range(NKV):
            src = ps[64 * kv:64 * kv + 64]
            copy(DC[0:64, n, kv, t0:t0 + 512], src)
            ins = copy(DC[64:128, n, kv, t0:t0 + 511], src[:, 1:512]) if t0 == 0 else \
                copy(DC[64:128, n, kv, t0 - 1:t0 + 511], src)
        return ins

    block = ctx.enter_context(nc.Block())

    @block.sync
    def _(sp):
        sp.dma_start(CT[:], a["consts"]).then_inc(s_const, 16)
        sp.dma_start(gpre[:], a["pre_norm"][0].rearrange("(k p) -> p k", p=P),
                     allow_slow_non_contiguous=True).then_inc(s_const, 16)
        for t in range(NT):
            sp.dma_start(XN[:, t], a["x"][0, t * P:(t + 1) * P, :]).then_inc(s_x[t], 16)

        def load_piece(i):
            c, k = piece[i]
            name = chunks[c][0]
            if i >= RAW:
                sp.wait_ge(s_wlo, i - RAW + 1)
            dst, s_in = raw[:, i % RAW], s_raw[i % RAW]
            rows = slice(k * P, (k + 1) * P)
            w = a["w_in"][0]
            if name == "ag":
                sp.dma_start(dst[:, 0:24], w[rows, NG_:NG_ + 24]).then_inc(s_in, 16)
                sp.dma_start(dst[:, 32:48], w[rows, GA:GA + RANK]).then_inc(s_in, 16)
                sp.dma_start(dst[:, 48:304], w[rows, NKC:NKC + 256]).then_inc(s_in, 16)
                return
            if name[:2] in ("wo", "pg", "pp"):
                w = {"wo": a["w_out"], "pg": a["ple_gate"], "pp": a["ple_proj"]}[name[:2]][0]
                col = 512 * int(name[2])
            else:
                col = {"gqk": GQ, "gv": GV_, "kv3": NKS, "nq": NQ_, "gz": GZ_, "nz": NZ_}[name]
            sp.dma_start(dst, w[rows, col:col + 512]).then_inc(s_in, 16)

        for i in range(piece0[1]):
            load_piece(i)
        for n, (w1, w2, pe) in enumerate((("cmp_w1_k", "cmp_w2_k", "cmp_pos_k"),
                                          ("cmp_w1_v", "cmp_w2_v", "cmp_pos_v"))):
            for l in range(16):
                sp.dma_start(W1[:, n, l], a[w1][0, l * P:(l + 1) * P, :]).then_inc(s_small, 16)
            sp.dma_start(W2[:, n], a[w2][0]).then_inc(s_small, 16)
            sp.dma_start(PB[:, n], a[pe][0].rearrange("(l a) d -> (a d) l", a=2),
                         allow_slow_non_contiguous=True).then_inc(s_small, 16)
        sp.dma_start(GAU[32:32 + RANK, :], a["gla_a_up"][0]).then_inc(s_small, 16)
        sp.dma_start(GBI[:], a["gla_a_bias"][0].rearrange("(c p) -> p c", p=P),
                     allow_slow_non_contiguous=True).then_inc(s_small, 16)
        sp.dma_start(GGN[:], a["gla_out_norm"][0].partition_broadcast(P)).then_inc(s_small, 16)
        for i in range(piece0[1], piece0[cidx["wo0"]]):
            load_piece(i)

        wait_used(sp, piece0[cidx["wo0"]] - 1)
        sp.dma_start(GM[:], a["gla_masks"].rearrange("p (l j) -> p l j", j=P)).then_inc(s_gm, 16)

        sp.wait_ge(s_qtr, 8)
        sp.dma_start(MK[:], a["masks"]).then_inc(s_mk, 16)

        sp.wait_ge(s_pv, len(units))
        for i in range(piece0[cidx["wo0"]], piece0[cidx["wo0"]] + RAW):
            load_piece(i)
        for t in range(NT):
            sp.dma_start(H[:, t], a["x"][0, t * P:(t + 1) * P, :]).then_inc(s_h, 16)
        sp.dma_start(GPO[:], a["post_norm"][0].partition_broadcast(P)).then_inc(s_gn, 16)
        sp.dma_start(GPL[:], a["ple_norm"][0].partition_broadcast(P)).then_inc(s_gn, 16)
        sp.dma_start(PR[:], a["p"][0, 0].rearrange("(t p) d -> p t d", p=P)).then_inc(s_pin, 16)
        for i in range(piece0[cidx["wo0"]] + RAW, len(piece)):
            load_piece(i)

        for t in range(NT):
            sp.wait_ge(s_eo, t + 1)
            sp.dma_start(a["out"][0, t * P:(t + 1) * P, :], H[:, t]).then_inc(s_out, 16)
        sp.wait_ge(s_out, 16 * NT)

    @block.tensor
    def _(pe):
        pe.wait_ge(s_const, 32)
        for half in range(2):
            pe.wait_ge(s_xn, 4 * half + 4)
            for k in range(KD):
                u = half * KD + k
                if u >= 8:
                    pe.wait_ge(s_xlo, u - 7)
                for t in range(4):
                    mm = pe.transpose(bank(u % 8)[:, t * P:(t + 1) * P],
                                      XN[:, 4 * half + t, k * P:(k + 1) * P], ident)
                mm.then_inc(s_xtr, 1)
        pe.wait_ge(s_xlo, 2 * KD)

        def project(name, tokens):
            c = cidx[name]
            _, moving, kt, banks, _ = chunks[c]
            cuts = [(0, 48), (48, 176), (176, 304)] if name == "ag" else \
                [(m * P, (m + 1) * P) for m in range(4)]
            for k in range(kt):
                i = piece0[c] + k
                pe.wait_ge(s_wlo, i + 1)
                wh, wl = Wh[:, i % SPLIT], Wl[:, i % SPLIT]
                xh, xl = tokens(k)
                for b in range(banks):
                    if k == 0 and c > 0:
                        prev = c - 1
                        if b < chunks[prev][3] and name != "wo0":
                            wait_read(pe, prev, b)
                    if moving:
                        lo, hi = cuts[b // 2]
                        ts = slice(b % 2 * 512, b % 2 * 512 + 512)
                        ops = ((wh[:, lo:hi], xh[:, ts]), (wh[:, lo:hi], xl[:, ts]), (wl[:, lo:hi], xh[:, ts]))
                        out = bank(b)[0:hi - lo, :]
                    else:
                        ts = slice(b * P, b * P + P)
                        ops = ((xh[:, ts], wh), (xh[:, ts], wl), (xl[:, ts], wh))
                        out = bank(b)
                    for n, (lhs, rhs) in enumerate(ops):
                        mm = pe.matmul(out, lhs, rhs, start=(k == 0 and n == 0),
                                       stop=(k == kt - 1 and n == 2))
                    if k == kt - 1:
                        mm.then_inc(s_bank, 1)
                if k < kt - 1:
                    mm.then_inc(s_wused, 1)

        def xt(k):
            return XTh[:, k], XTl[:, k]

        for name in ("gqk", "gv", "kv3", "nq", "ag"):
            project(name, xt)

        wait_chunk_read(pe, cidx["nq"])
        wait_chunk_read(pe, cidx["ag"])
        pe.wait_ge(s_small, 16 * 39)
        for n in range(2):
            out = bank(6 + n)[0:CROWS, 0:P]
            for l in range(16):
                flat = DC[:, n].rearrange("p c t -> p (c t)")
                blocks = flat[:, 2 * l:2 * l + CSTR * (CROWS - 1) + 1:CSTR]
                pe.matmul(out, blocks, W1[:, n, l], start=(l == 0), stop=False)
            for l in range(16):
                mm = pe.matmul(out, PB[:, n, l:l + 1].to_broadcast([P, CROWS]), W1[:, n, l],
                               start=False, stop=(l == 15))
        mm.then_inc(s_cmp, 1)
        for t in range(NT):
            mm = pe.transpose(bank(5)[:, t * 24:t * 24 + 24], AG[0:24, t * P:(t + 1) * P], ident[0:24, 0:24])
        mm.then_inc(s_cmp, 1)
        pe.wait_ge(s_ch, 1)
        for n in range(2):
            mm = pe.transpose(bank(6 + n)[:, 0:CROWS], HC[0:CROWS, n, :], ident[0:CROWS, 0:CROWS])
        mm.then_inc(s_cht, 1)
        pe.wait_ge(s_chc, 1)
        for n in range(2):
            for kv in range(NKV):
                mm = pe.matmul(bank(6 + n)[0:NCMP, kv * DH:(kv + 1) * DH],
                               HCT[:, n, kv * 64:kv * 64 + NCMP], W2[:, n], start=True, stop=True)
        mm.then_inc(s_cout, 1)
        pe.wait_ge(s_cend, 1)

        project("gz", xt)
        project("nz", xt)

        wait_chunk_read(pe, cidx["nz"])
        for ct in range(2):
            for half in range(2):
                pe.matmul(bank(ct * 2 + half), GAU[32:32 + RANK, ct * P:(ct + 1) * P],
                          AG[32:32 + RANK, half * 512:half * 512 + 512],
                          start=True, stop=True).then_inc(s_la, 1)
        pe.wait_ge(s_prod, 1)
        pe.wait_ge(s_z, 4)
        for t in range(NT):
            for ct in range(2):
                mm = pe.matmul(bank(7)[:, t * GH + 2 * ct:t * GH + 2 * ct + 2],
                               ATT[:].rearrange("p t h q -> p (t h q)")[:, ct * SEQ + t * P:ct * SEQ + (t + 1) * P],
                               HS[:], start=True, stop=True)
        mm.then_inc(s_diag, 1)
        for lev in range(len(LEVELS)):
            pe.wait_ge(s_dec_x, 2 * lev + 2)
            pe.wait_ge(s_dec_q, lev + 1)
            for t in range(NT):
                u = lev * NT + t
                if u >= 7:
                    pe.wait_ge(s_cp, u - 6)
                for ct in range(2):
                    mm = pe.matmul(bank(u % 7)[:, ct * P:(ct + 1) * P], XB[:, lev % 2, ct, t * P:(t + 1) * P],
                                   QP[lev % 2][:, ct, t].rearrange("p r j -> p (r j)"), start=True, stop=True)
                mm.then_inc(s_lv, 1)
        pe.wait_ge(s_cp, NT * len(LEVELS))
        pe.wait_ge(s_p, 2)
        for w in range(4):
            for i in range(4):
                t, ct = 2 * w + i // 2, i % 2
                mm = pe.transpose(bank(w)[:, i * P:(i + 1) * P], KTI[:, ct, t * P:(t + 1) * P], ident)
            mm.then_inc(s_kt, 1)
        pe.wait_ge(s_ktn, 4)
        for t in range(NT):
            if t < NT - 1:
                if t >= 2:
                    pe.wait_ge(s_st, t - 1)
                for ct in range(2):
                    mm = pe.matmul(bank(2 * (t % 2) + ct)[:, 0:256], KTN[:, t, ct * P:(ct + 1) * P],
                                   GV[:, t, ct * 256:ct * 256 + 256], start=True, stop=True)
                mm.then_inc(s_ds, 1)
            if t >= 2:
                pe.wait_ge(s_og, t - 1)
            if t >= 1:
                pe.wait_ge(s_st, t)
            for h in range(GH):
                ct, par = h // 2, h % 2
                r = slice(64 * par, 64 * par + 64)
                out = bank(4 + 2 * (t % 2) + par)[:, ct * P:(ct + 1) * P]
                mm = pe.matmul(out, ATT[:, t, h], GV[:, t, h * P:(h + 1) * P],
                               start=True, stop=(t == 0))
                if t:
                    mm = pe.matmul(out, QTI[r, ct, t * P:(t + 1) * P], GS[r, t % 2, ct],
                                   start=False, stop=True)
            mm.then_inc(s_o, 1)
        pe.wait_ge(s_og, NT)

        pe.wait_ge(s_gend, NT)
        for u in range(13):
            if u >= 8:
                pe.wait_ge(s_qlo, u - 7)
            for i in range(4):
                t = 4 * (u % 2) + i
                if u < 8:
                    src = NQ[:, t, u // 2 * 2:u // 2 * 2 + 2].rearrange("p h d -> p (h d)")
                elif u < 12:
                    k = (u - 8) // 2 * 2
                    src = KSW[:, t, k:k + 2].rearrange("p h d -> p (h d)")
                if u < 12:
                    mm = pe.transpose(bank(u % 8)[:, i * P:(i + 1) * P], src, ident)
            if u == 12:
                mm = pe.transpose(bank(u % 8)[:, 0:NCMP], KCN[0:NCMP].rearrange("p h d -> p (h d)"),
                                  ident[0:NCMP, 0:NCMP])
            mm.then_inc(s_qtr, 1)
        pe.wait_ge(s_qlo, 13)

        def scores(n):
            s, g = divmod(n, GRP)
            kv, qt, br = steps[s]
            k0, nk = span(qt, br)
            if n >= 2:
                pe.wait_ge(s_ttr, n - 1)
            lhs = QS[:, kv * GRP + g, qt * P:(qt + 1) * P]
            for c0 in range(0, nk, 512):
                w = min(512, nk - c0) if br else NCMP + 1
                out = bank(n % 2 * 2 + c0 // 512)[:, 0:w]
                if br == 0:
                    kk = [KC1[:, kv], KC2[:, kv]]
                else:
                    ks = slice(k0 + c0, k0 + c0 + w)
                    kk = [K1[:, (br - 1) * NKV + kv, ks], K2[:, (br - 1) * NKV + kv, ks]]
                pe.matmul(out, lhs, kk[0], start=True, stop=False)
                mm = pe.matmul(out, lhs, kk[1], start=False, stop=True)
            mm.then_inc(s_qk, 1)

        def tile_made(u):
            if whole(u):
                pe.wait_ge(s_phi, u + 1)
            else:
                pe.wait_ge(s_plo, lows(u))

        def turn(u):
            s, i = units[u]
            kv, qt, br = steps[s]
            if i == 0:
                for e in sorted(set(scaler)):
                    pe.wait_ge(scaled[e], scaler.count(e) * (s + 1))
            if u >= TRING:
                tile_made(u - TRING)
            n = min(P, span(qt, br)[1])
            for g in range(GRP):
                mm = pe.transpose(bank(4 + u % TRING)[0:n, g * P:(g + 1) * P],
                                  probs(s)[:, g, i * P:i * P + n], ident)
            mm.then_inc(s_pt, 1)

        def values(u):
            s, i = units[u]
            kv, qt, br = steps[s]
            first = br == 0
            last = u + 1 == len(units) or (units[u + 1][0] // 3 != s // 3)
            j = s // 3
            if first and j >= ORING:
                pe.wait_ge(s_oev, j - ORING + 1)
            tile_made(u)
            n = NCMP if br == 0 else P
            v = VC[0:n, kv] if br == 0 else VS[:, span(qt, br)[0] // P + i, br - 1, kv]
            if whole(u):
                pe.matmul(bank(6 + j % ORING), v.bitcast(F32), PTh[0:n, u % 4].bitcast(F32),
                          start=first, stop=last).then_inc(s_pv, 1)
                return
            pe.matmul(bank(6 + j % ORING), v, PTh[0:n, u % 4], start=first, stop=False)
            pe.matmul(bank(6 + j % ORING), v, PTl[0:n, u % 4], start=False, stop=last).then_inc(s_pv, 1)

        for kind, n in timeline:
            if kind == "score":
                scores(n)
            elif kind == "turn":
                turn(n)
            elif kind == "values":
                values(n)

        pe.wait_ge(s_oev, 2 * NT)
        for u in range(8):
            for i in range(4):
                t = 4 * (u % 2) + i
                mm = pe.transpose(bank(u)[:, i * P:(i + 1) * P], GZ[:, t, (u // 2) * P:(u // 2 + 1) * P], ident)
            mm.then_inc(s_mtr, 1)
        pe.wait_ge(s_mlo, 8)
        pe.wait_ge(s_nlo, 4)

        def mixed(k):
            return (MGh[:, k], MGl[:, k]) if k < 4 else (MNh[:, k - 4], MNl[:, k - 4])

        project("wo0", mixed)
        project("wo1", mixed)
        wait_chunk_read(pe, cidx["wo1"])
        pe.wait_ge(s_pin, 16)
        for u in range(4):
            for i in range(4):
                t = 4 * (u % 2) + i
                mm = pe.transpose(bank(u)[:, i * P:(i + 1) * P], PR[:, t, (u // 2) * P:(u // 2 + 1) * P], ident)
            mm.then_inc(s_ptr, 1)
        for u in range(2 * KD):
            half, k = divmod(u, KD)
            pe.wait_ge(s_hh, 4 * half + 4)
            if u >= 4:
                pe.wait_ge(s_hlo, u - 3)
            for i in range(4):
                mm = pe.transpose(bank(4 + u % 4)[:, i * P:(i + 1) * P],
                                  H[:, 4 * half + i, k * P:(k + 1) * P], ident)
            mm.then_inc(s_htr, 1)
        pe.wait_ge(s_pplo, 4)
        pe.wait_ge(s_hlo, 2 * KD)
        for name in ("pg0", "pg1"):
            project(name, lambda k: (HTh[:, k], HTl[:, k]))
        for name in ("pp0", "pp1"):
            project(name, lambda k: (pTh[:, k], pTl[:, k]))

    @block.scalar
    def _(act):
        chain = [0]

        def link(ins):
            chain[0] += 1
            ins.then_inc(s_a, 1)
            act.wait_ge(s_a, chain[0])

        act.wait_ge(s_const, 32)
        for t in range(0, NT, 2):
            act.wait_ge(s_x[t], 16)
            link(act.activation(GQK[:, 0], XN[:, t], ACT.Square, accum_out=st[:, 0, t:t + 1]))

        def split_hi(i):
            c, k = piece[i]
            w = chunks[c][4]
            act.wait_ge(s_raw[i % RAW], raw_count(i))
            if i >= SPLIT:
                wait_used(act, i - SPLIT)
            act.activation(Wh[:, i % SPLIT, 0:w], raw[:, i % RAW, 0:w], ACT.Copy).then_inc(s_whi, 1)

        for u in range(2 * KD):
            half, k = divmod(u, KD)
            if u == 8:
                for i in range(2):
                    split_hi(i)
            act.wait_ge(s_xtr, u + 1)
            act.activation(XTh[:, k, half * 512:half * 512 + 512], bank(u % 8), ACT.Copy,
                           scale=gpre[:, k:k + 1]).then_inc(s_xhi, 1)

        def read_out(c):
            name = chunks[c][0]
            for b in range(chunks[c][3]):
                ps, done = bank(b), bank0[c] + b + 1
                mine = reader(c, b) == "A"
                out = None
                if name in plain and mine:
                    act.wait_ge(s_bank, done)
                    scale = 1.0
                    if name == "gqk":
                        out = GQK[:, b // 2, b % 2 * 512:b % 2 * 512 + 512]
                        scale = GDK ** -0.5 if b < 4 else 1.0
                    elif name == "gv":
                        out = GV[:, b]
                    elif name == "nq":
                        out = NQ[:, b].rearrange("p h d -> p (h d)")
                    else:
                        out = MIX[:, b, 512 * int(name[2]):512 * int(name[2]) + 512]
                    act.activation(out, ps, ACT.Copy, scale=scale).then_inc(s_eva, 1)
                elif name == "kv3":
                    act.wait_ge(s_bank, done)
                    v = ps.rearrange("p (r w c) -> p r w c", r=2, w=2)
                    act.activation(KSW[:, b].rearrange("p (r c) d -> p r (c d)", r=2), v[:, :, 0], ACT.Copy)
                    act.activation(VS[:, b, :, :, 0:DH], v[:, :, 1].rearrange("p r (c d) -> p r c d", c=2),
                                   ACT.Copy).then_inc(s_vhi, 1)
                elif name == "ag" and mine:
                    act.wait_ge(s_bank, done)
                    if b < 2:
                        cols = slice(b * 512, b * 512 + 512)
                        act.activation(AG[0:24, cols], ps[0:24], ACT.Sigmoid)
                        act.activation(AG[32:48, cols], ps[32:48], ACT.Copy).then_inc(s_eva, 1)
                    else:
                        spread(lambda o, i_: act.activation(o, i_, ACT.Copy), b).then_inc(s_eva, 1)
                elif name in ("gz", "nz"):
                    act.wait_ge(s_bank, done)
                    if b >= 2:
                        wait_read(act, c, b - 2)
                    elif name == "nz":
                        wait_read(act, cidx["gz"], 6 + b)
                    act.activation(SG[:, b % 2], ps, ACT.Sigmoid).then_inc(s_sig, 1)
                elif name in ("pg0", "pg1"):
                    act.wait_ge(s_bank, done)
                    col = 512 * int(name[2])
                    act.activation(GATE[:, b, col:col + 512], ps, ACT.Sigmoid).then_inc(s_eva, 1)

        def chunk_work(c, start):
            for k in range(start, chunks[c][2]):
                split_hi(piece0[c] + k)
                if k == 1 and c > 0 and chunks[c - 1][0] not in ("ag", "nz"):
                    read_out(c - 1)

        for c in range(cidx["wo0"]):
            chunk_work(c, 2 if c == 0 else 0)
            if chunks[c][0] == "ag":
                read_out(c)
                act.wait_ge(s_cmp, 1)
                for n in range(2):
                    ins = act.activation(SC[0:CROWS, n], bank(6 + n)[0:CROWS, 0:P], ACT.Sigmoid)
                ins.then_inc(s_csig, 1)
                act.wait_ge(s_cout, 1)
                act.activation(VC[0:NCMP, :, 0:DH], bank(7)[0:NCMP, 0:P].rearrange("p (c d) -> p c d", c=2),
                               ACT.Copy).then_inc(s_cvh, 1)
        read_out(cidx["nz"])

        act.wait_ge(s_z, 4)
        link(act.activation(XB[:, 0], GB[:], ACT.Abs))
        link(act.activation(XB[:, 0], XB[:, 0], ACT.Exp, scale=-1.0))
        act.activation(XB[:, 0], XB[:, 0], ACT.Ln, bias=1.0).then_inc(s_sp, 1)
        act.wait_ge(s_b, 1)
        act.activation(QTI[:], GB[:], ACT.Exp, scale=1.0 / 16).then_inc(s_dec_e, 1)
        act.activation(GBL[:], GB[:].rearrange("p c (t j) -> p c t j", j=P)[:, :, :, P - 1], ACT.Exp,
                       scale=1.0 / 16)
        act.wait_ge(s_dec_d, 1)
        act.activation(KTI[:], KTI[:], ACT.Exp, scale=1.0 / 16).then_inc(s_dec_e, 1)
        for lev, z in enumerate(LEVELS):
            x = XB[:, lev % 2]
            act.wait_ge(s_dec_d, lev + 2)
            act.activation(halves(x, z, True), halves(x, z, True), ACT.Exp, scale=-1.0 / 16)
            act.activation(halves(x, z, False), halves(x, z, False), ACT.Exp, scale=1.0 / 16).then_inc(s_dec_e, 1)
        for w in range(4):
            act.wait_ge(s_kt, w + 1)
            act.activation(KTN[:, 2 * w:2 * w + 2].rearrange("p t c -> p (t c)"), bank(w),
                           ACT.Copy).then_inc(s_ktn, 1)
        for t in range(NT):
            act.wait_ge(s_o, t + 1)
            b = 4 + 2 * (t % 2)
            link(act.activation(OG[:, t].rearrange("p (c r d) -> p r c d", c=2, r=2),
                                PSUM[:, b:b + 2, 0:256].rearrange("p r (c d) -> p r c d", c=2), ACT.Copy))
            for h in range(GH):
                ins = act.activation(GSQ[:, h], OG[:, t, h * P:(h + 1) * P], ACT.Square,
                                     accum_out=GSS[:, 0, t * GH + h:t * GH + h + 1])
            ins.then_inc(s_og, 1)

        for u in range(13):
            act.wait_ge(s_qtr, u + 1)
            cols = slice(u % 2 * 512, u % 2 * 512 + 512)
            for par in range(2):
                ps = bank(u % 8)[64 * par:64 * par + 64]
                if u < 8:
                    ins = act.activation(QS[0:64, u // 2 * 2 + par, cols], ps, ACT.Copy)
                    continue
                for r in (slice(0, 64), slice(64, 128)):
                    if u < 12:
                        ins = act.activation(K1[r, (u - 8) // 2 * 2 + par, cols], ps, ACT.Copy)
                    else:
                        ins = act.activation(KC1[r, par, 0:NCMP], ps[:, 0:NCMP], ACT.Copy)
            ins.then_inc(s_qhi, 1)

        def exponent(n):
            s, g = divmod(n, GRP)
            kv, qt, br = steps[s]
            nk = span(qt, br)[1]
            act.wait_ge(s_ttr, n + 1)
            act.activation(probs(s)[:, g, 0:nk], probs(s)[:, g, 0:nk], ACT.Exp, bias=NM[:, n:n + 1],
                           scale=-1.0, accum_out=SU[:, n:n + 1]).then_inc(s_exp, 1)

        def tile_hi(u):
            s, i = units[u]
            n = min(P, span(*steps[s][1:])[1])
            act.wait_ge(s_pt, u + 1)
            if u >= 4:
                act.wait_ge(s_pv, u - 3)
            out = PTh[0:n, u % 4]
            act.activation(out.bitcast(F32) if whole(u) else out, bank(4 + u % TRING)[0:n],
                           ACT.Copy).then_inc(s_phi, 1)

        def output_half(j):
            act.wait_ge(s_pv, first_unit[3 * (j + 1)])
            if j:
                act.wait_ge(s_oev, j)
            act.activation(OB[:], bank(6 + j % ORING)[64:128], ACT.Copy).then_inc(s_ob, 1)

        def scale_act(n):
            s, g = divmod(n, GRP)
            nk = span(*steps[s][1:])[1]
            act.wait_ge(s_rg, s + 1)
            x = probs(s)[:, g, 0:nk]
            act.activation(x, x, ACT.Copy, scale=RG[:, n:n + 1]).then_inc(s_norma, 1)

        for kind, n in timeline:
            if kind == "exponent":
                exponent(n)
            elif kind == "scaleA":
                scale_act(n)
            elif kind == "high":
                tile_hi(n)
            elif kind == "half":
                output_half(n)

        for u in range(8):
            act.wait_ge(s_mtr, u + 1)
            act.activation(MGh[:, u // 2, u % 2 * 512:u % 2 * 512 + 512], bank(u), ACT.Copy).then_inc(s_mhi, 1)
        act.wait_ge(s_nend, 2 * NT)
        for m in range(4):
            act.activation(MNh[:, m], NZ[:, m], ACT.Copy).then_inc(s_nhi, 1)
        chunk_work(cidx["wo0"], 0)
        chunk_work(cidx["wo1"], 0)
        split_hi(piece0[cidx["pg0"]])
        split_hi(piece0[cidx["pg0"]] + 1)
        read_out(cidx["wo1"])
        for u in range(4):
            act.wait_ge(s_ptr, u + 1)
            act.activation(pTh[:, u // 2, u % 2 * 512:u % 2 * 512 + 512], bank(u), ACT.Copy).then_inc(s_pphi, 1)
        for u in range(2 * KD):
            half, k = divmod(u, KD)
            act.wait_ge(s_htr, u + 1)
            act.activation(HTh[:, k, half * 512:half * 512 + 512], bank(4 + u % 4), ACT.Copy).then_inc(s_hhi, 1)
        for k in range(2, KD):
            split_hi(piece0[cidx["pg0"]] + k)
        chunk_work(cidx["pg1"], 0)
        chunk_work(cidx["pp0"], 0)
        chunk_work(cidx["pp1"], 0)

    @block.gpsimd
    def _(pool):
        chain = [0]

        def link(ins):
            chain[0] += 1
            ins.then_inc(s_p, 1)
            pool.wait_ge(s_p, chain[0])

        def inverse_rms(mean_eps, out, total, n, width, done):
            pool.tensor_scalar(mean_eps, total, 1.0 / n, EPS, ALU.mult, ALU.add).then_inc(s_pow, 1)
            pow_count[0] += 1
            pool.wait_ge(s_pow, pow_count[0])
            pool.tensor_tensor(out, mean_eps, CT[:, C_HALF:C_HALF + 1].to_broadcast([P, width]),
                               ALU.pow).then_inc(done, 1)

        pow_count = [0]
        pool.wait_ge(s_const, 32)
        pool.wait_ge(s_a, NT // 2)
        pool.wait_ge(s_ssq_d, 4)
        inverse_rms(st[:, 1], st[:, 2], st[:, 0], DM, NT, s_rms)

        def split_lo(i):
            c, k = piece[i]
            w = chunks[c][4]
            pool.wait_ge(s_whi, i + 1)
            pool.tensor_tensor(Wl[:, i % SPLIT, 0:w], raw[:, i % RAW, 0:w],
                               Wh[:, i % SPLIT, 0:w].bitcast(F32), ALU.subtract).then_inc(s_wlo, 1)

        for i in range(piece0[cidx["nz"]] + 2):
            split_lo(i)
        pool.wait_ge(s_small, 16 * 39)
        for t in range(NT):
            wait_read(pool, cidx["gz"], t)
            pool.tensor_tensor(GZ[:, t].rearrange("p (h d) -> p h d", h=GH),
                               GZ[:, t].rearrange("p (h d) -> p h d", h=GH),
                               GGN[:].unsqueeze(1).to_broadcast([P, GH, GDV]), ALU.mult).then_inc(s_gain, 1)
            if t < 6:
                split_lo(piece0[cidx["nz"]] + 2 + t)
        pool.wait_ge(s_dec_e, 1)
        pool.tensor_tensor(QTI[:], QTI[:], GQK[:, 0:2], ALU.mult).then_inc(s_p, 1)
        pool.wait_ge(s_dec_e, 2)
        pool.tensor_tensor(KTI[:], KTI[:], GQK[:, 2:4], ALU.mult).then_inc(s_p, 1)
        chain[0] += 2
        for lev, z in enumerate(LEVELS):
            x = XB[:, lev % 2]
            pool.wait_ge(s_dec_e, lev + 3)
            pool.tensor_tensor(halves(x, z, True), halves(x, z, True), halves(GQK[:, 2:4], z, True),
                               ALU.mult).then_inc(s_dec_x, 1)
            if lev == 0:
                pool.wait_ge(s_qpz, 1)
            decay_queries(pool, lev, 0).then_inc(s_dec_x, 1)
        pool.wait_ge(s_og, NT)
        inverse_rms(GSS[:, 1], GSS[:, 2], GSS[:, 0], GDV, NT * GH, s_orms)

        for n in [n for kind, n in timeline if kind == "scaleP"]:
            s, g = divmod(n, GRP)
            nk = span(*steps[s][1:])[1]
            pool.wait_ge(s_rg, s + 1)
            pool.tensor_scalar(probs(s)[:, g, 0:nk], probs(s)[:, g, 0:nk], RG[:, n:n + 1], None,
                               ALU.mult).then_inc(s_norm, 1)

        for i in range(piece0[cidx["wo0"]], piece0[cidx["pg0"]] + 2):
            split_lo(i)
        pool.wait_ge(s_hss, NT)
        inverse_rms(st[:, 1], st[:, 2], st[:, 0], DM, NT, s_hr)
        for t in range(NT):
            pool.wait_ge(s_hm, t + 1)
            pool.wait_ge(s_h, 16 * NT)
            pool.tensor_tensor(H[:, t], H[:, t], TMP[:, t % 2], ALU.add).then_inc(s_hh, 1)
        for i in range(piece0[cidx["pg0"]] + 2, len(piece)):
            split_lo(i)
        pool.wait_ge(s_ess, NT)
        inverse_rms(st[:, 1], st[:, 2], st[:, 0], DM, NT, s_er)
        for t in range(NT):
            pool.wait_ge(s_em, t + 1)
            pool.tensor_tensor(H[:, t], H[:, t], TMP[:, t % 2], ALU.add).then_inc(s_eo, 1)

    @block.vector
    def _(dve):
        chain = [0]

        def link(ins):
            chain[0] += 1
            ins.then_inc(s_d, 1)
            dve.wait_ge(s_d, chain[0])

        dve.wait_ge(s_const, 32)
        for t in range(1, NT, 2):
            dve.wait_ge(s_x[t], 16)
            if t > 1:
                dve.wait_ge(s_ssq_d, t // 2)
            dve.tensor_tensor_reduce(GV[:, 0:2].rearrange("p a b -> p (a b)"), XN[:, t], XN[:, t], 1.0, 0.0,
                                     ALU.mult, ALU.add, st[:, 0, t:t + 1]).then_inc(s_ssq_d, 1)
        dve.wait_ge(s_rms, 1)
        for t in range(NT):
            dve.wait_ge(s_x[t], 16)
            dve.tensor_scalar(XN[:, t], XN[:, t], st[:, 2, t:t + 1], None, ALU.mult).then_inc(s_xn, 1)
        for u in range(2 * KD):
            half, k = divmod(u, KD)
            cols = slice(half * 512, half * 512 + 512)
            dve.wait_ge(s_xhi, u + 1)
            dve.scalar_tensor_tensor(XTl[:, k, cols], bank(u % 8), gpre[:, k:k + 1],
                                     XTh[:, k, cols].bitcast(F32), ALU.mult, ALU.subtract).then_inc(s_xlo, 1)

        def read_out(c):
            name = chunks[c][0]
            for b in range(chunks[c][3]):
                ps, done = bank(b), bank0[c] + b + 1
                mine = reader(c, b) == "D"
                if not mine:
                    continue
                if name in plain:
                    dve.wait_ge(s_bank, done)
                    if name == "gqk":
                        out = GQK[:, b // 2, b % 2 * 512:b % 2 * 512 + 512]
                        if b < 4:
                            dve.tensor_scalar(out, ps, GDK ** -0.5, None, ALU.mult).then_inc(s_evd, 1)
                            continue
                    elif name == "gv":
                        out = GV[:, b]
                    elif name == "nq":
                        out = NQ[:, b].rearrange("p h d -> p (h d)")
                    else:
                        out = MIX[:, b, 512 * int(name[2]):512 * int(name[2]) + 512]
                    dve.tensor_copy(out, ps).then_inc(s_evd, 1)
                elif name == "kv3":
                    dve.wait_ge(s_vhi, b + 1)
                    v = ps.rearrange("p (r w c) -> p r w c", r=2, w=2)[:, :, 1]
                    dve.tensor_tensor(VS[:, b, :, :, DH:P], v.rearrange("p r (c d) -> p r c d", c=2),
                                      VS[:, b, :, :, 0:DH].bitcast(F32), ALU.subtract).then_inc(s_evd, 1)
                elif name == "ag":
                    dve.wait_ge(s_bank, done)
                    spread(lambda o, i_: dve.tensor_copy(o, i_), b).then_inc(s_evd, 1)
                elif name in ("gz", "nz"):
                    dve.wait_ge(s_sig, b + 1 + (8 if name == "nz" else 0))
                    out = GZ[:, b] if name == "gz" else NZ[:, b // 2, b % 2 * 512:b % 2 * 512 + 512]
                    dve.tensor_tensor(out, ps, SG[:, b % 2], ALU.mult).then_inc(s_evd, 1)
                elif name in ("pp0", "pp1"):
                    dve.wait_ge(s_bank, done)
                    col = 512 * int(name[2])
                    g = GATE[:, b, col:col + 512]
                    dve.tensor_tensor(g, ps, g, ALU.mult).then_inc(s_evd, 1)

        def rotate(x, cos, sin, n):
            x1, x2 = x[..., 0:ROT], x[..., ROT:2 * ROT]
            t1, t2 = RT[0:n, 0], RT[0:n, 1]
            sh = list(x1.shape)

            def like(t):
                size = 1
                for d in sh[1:]:
                    size *= d
                t = t[:, 0:size]
                return t.rearrange("p (a b c) -> p a b c", a=sh[1], b=sh[2]) if len(sh) == 4 \
                    else t.rearrange("p (a c) -> p a c", a=sh[1])

            t1, t2 = like(t1), like(t2)
            dve.tensor_tensor(t1, x1, sin, ALU.mult)
            link(dve.tensor_tensor(t2, x2, sin, ALU.mult))
            dve.tensor_tensor(x1, x1, cos, ALU.mult)
            link(dve.tensor_tensor(x2, x2, cos, ALU.mult))
            dve.tensor_tensor(x1, x1, t2, ALU.subtract)
            link(dve.tensor_tensor(x2, x2, t1, ALU.add))

        def tables(w):
            sh = [P, NT, w, ROT]
            cos = CT[:, C_COS:C_COS + NT * ROT].rearrange("p (t r) -> p t r", t=NT)
            sin = CT[:, C_SIN:C_SIN + NT * ROT].rearrange("p (t r) -> p t r", t=NT)
            return cos.unsqueeze(2).to_broadcast(sh), sin.unsqueeze(2).to_broadcast(sh)

        for c in range(cidx["wo0"]):
            read_out(c)
            name = chunks[c][0]
            if name == "kv3":
                rotate(KSW[:], *tables(4), P)
            elif name == "nq":
                wait_chunk_read(dve, c)
                rotate(NQ[:], *tables(NH), P)
            elif name == "ag":
                dve.wait_ge(s_csig, 1)
                dve.wait_ge(s_cmp, 2)
                for n in range(2):
                    dve.tensor_tensor(HC[0:CROWS, n], bank(6 + n)[0:CROWS, 0:P], SC[0:CROWS, n],
                                      ALU.mult)
                link(dve.tensor_copy(GT[:].rearrange("p t h b -> p (t h b)"), bank(5)[:, 0:NT * 24]))
                dve.tensor_scalar(GT[:, 0, :, 0], GT[:, 0, :, 0], CT[:, C_V31:C_V31 + 1], None,
                                  ALU.mult).then_inc(s_ch, 1)
                dve.wait_ge(s_cht, 1)
                for n in range(2):
                    ins = dve.tensor_copy(HCT[:, n, 0:CROWS], bank(6 + n)[:, 0:CROWS])
                ins.then_inc(s_chc, 1)
                dve.wait_ge(s_cout, 1)
                link(dve.tensor_copy(KCN[0:NCMP].rearrange("p c d -> p (c d)"), bank(6)[0:NCMP, 0:P]))
                dve.wait_ge(s_cvh, 1)
                dve.tensor_tensor(VC[0:NCMP, :, DH:P], bank(7)[0:NCMP, 0:P].rearrange("p (c d) -> p c d", c=2),
                                  VC[0:NCMP, :, 0:DH].bitcast(F32), ALU.subtract).then_inc(s_cend, 1)
                sh = [NCMP, NKV, ROT]
                rotate(KCN[0:NCMP], CT[0:NCMP, C_CCOS:C_CCOS + ROT].unsqueeze(1).to_broadcast(sh),
                       CT[0:NCMP, C_CSIN:C_CSIN + ROT].unsqueeze(1).to_broadcast(sh), NCMP)

        wait_used(dve, piece0[cidx["wo0"]] - 1)
        dve.memset(ONE[:], 1.0)
        for i in range(2):
            dve.memset(HS[:, i:i + 1], 0.0).then_inc(s_hs, 1)
        dve.wait_ge(s_hs, 2)
        for i in range(2):
            dve.memset(HS[64 * i:64 * i + 64, i:i + 1], 1.0)
        dve.tensor_tensor(ATT[:].rearrange("p t h q -> p (t h q)")[:, 0:2 * SEQ],
                          GQK[:, 0:2].rearrange("p c t -> p (c t)"),
                          GQK[:, 2:4].rearrange("p c t -> p (c t)"), ALU.mult).then_inc(s_prod, 1)
        for i in range(2):
            ins = dve.memset(QP[i][:].rearrange("p c t r j -> p (c t r j)"), 0.0)
        ins.then_inc(s_qpz, 1)
        for i in range(4):
            ct, half = divmod(i, 2)
            dve.wait_ge(s_la, i + 1)
            dve.tensor_scalar(GB[:, ct, half * 512:half * 512 + 512], bank(i), GBI[:, ct:ct + 1], None,
                              ALU.add).then_inc(s_z, 1)
        dve.wait_ge(s_sp, 1)
        link(dve.scalar_tensor_tensor(XB[:, 1], GB[:], 0.0, XB[:, 0], ALU.min, ALU.subtract))
        for ct in range(2):
            for t in range(NT):
                ts = slice(t * P, (t + 1) * P)
                ins = dve.tensor_tensor_scan(GB[:, ct, ts], ONE[:], XB[:, 1, ct, ts], 0.0, ALU.mult, ALU.add)
        ins.then_inc(s_b, 1)
        dve.wait_ge(s_b, 1)
        b3 = GB[:].rearrange("p c (t j) -> p (c t) j", j=P)
        dve.tensor_tensor(KTI[:].rearrange("p c (t j) -> p (c t) j", j=P),
                          b3[:, :, P - 1:P].to_broadcast([P, 2 * NT, P]), b3, ALU.subtract).then_inc(s_dec_d, 1)

        def level_diff(lev):
            z = LEVELS[lev]
            if lev >= 2:
                dve.wait_ge(s_lv, NT * (lev - 1))
            b2 = GB[:].rearrange("p c (n z) -> p (c n) z", z=z)
            dve.tensor_tensor(XB[:, lev % 2].rearrange("p c (n z) -> p (c n) z", z=z), b2,
                              b2[:, :, z // 2 - 1:z // 2].to_broadcast([P, 2 * SEQ // z, z]),
                              ALU.subtract).then_inc(s_dec_d, 1)

        dve.wait_ge(s_gm, 16)
        level_diff(0)
        level_diff(1)
        dve.wait_ge(s_qpz, 1)
        dve.wait_ge(s_dec_e, 3)
        decay_queries(dve, 0, 1).then_inc(s_dec_q, 1)
        dve.wait_ge(s_diag, 1)
        link(dve.tensor_copy(DG[:].rearrange("p t h -> p (t h)"), bank(7)[:, 0:NT * GH]))
        for t in range(NT):
            link(dve.tensor_tensor(ATT[:, t], ident.unsqueeze(1).to_broadcast([P, GH, P]),
                                   DG[:, t].unsqueeze(2).to_broadcast([P, GH, P]), ALU.mult))
        for lev, z in enumerate(LEVELS):
            if lev + 1 < len(LEVELS):
                dve.wait_ge(s_dec_e, lev + 4)
                decay_queries(dve, lev + 1, 1).then_inc(s_dec_q, 1)
            mask = GM[:, lev].bitcast(U32).rearrange("p (n z) -> p n z", z=z)[:, :, z // 2:z]
            for t in range(NT):
                u = lev * NT + t
                dve.wait_ge(s_lv, u + 1)
                dve.copy_predicated(
                    ATT[:, t].rearrange("p h (n z) -> p h n z", z=z)[:, :, :, z // 2:z],
                    mask.unsqueeze(1).to_broadcast([P, GH, P // z, z // 2]),
                    bank(u % 7)[:, 0:GH * P // 2].rearrange("p (h n z) -> p h n z", h=GH, z=z // 2)
                ).then_inc(s_cp, 1)
            if lev + 2 < len(LEVELS):
                level_diff(lev + 2)
        for t in range(NT - 1):
            dve.wait_ge(s_ds, t + 1)
            if t:
                dve.wait_ge(s_o, t)
                dve.wait_ge(s_st, t)
            for ct in range(2):
                for par in range(2):
                    r = slice(64 * par, 64 * par + 64)
                    new, add = GS[r, (t + 1) % 2, ct], bank(2 * (t % 2) + ct)[r, par * P:(par + 1) * P]
                    if t == 0:
                        ins = dve.tensor_copy(new, add)
                    else:
                        ins = dve.scalar_tensor_tensor(new, GS[r, t % 2, ct], GBL[r, ct, t:t + 1], add,
                                                       ALU.mult, ALU.add)
            ins.then_inc(s_st, 1)
        dve.wait_ge(s_orms, 1)
        for t in range(NT):
            dve.wait_ge(s_gain, t + 1)
            dve.wait_ge(s_og, t + 1)
            for h in range(GH):
                hs = slice(h * P, (h + 1) * P)
                i = t * GH + h
                ins = dve.scalar_tensor_tensor(GZ[:, t, hs], OG[:, t, hs], GSS[:, 2, i:i + 1], GZ[:, t, hs],
                                               ALU.mult, ALU.mult)
            ins.then_inc(s_gend, 1)

        for kc in (KC1, KC2):
            dve.memset(kc[:, :, NCMP:NCMP + 1].bitcast(F32), 0.0)
        for u in range(13):
            dve.wait_ge(s_qhi, u + 1)
            cols = slice(u % 2 * 512, u % 2 * 512 + 512)
            for par in range(2):
                ps = bank(u % 8)[64 * par:64 * par + 64]
                if u < 8:
                    h = u // 2 * 2 + par
                    ins = dve.tensor_tensor(QS[64:128, h, cols], ps, QS[0:64, h, cols].bitcast(F32),
                                            ALU.subtract)
                    continue
                for r in (slice(0, 64), slice(64, 128)):
                    if u < 12:
                        k = (u - 8) // 2 * 2 + par
                        ins = dve.tensor_tensor(K2[r, k, cols], ps, K1[r, k, cols].bitcast(F32), ALU.subtract)
                    else:
                        ins = dve.tensor_tensor(KC2[r, par, 0:NCMP], ps[:, 0:NCMP],
                                                KC1[r, par, 0:NCMP].bitcast(F32), ALU.subtract)
            ins.then_inc(s_qlo, 1)
        dve.wait_ge(s_mk, 16)

        def mask_max(n):
            s, g = divmod(n, GRP)
            kv, qt, br = steps[s]
            nk = span(qt, br)[1]
            m0 = {0: M_CMP + 7 * 8 - 8 * qt, 1: SEQ - nk, 2: M_WIN + WT * P - nk}[br]
            dve.wait_ge(s_qk, n + 1)
            if g == 0 and s >= 6:
                dve.wait_ge(s_pt, first_unit[s - 5])
            ps = PSUM[:, n % 2 * 2:n % 2 * 2 + 2].rearrange("p a b -> p (a b)")[:, 0:nk]
            dve.tensor_tensor_reduce(probs(s)[:, g, 0:nk], ps, MK[:, m0:m0 + nk].bitcast(BF16),
                                     -(DH ** -0.5), 3.0e38, ALU.add, ALU.min,
                                     NM[:, n:n + 1]).then_inc(s_ttr, 1)

        def gate_over_sum(s):
            kv, qt, br = steps[s]
            n = slice(GRP * s, GRP * s + GRP)
            dve.wait_ge(s_exp, GRP * (s + 1))
            link(dve.reciprocal(RG[:, n], SU[:, n]))
            dve.tensor_tensor(RG[:, n], RG[:, n], GT[:, qt, kv * GRP:(kv + 1) * GRP, br],
                              ALU.mult).then_inc(s_rg, 1)

        def scale_dve(n):
            s, g = divmod(n, GRP)
            nk = span(*steps[s][1:])[1]
            dve.wait_ge(s_rg, s + 1)
            x = probs(s)[:, g, 0:nk]
            dve.tensor_scalar(x, x, RG[:, n:n + 1], None, ALU.mult).then_inc(s_normd, 1)

        def tile_lo(u):
            s, i = units[u]
            n = min(P, span(*steps[s][1:])[1])
            dve.wait_ge(s_phi, u + 1)
            dve.tensor_tensor(PTl[0:n, u % 4], bank(4 + u % TRING)[0:n], PTh[0:n, u % 4].bitcast(F32),
                              ALU.subtract).then_inc(s_plo, 1)

        def output_tile(j):
            kv, qt, _ = steps[3 * j]
            dve.wait_ge(s_ob, j + 1)
            o = bank(6 + j % ORING)[0:64].rearrange("p (a r q) -> p a r q", a=2, r=2)
            ob = OB[:].rearrange("p (a r q) -> p a r q", a=2, r=2)
            for par in range(2):
                ins = dve.tensor_tensor(OT[64 * par:64 * par + 64], o[:, :, par], ob[:, :, par], ALU.add)
            ins.then_inc(s_oev, 1)
            dve.wait_ge(s_oev, j + 1)
            z = NZ[:, 2 * kv:2 * kv + 2, qt * P:(qt + 1) * P]
            dve.tensor_tensor(z, z, OT[:], ALU.mult).then_inc(s_nend, 1)

        for kind, n in timeline:
            if kind == "mask_max":
                mask_max(n)
            elif kind == "gate":
                gate_over_sum(n)
            elif kind == "scaleV":
                scale_dve(n)
            elif kind == "low":
                tile_lo(n)
            elif kind == "output":
                output_tile(n)

        for u in range(8):
            cols = slice(u % 2 * 512, u % 2 * 512 + 512)
            dve.wait_ge(s_mhi, u + 1)
            dve.tensor_tensor(MGl[:, u // 2, cols], bank(u), MGh[:, u // 2, cols].bitcast(F32),
                              ALU.subtract).then_inc(s_mlo, 1)
        for m in range(4):
            dve.wait_ge(s_nhi, m + 1)
            dve.tensor_tensor(MNl[:, m], NZ[:, m], MNh[:, m].bitcast(F32), ALU.subtract).then_inc(s_nlo, 1)
        read_out(cidx["wo0"])
        read_out(cidx["wo1"])
        wait_chunk_read(dve, cidx["wo1"])

        def sum_squares(x, t, done):
            if t >= 2:
                dve.wait_ge(done, t - 1)
            dve.tensor_tensor_reduce(TMP[:, t % 2], x, x, 1.0, 0.0, ALU.mult, ALU.add,
                                     st[:, 0, t:t + 1]).then_inc(done, 1)

        for t in range(NT):
            sum_squares(MIX[:, t], t, s_hss)
        dve.wait_ge(s_gn, 32)
        dve.wait_ge(s_hr, 1)
        for t in range(NT):
            if t >= 2:
                dve.wait_ge(s_hh, t - 1)
            dve.scalar_tensor_tensor(TMP[:, t % 2], MIX[:, t], st[:, 2, t:t + 1], GPO[:],
                                     ALU.mult, ALU.mult).then_inc(s_hm, 1)
        for u in range(4):
            cols = slice(u % 2 * 512, u % 2 * 512 + 512)
            dve.wait_ge(s_pphi, u + 1)
            dve.tensor_tensor(pTl[:, u // 2, cols], bank(u), pTh[:, u // 2, cols].bitcast(F32),
                              ALU.subtract).then_inc(s_pplo, 1)
        for u in range(2 * KD):
            half, k = divmod(u, KD)
            cols = slice(half * 512, half * 512 + 512)
            dve.wait_ge(s_hhi, u + 1)
            dve.tensor_tensor(HTl[:, k, cols], bank(4 + u % 4), HTh[:, k, cols].bitcast(F32),
                              ALU.subtract).then_inc(s_hlo, 1)
        for name in ("pg0", "pg1", "pp0", "pp1"):
            read_out(cidx[name])
        for t in range(NT):
            wait_read(dve, cidx["pp1"], t)
            sum_squares(GATE[:, t], t, s_ess)
        dve.wait_ge(s_er, 1)
        for t in range(NT):
            if t >= 2:
                dve.wait_ge(s_eo, t - 1)
            dve.scalar_tensor_tensor(TMP[:, t % 2], GATE[:, t], st[:, 2, t:t + 1], GPL[:],
                                     ALU.mult, ALU.mult).then_inc(s_em, 1)

    ctx.close()


_INS = ["x", "p", "pre_norm", "w_in", "gla_a_up", "gla_a_bias", "gla_out_norm", "cmp_pos_k", "cmp_w1_k",
        "cmp_w2_k", "cmp_pos_v", "cmp_w1_v", "cmp_w2_v", "w_out", "post_norm", "ple_proj", "ple_gate",
        "ple_norm"]


def kernel(**inputs):
    import numpy as _np
    import concourse.bacc as _bacc
    from concourse import mybir as _mybir
    from concourse.bass_utils import run_bass_kernel_spmd as _run

    nc = _bacc.Bacc("TRN2", target_bir_lowering=False, num_devices=1)
    arrays, aps = {}, {}
    named = {n: _np.ascontiguousarray(inputs[n]) for n in _INS}
    named["consts"], named["masks"], named["gla_masks"] = shape_constants()
    for n, v in named.items():
        arrays[f"in_{n}"] = v
        aps[n] = nc.dram_tensor(f"in_{n}", v.shape, _mybir.dt.from_np(v.dtype), kind="ExternalInput").ap()
    aps["out"] = nc.dram_tensor("out_0", (1, SEQ, DM), _mybir.dt.float32, kind="ExternalOutput").ap()
    build_program(nc, aps)
    r = _run(nc, [arrays], core_ids=[0])
    return r.results[0]["out_0"]
```

```python
from contextlib import ExitStack

import numpy as np

import concourse.bass as bass
from concourse import mybir

F32 = mybir.dt.float32
F32R = mybir.dt.float32r
BF16 = mybir.dt.bfloat16
U16 = mybir.dt.uint16
U32 = mybir.dt.uint32
ALU = mybir.AluOpType
ACT = mybir.ActivationFunctionType

P = 128
SEQ, DM = 1024, 1024
NT = SEQ // P
KD = DM // P
EPS = 1e-6
GH, GDK, GDV, RANK = 4, 64, 128, 16
NH, NKV, DH = 8, 2, 64
GRP = NH // NKV
CLEN, CSTR = 32, 16
NCMP = (SEQ - CLEN) // CSTR + 1
CROWS = SEQ // CSTR + NCMP
WINDOW = 512
WT = WINDOW // P + 1
ROT = DH // 4 // 2
THETA = 500000.0
PLE = 256
GQ, GV_, GA, GZ_ = 0, 512, 1024, 1040
NQ_, NKC, NKS, NG_, NZ_ = 1552, 2064, 2320, 2832, 2856
SUM_ACT, SUM_DVE = (0, 2, 4, 6, 7), (1, 3, 5)
LEVELS = (2, 4, 8, 16, 32, 64, 128)

C_ID, C_COS, C_SIN, C_CCOS, C_CSIN, C_V31, C_HALF, C_ONE, C_HEAD = 0, 128, 192, 256, 264, 272, 273, 274, 275
C_END = 277
M_WIN, M_CMP = SEQ, SEQ + WT * P
M_END = M_CMP + NCMP + 7 * 8 + 1


def shape_constants():
    c = np.zeros((P, C_END), np.float32)
    c[:, C_ID:C_ID + P] = np.eye(P, dtype=np.float32)
    inv = THETA ** (-(np.arange(ROT, dtype=np.float32) * 2.0) / (2 * ROT))
    pos = np.arange(SEQ, dtype=np.float32).reshape(NT, P).T
    ang = (pos[:, :, None] * inv.astype(np.float32)).astype(np.float32)
    c[:, C_COS:C_COS + NT * ROT] = np.cos(ang).reshape(P, -1)
    c[:, C_SIN:C_SIN + NT * ROT] = np.sin(ang).reshape(P, -1)
    end = np.arange(P, dtype=np.float32) * CSTR + CLEN - 1
    angc = (end[:, None] * inv.astype(np.float32)).astype(np.float32)
    c[:, C_CCOS:C_CCOS + ROT] = np.cos(angc)
    c[:, C_CSIN:C_CSIN + ROT] = np.sin(angc)
    c[:, C_V31] = np.arange(P) >= CLEN - 1
    c[:, C_HALF] = -0.5
    c[:, C_ONE] = 1.0
    c[0:P // 2, C_HEAD] = c[P // 2:P, C_HEAD + 1] = 1.0
    q = np.arange(P)[:, None]
    k = np.arange(P)[None, :]
    low = 0xF14A
    m = np.zeros((P, M_END), np.uint16)
    m[:, SEQ - P:SEQ] = np.where(k <= q, 0, low)
    m[:, M_WIN:M_WIN + P] = np.where(k > q, 0, low)
    m[:, M_WIN + (WT - 1) * P:M_WIN + WT * P] = np.where(k <= q, 0, low)
    i = np.arange(M_END - M_CMP)[None, :] - 7 * 8
    m[:, M_CMP:] = np.where(i * CSTR + CLEN - 1 <= q, 0, low)
    j, t = np.arange(P)[:, None], np.arange(P)[None, :]
    g = np.zeros((P, len(LEVELS), P), np.float32)
    for n, z in enumerate(LEVELS):
        g[:, n] = (j // z == t // z) & (j % z < z // 2) & (t % z >= z // 2)
    return c, m, g.reshape(P, -1)


def chunk_plan():
    return [("gqk", True, KD, 8, 512), ("gv", False, KD, 8, 512), ("kv3", False, KD, 8, 512),
            ("nq", False, KD, 8, 512), ("ag", True, KD, 6, 304), ("gz", False, KD, 8, 512),
            ("nz", True, KD, 8, 512),
            ("woA", False, 2 * KD, 8, 512), ("woB", False, 2 * KD, 8, 512),
            ("pgA", False, 2 * KD, 8, 512), ("ppA", False, 2 * (PLE // P), 8, 512),
            ("pgB", False, 2 * KD, 8, 512), ("ppB", False, 2 * (PLE // P), 8, 512)]


def build_program(nc, a):
    chunks = chunk_plan()
    cidx = {c[0]: i for i, c in enumerate(chunks)}
    piece0 = [sum(c[2] for c in chunks[:i]) for i in range(len(chunks) + 1)]
    bank0 = [sum(c[3] for c in chunks[:i]) for i in range(len(chunks) + 1)]
    RAW, SPLIT = 3, 3

    ctx = ExitStack()
    base = (nc.sbuf_base + 31) // 32 * 32
    used = [base]

    def region(kb):
        at = used[0]
        used[0] += int(kb * 1024)
        return at

    def sb(name, shape, dt, at):
        return nc.alloc_sbuf_tensor_at(name, shape, dt, offset=at)

    R1 = region(64)
    R2 = region(18)
    R3 = region(32)
    R4 = region(22)
    R5 = region(16)
    R6 = region(32)
    R7 = region(16)
    R8 = region(7.9)

    XTh = sb("xT_hi", [P, KD, SEQ], F32R, R1)
    XTl = sb("xT_lo", [P, KD, SEQ], F32R, R1 + 32768)
    raw = sb("w_raw", [P, RAW, 512], F32, R2)
    Wh = sb("w_hi", [P, SPLIT, 512], F32R, R2 + 6144)
    Wl = sb("w_lo", [P, SPLIT, 512], F32R, R2 + 12288)
    GQK = sb("gla_qkT", [P, 4, SEQ], F32, R3)
    GV = sb("gla_v", [P, NT, 512], F32, R3 + 16384)
    KSW = sb("rot_keys", [P, NT, 4, DH], F32, R4)
    AG = sb("gate_rank_T", [P, SEQ], F32, R4 + 8192)
    SG = sb("sigmoid_tmp", [P, 2, 512], F32, R4 + 8192)
    RT = sb("rot_tmp", [P, 3, 512], F32, R4 + 16384)
    VS = sb("v_hi_lo", [P, NT, 2, NKV, P], F32R, R5)
    XN = sb("x_tok", [P, NT, DM], F32, R6)
    NQ = sb("nsa_q", [P, NT, NH, DH], F32, R6)
    DC = sb("cmp_in", [P, 2, NKV, SEQ], F32, R6 + 16384)
    NZ = sb("nsa_zT", [P, 4, SEQ], F32, R6 + 16384)
    W1 = sb("cmp_w1", [P, 2, 16, P], F32, R7)
    GZ = sb("gla_z", [P, NT, 512], F32, R7)
    small = [R8]

    def sm(name, shape, dt=F32, size=4):
        n = size
        for s in shape[1:]:
            n *= s
        at = small[0]
        small[0] += (n + 31) // 32 * 32
        assert small[0] <= R8 + int(7.9 * 1024)
        return sb(name, shape, dt, at)

    CT = sm("consts", [P, C_END])
    gpre = sm("pre_gain", [P, KD])
    st = sm("stats", [P, 3, 8])
    st2 = sm("stats_gated", [P, 3, 8])
    GT = sm("gates", [P, NT, NH, 3])
    VC = sm("vc_hi_lo", [P, NKV, P], F32R)
    KCN = sm("kc_tok", [P, NKV, DH])
    NM = sm("neg_max", [P, 4 * 48])
    SU = sm("exp_sum", [P, 4 * 48])
    RG = sm("gate_over_sum", [P, 4 * 48])
    ident = CT[:, C_ID:C_ID + P]
    W2 = sm("cmp_w2", [P, 2, DH])
    PB = sm("cmp_pos", [P, 2, 16])
    HC = sb("cmp_h", [P, 2, P], F32, R6 + 16384)
    HCT = sb("cmp_hT", [P, 2, 128], F32, R6 + 17408)
    SC = sb("cmp_sig", [P, 2, P], F32, R6 + 18432)
    GAU = sb("gla_a_up", [P, 256], F32, R4 + 20480)
    GGN = sb("gla_gain", [P, GDV], F32, R4 + 21504)
    GBI = sb("gla_bias", [P, 2], F32, R4 + 22016)
    XB = sb("gla_x", [P, 2, 2, SEQ], F32, R1)
    GB = sb("gla_b", [P, 2, SEQ], F32, R4 + 12288)
    GLS = sb("gla_softplus", [P, 2, SEQ], F32, R6 + 16384)
    GLZ = sb("gla_log_decay", [P, 2, SEQ], F32, R6 + 24576)
    QTI = sb("gla_q_dec", [P, 2, SEQ], F32, R1 + 24576)
    KTI = sb("gla_k_dec", [P, 2, SEQ], F32, R1 + 32768)
    KTN = sb("gla_k_dec_tok", [P, NT, 256], F32, R1 + 40960)
    ATT = sb("gla_att", [P, NT, GH, P], F32, R1 + 49152)
    OG = sb("gla_o", [P, NT, 512], F32, R1)
    QP = [sb(f"gla_q_pairs{i}", [P, 2, NT, 2, P // 2], F32, at) for i, at in enumerate((R2 + 10240, R1 + 16384))]
    GM = sb("gla_masks", [P, len(LEVELS), P], F32, R2)
    DG = sb("gla_diag", [P, NT, GH], F32, R2 + 9728)
    GS = sb("gla_state", [P, 2, 2, P], F32, R2 + 4608)
    GBL = sb("gla_decay_last", [P, 2, NT], F32, R2 + 6656)
    GSS = sb("gla_ss", [P, 3, NT * GH], F32, R2 + 6784)
    GSQ = sb("gla_sq", [P, GH, P], F32, R2 + 10240)
    QS = sb("qT_hi_lo", [P, NH, SEQ], F32R, R1)
    K1 = sb("kT_hi_hi", [P, 4, SEQ], F32R, R1 + 32768)
    K2 = sb("kT_lo_lo", [P, 4, SEQ], F32R, R1 + 49152)
    PSL = sb("p_slc", [P, 2, GRP, SEQ], F32, R3)
    PWN = sb("p_win", [P, 2, GRP, WT * P], F32, R4)
    PCM = sb("p_cmp", [P, 2, GRP, 64], F32, R4 + 20480)
    PTh = sb("pT_hi", [P, 4, 512], F32R, R2)
    PTl = sb("pT_lo", [P, 4, 512], F32R, R2 + 8192)
    KC1 = sb("kcT_hi_hi", [P, NKV, 64], F32R, R2 + 16384)
    KC2 = sb("kcT_lo_lo", [P, NKV, 64], F32R, R2 + 16896)
    MK = sb("masks", [P, M_END], U16, R6)
    OB = sb("o_low_half", [64, 512], F32, R6 + 4096)
    OT = sb("o_sum", [P, 2, P], F32, R6 + 6144)
    MGh = sb("mix_glaT_hi", [P, 4, SEQ], F32R, R1)
    MGl = sb("mix_glaT_lo", [P, 4, SEQ], F32R, R1 + 16384)
    MNh = sb("mix_nsaT_hi", [P, 4, SEQ], F32R, R6)
    MNl = sb("mix_nsaT_lo", [P, 4, SEQ], F32R, R6 + 16384)
    H = sb("h_tok", [P, NT, DM], F32, R1 + 32768)
    MIX = sb("mixed", [P, NT, DM], F32, R3)
    GPO = sb("post_gain", [P, DM], F32, R4)
    GPL = sb("ple_gain", [P, DM], F32, R4 + 4096)
    TMP = sb("out_tmp", [P, 3, DM], F32, R4 + 8192)
    HTh = sb("hT_hi", [P, KD, SEQ], F32R, R1)
    HTl = sb("hT_lo", [P, KD, SEQ], F32R, R6)
    GATE = sb("ple_gate_e", [P, NT, DM], F32, R3)
    SQ = sb("squares", [P, 2, DM], F32, R5 + 8192)
    PR = sb("p_tok", [P, NT, PLE], F32, R5)
    pTh = sb("pT_ple_hi", [P, 2, SEQ], F32R, R7)
    pTl = sb("pT_ple_lo", [P, 2, SEQ], F32R, R7 + 8192)

    PSUM = ctx.enter_context(nc.psum_tensor("psum", [P, 8, 512], F32))

    def bank(i):
        return PSUM[:, i, :]

    def sem(name):
        return ctx.enter_context(nc.semaphore(name))

    s_const = sem("const_in")
    s_small = sem("small_in")
    s_x = [sem(f"x_in{i}") for i in range(NT)]
    s_ssq_d = sem("x_sumsq_dve")
    s_rms = sem("x_rms")
    s_xn = sem("x_scaled")
    s_xtr = sem("x_turned")
    s_xhi = sem("xT_hi_made")
    s_xlo = sem("xT_lo_made")
    s_raw = [sem(f"w_raw_in{i}") for i in range(RAW)]
    s_whi = sem("w_hi_made")
    s_wlo = sem("w_lo_made")
    s_wused = sem("w_used")
    s_bank = sem("bank_done")
    s_eva = sem("bank_read_act")
    s_evd = sem("bank_read_dve")
    s_sig = sem("sigmoid_made")
    s_vhi = sem("v_hi_made")
    s_gain = sem("gla_z_gained")
    s_d = sem("dve_chain")
    s_a = sem("act_chain")
    s_cmp = sem("cmp_hidden")
    s_csig = sem("cmp_sigmoid")
    s_ch = sem("cmp_silu")
    s_cht = sem("cmp_turned")
    s_chc = sem("cmp_hT")
    s_cout = sem("cmp_out")
    s_cvh = sem("cmp_v_hi")
    s_cend = sem("cmp_end")
    s_mean = sem("pool_mean")
    s_gm = sem("gla_masks_in")
    s_mk = sem("masks_in")
    s_h = sem("x_again_in")
    s_pin = sem("p_in")
    s_gn = sem("gains_in")
    s_soft = sem("softplus_steps")
    s_dec_t = sem("decay_exp_tile")
    s_ddk = sem("decay_diff_k")
    s_la = sem("gla_rank_up")
    s_z = sem("gla_z_made")
    s_sp = sem("gla_softplus")
    s_b = sem("gla_b_made")
    s_dec_d = sem("decay_diff")
    s_dec_e = sem("decay_exp")
    s_dec_x = sem("decay_mul")
    s_qpz1 = sem("odd_q_pairs_zeroed")
    s_qpz = sem("q_pairs_zeroed")
    s_dec_q = sem("decay_mul_odd")
    s_prod = sem("qk_products")
    s_diag = sem("diagonal")
    s_lv = sem("level_scores")
    s_cp = sem("level_taken")
    s_kdec = sem("k_dec_made")
    s_qdec = sem("q_dec_made")
    s_kt = sem("k_turned")
    s_ktn = sem("k_tok")
    s_ds = sem("state_add")
    s_st = sem("state_new")
    s_o = sem("gla_out")
    s_og = sem("gla_out_read")
    s_orms = sem("gla_rms")
    s_gend = sem("gla_end")
    s_qtr = sem("qk_turned")
    s_qhi = sem("qk_hi")
    s_qlo = sem("qk_lo")
    s_qk = sem("scores")
    s_ttr = sem("scores_masked")
    s_exp = sem("probs")
    s_rg = sem("gate_over_sum")
    s_norm = sem("probs_scaled")
    s_normd = sem("probs_scaled_dve")
    s_norma = sem("probs_scaled_act")
    s_pt = sem("probs_turned")
    s_phi = sem("pT_hi_made")
    s_plo = sem("pT_lo_made")
    s_pv = sem("pv_done")
    s_ob = sem("o_half_copied")
    s_oev = sem("o_read")
    s_nend = sem("nsa_tile_end")
    s_mtr = sem("mix_turned")
    s_mhi = sem("mixT_hi")
    s_mlo = sem("mixT_lo")
    s_nhi = sem("nsaT_hi")
    s_nlo = sem("nsaT_lo")
    s_hss = sem("mix_sumsq")
    s_hr = sem("mix_rms")
    s_hh = sem("h_made")
    s_htr = sem("h_turned")
    s_hhi = sem("hT_hi_made")
    s_hlo = sem("hT_lo_made")
    s_ptr = sem("p_turned")
    s_pphi = sem("p_hi_made")
    s_pplo = sem("p_lo_made")
    s_ess = sem("e_sumsq")
    s_er = sem("e_rms")
    s_eo = sem("out_made")
    s_out = sem("out_stored")

    plain = {"gqk", "gv", "nq", "woA", "woB"}
    wide = {"woA", "woB", "pgA", "pgB", "ppA", "ppB"}

    def reader(c, b):
        name = chunks[c][0]
        if name in plain:
            return "A" if b % 2 == 0 else "D"
        if name == "ag":
            return "A" if b in (0, 1, 2, 4) else "D"
        return "A" if name in ("pgA", "pgB") else "D"

    order = [(c, b) for c in range(len(chunks)) for b in range(chunks[c][3])]
    read_count = {}
    n_read = {"A": 0, "D": 0}
    for c, b in order:
        e = reader(c, b)
        n_read[e] += 1
        read_count[c, b] = n_read[e]

    def wait_read(eng, c, b):
        eng.wait_ge(s_eva if reader(c, b) == "A" else s_evd, read_count[c, b])

    def wait_chunk_read(eng, c):
        last = {reader(c, b): b for b in range(chunks[c][3])}
        for b in last.values():
            wait_read(eng, c, b)

    piece = [(c, k) for c in range(len(chunks)) for k in range(chunks[c][2])]

    def final_piece(c):
        return chunks[c][2] - (2 if chunks[c][0] in wide else 1)

    def place(c, b):
        col, t = divmod(b, 4)
        return t + 4 * (chunks[c][0][2] == "B"), slice(512 * col, 512 * col + 512)

    used_count = []
    for c, k in piece:
        used_count.append((used_count[-1] if used_count else 0) + (k < final_piece(c)))

    def wait_used(eng, i):
        c, k = piece[i]
        if k < final_piece(c):
            eng.wait_ge(s_wused, used_count[i])
        elif k == chunks[c][2] - 1:
            eng.wait_ge(s_bank, bank0[c + 1])
        else:
            eng.wait_ge(s_bank, bank0[c] + 4)

    def raw_count(i):
        return sum(16 * (3 if chunks[piece[j][0]][0] == "ag" else 1) for j in range(i % RAW, i + 1, RAW))

    def halves(ap, z, first):
        v = ap.rearrange("p c (n z) -> p (c n) z", z=z)
        return v[:, :, 0:z // 2] if first else v[:, :, z // 2:z]

    def decay_queries(eng, lev, par):
        z, r = LEVELS[lev], slice(64 * par, 64 * par + 64)

        def second(ap):
            return ap.rearrange("p c (t n z) -> p (c t) n z", z=z, t=NT)[:, :, :, z // 2:z]

        out = QP[lev % 2][r].rearrange("p c t r (n z) -> p (c t) r n z", z=z // 2)[:, :, par]
        return eng.tensor_tensor(out, second(XB[r, lev % 2]), second(GQK[r, 0:2]), ALU.mult)

    qorder = [t for i in reversed(range(NT // 2)) for t in (NT - 1 - i, i)]
    TRING, ORING = 2, 2
    steps = [(kv, qt, br) for kv in range(NKV) for qt in qorder for br in range(3)]

    def span(qt, br):
        if br == 0:
            return 0, NCMP
        n = qt + 1 if br == 1 else min(qt + 1, WT)
        return (qt + 1 - n) * P, n * P

    units = []
    first_unit = []
    for s, (kv, qt, br) in enumerate(steps):
        first_unit.append(len(units))
        units += [(s, i) for i in range(-(-span(qt, br)[1] // P))]
    first_unit.append(len(units))

    scaler = ("PPPP", "VPAP", "VPAP")

    def scaled_count(e, s):
        return sum(scaler[br].count(e) for _, _, br in steps[:s + 1])

    def attention_timeline():
        ops, after = {}, {}
        for s, step in enumerate(steps):
            nk = span(*step[1:])[1]
            for g in range(GRP):
                n = GRP * s + g
                ops["score", n] = "P", 0.83 * nk + 60, s
                after["score", n] = [("mask_max", n - 2)]
                ops["mask_max", n] = "V", 1.04 * nk + 120, s
                after["mask_max", n] = [("score", n), ("turn", first_unit[s - 5] - 1 if s >= 6 else -1)]
                ops["exponent", n] = "A", 0.83 * nk + 250, s
                after["exponent", n] = [("mask_max", n)]
                e = scaler[step[2]][g]
                ops["scale" + e, n] = e if e != "P" else "G", {"V": 0.6, "A": 0.83, "P": 3.6}[e] * nk + 150, s
                after["scale" + e, n] = [("gate", s)]
            ops["gate", s] = "V", 250, s
            after["gate", s] = [("exponent", GRP * s + GRP - 1)]
        for u, (s, i) in enumerate(units):
            j = s // 3
            ops["turn", u] = "P", 430, s
            after["turn", u] = [("scale" + scaler[steps[s][2]][g], GRP * s + g) for g in range(GRP)] \
                + [("low", u - TRING)]
            ops["high", u] = "A", 600, s
            after["high", u] = [("turn", u), ("values", u - 4)]
            ops["low", u] = "V", 720, s
            after["low", u] = [("high", u)]
            ops["values", u] = "P", 430, s
            after["values", u] = [("low", u), ("output", j - ORING)]
        for j in range(2 * NT):
            ops["half", j] = "A", 600, 3 * j + 2
            after["half", j] = [("values", first_unit[3 * j + 3] - 1), ("output", j - 1)]
            ops["output", j] = "V", 900, 3 * j + 2
            after["output", j] = [("half", j)]
        kinds = ["values", "half", "output", "low", "high", "turn", "gate", "scaleV", "scaleA", "scaleP",
                 "exponent", "mask_max", "score"]
        queue = {k: sorted(n for kind, n in ops if kind == k) for k in kinds}
        free, end, line = {"P": 0, "V": 0, "A": 0, "G": 0}, {}, []
        while len(line) < len(ops):
            best = None
            for rank, kind in enumerate(kinds):
                if not queue[kind]:
                    continue
                op = kind, queue[kind][0]
                deps = [d for d in after[op] if d in ops]
                if any(d not in end for d in deps):
                    continue
                eng, dur, s = ops[op]
                start = max([free[eng]] + [end[d] + 200 for d in deps])
                key = (start + 10 * s, start, s, rank)
                if best is None or key < best[0]:
                    best = key, op
            (_, start, _, _), op = best
            eng, dur, _ = ops[op]
            free[eng] = end[op] = start + dur
            queue[op[0]].pop(0)
            line.append(op)
        return line

    timeline = attention_timeline()

    scaled = {"V": s_normd, "A": s_norma, "P": s_norm}

    stacks = [("k", h, half) for h in range(4) for half in range(2)] + [("c", 0, 0)] \
        + [("q", h, half) for h in range(4) for half in range(2)]

    def probs(s):
        kv, qt, br = steps[s]
        return (PCM, PSL, PWN)[br][:, (s // 3) % 2]

    def spread(copy, b):
        n, half = divmod(b - 2, 2)
        ps, t0 = bank(b), half * 512
        for kv in range(NKV):
            src = ps[64 * kv:64 * kv + 64]
            copy(DC[0:64, n, kv, t0:t0 + 512], src)
            ins = copy(DC[64:128, n, kv, t0:t0 + 511], src[:, 1:512]) if t0 == 0 else \
                copy(DC[64:128, n, kv, t0 - 1:t0 + 511], src)
        return ins

    block = ctx.enter_context(nc.Block())

    @block.sync
    def _(sp):
        sp.dma_start(CT[:], a["consts"]).then_inc(s_const, 16)
        sp.dma_start(gpre[:], a["pre_norm"][0].rearrange("(k p) -> p k", p=P),
                     allow_slow_non_contiguous=True).then_inc(s_const, 16)
        for t in range(NT):
            sp.dma_start(XN[:, t], a["x"][0, t * P:(t + 1) * P, :]).then_inc(s_x[t], 16)

        def load_piece(i):
            c, k = piece[i]
            name = chunks[c][0]
            if i >= RAW:
                sp.wait_ge(s_wlo, i - RAW + 1)
            dst, s_in = raw[:, i % RAW], s_raw[i % RAW]
            if name in wide:
                k, half = divmod(k, 2)
            rows = slice(k * P, (k + 1) * P)
            w = a["w_in"][0]
            if name == "ag":
                sp.dma_start(dst[:, 0:24], w[rows, NG_:NG_ + 24]).then_inc(s_in, 16)
                sp.dma_start(dst[:, 32:48], w[rows, GA:GA + RANK]).then_inc(s_in, 16)
                sp.dma_start(dst[:, 48:304], w[rows, NKC:NKC + 256]).then_inc(s_in, 16)
                return
            if name[:2] in ("wo", "pg", "pp"):
                w = {"wo": a["w_out"], "pg": a["ple_gate"], "pp": a["ple_proj"]}[name[:2]][0]
                col = 512 * half
            else:
                col = {"gqk": GQ, "gv": GV_, "kv3": NKS, "nq": NQ_, "gz": GZ_, "nz": NZ_}[name]
            sp.dma_start(dst, w[rows, col:col + 512]).then_inc(s_in, 16)

        for i in range(piece0[1]):
            load_piece(i)
        for n, (w1, w2, pe) in enumerate((("cmp_w1_k", "cmp_w2_k", "cmp_pos_k"),
                                          ("cmp_w1_v", "cmp_w2_v", "cmp_pos_v"))):
            for l in range(16):
                sp.dma_start(W1[:, n, l], a[w1][0, l * P:(l + 1) * P, :]).then_inc(s_small, 16)
            sp.dma_start(W2[:, n], a[w2][0]).then_inc(s_small, 16)
            sp.dma_start(PB[:, n], a[pe][0].rearrange("(l a) d -> (a d) l", a=2),
                         allow_slow_non_contiguous=True).then_inc(s_small, 16)
        sp.dma_start(GAU[32:32 + RANK, :], a["gla_a_up"][0]).then_inc(s_small, 16)
        sp.dma_start(GBI[:], a["gla_a_bias"][0].rearrange("(c p) -> p c", p=P),
                     allow_slow_non_contiguous=True).then_inc(s_small, 16)
        sp.dma_start(GGN[:], a["gla_out_norm"][0].partition_broadcast(P)).then_inc(s_small, 16)
        for i in range(piece0[1], piece0[cidx["woA"]]):
            load_piece(i)

        wait_used(sp, piece0[cidx["woA"]] - 1)
        sp.dma_start(GM[:], a["gla_masks"].rearrange("p (l j) -> p l j", j=P)).then_inc(s_gm, 16)

        sp.wait_ge(s_qtr, len(stacks))
        sp.dma_start(MK[:], a["masks"]).then_inc(s_mk, 16)

        sp.wait_ge(s_pv, len(units))
        for i in range(piece0[cidx["woA"]], len(piece)):
            load_piece(i)
            n = i - piece0[cidx["woA"]] - RAW
            if n == 0:
                sp.dma_start(PR[:], a["p"][0, 0].rearrange("(t p) d -> p t d", p=P)).then_inc(s_pin, 16)
            elif 0 < n <= NT:
                sp.dma_start(H[:, n - 1], a["x"][0, (n - 1) * P:n * P, :]).then_inc(s_h, 16)
            elif n == NT + 1:
                sp.dma_start(GPO[:], a["post_norm"][0].partition_broadcast(P)).then_inc(s_gn, 16)
                sp.dma_start(GPL[:], a["ple_norm"][0].partition_broadcast(P)).then_inc(s_gn, 16)

        for t in range(NT):
            sp.wait_ge(s_eo, t + 1)
            sp.dma_start(a["out"][0, t * P:(t + 1) * P, :], H[:, t]).then_inc(s_out, 16)
        sp.wait_ge(s_out, 16 * NT)

    @block.tensor
    def _(pe):
        pe.wait_ge(s_const, 32)
        for half in range(2):
            pe.wait_ge(s_xn, 4 * half + 4)
            for k in range(KD):
                u = half * KD + k
                if u >= 8:
                    pe.wait_ge(s_xlo, u - 7)
                for t in range(4):
                    mm = pe.transpose(bank(u % 8)[:, t * P:(t + 1) * P],
                                      XN[:, 4 * half + t, k * P:(k + 1) * P], ident)
                mm.then_inc(s_xtr, 1)
        def project(name, tokens, ready=None):
            c = cidx[name]
            _, moving, kt, banks, _ = chunks[c]
            cuts = [(0, 48), (48, 176), (176, 304)] if name == "ag" else \
                [(m * P, (m + 1) * P) for m in range(4)]
            for k in range(kt):
                i = piece0[c] + k
                pe.wait_ge(s_wlo, i + 1)
                wh, wl = Wh[:, i % SPLIT], Wl[:, i % SPLIT]
                kk, col = divmod(k, 2) if name in wide else (k, 0)
                first, final = kk == 0, k >= final_piece(c)
                xh, xl = tokens(kk)
                for b in range(4 * col, 4 * col + 4) if name in wide else range(banks):
                    if first and ready:
                        ready(b)
                    elif first and c > 0 and b < chunks[c - 1][3]:
                        wait_read(pe, c - 1, b)
                    if moving:
                        lo, hi = cuts[b // 2]
                        ts = slice(b % 2 * 512, b % 2 * 512 + 512)
                        ops = ((wh[:, lo:hi], xh[:, ts]), (wh[:, lo:hi], xl[:, ts]), (wl[:, lo:hi], xh[:, ts]))
                        out = bank(b)[0:hi - lo, :]
                    else:
                        t = place(c, b)[0] if name in wide else b
                        ts = slice(t * P, t * P + P)
                        ops = ((xh[:, ts], wh), (xh[:, ts], wl), (xl[:, ts], wh))
                        out = bank(b)
                    for n, (lhs, rhs) in enumerate(ops):
                        mm = pe.matmul(out, lhs, rhs, start=(first and n == 0), stop=(final and n == 2))
                    if final:
                        mm.then_inc(s_bank, 1)
                if not final:
                    mm.then_inc(s_wused, 1)

        def xt(k):
            return XTh[:, k], XTl[:, k]

        def first_xt(k):
            pe.wait_ge(s_xlo, KD + k + 1)
            return xt(k)

        project("gqk", first_xt, lambda b: pe.wait_ge(s_xlo, KD + b + 1))
        for name in ("gv", "kv3", "nq", "ag"):
            project(name, xt)

        wait_chunk_read(pe, cidx["nq"])
        pe.wait_ge(s_small, 16 * 39)
        for n in range(2):
            for l in range(16):
                pe.matmul(bank(6 + n)[0:CROWS, 0:P], PB[:, n, l:l + 1].to_broadcast([P, CROWS]), W1[:, n, l],
                          start=(l == 0), stop=False)
        wait_chunk_read(pe, cidx["ag"])
        for n in range(2):
            out = bank(6 + n)[0:CROWS, 0:P]
            for l in range(16):
                flat = DC[:, n].rearrange("p c t -> p (c t)")
                blocks = flat[:, 2 * l:2 * l + CSTR * (CROWS - 1) + 1:CSTR]
                mm = pe.matmul(out, blocks, W1[:, n, l], start=False, stop=(l == 15))
        mm.then_inc(s_cmp, 1)
        for t in range(NT):
            mm = pe.transpose(bank(5)[:, t * 24:t * 24 + 24], AG[0:24, t * P:(t + 1) * P], ident[0:24, 0:24])
        mm.then_inc(s_cmp, 1)
        for ct in range(2):
            for half in range(2):
                pe.matmul(bank(ct * 2 + half), GAU[32:32 + RANK, ct * P:(ct + 1) * P],
                          AG[32:32 + RANK, half * 512:half * 512 + 512],
                          start=True, stop=True).then_inc(s_la, 1)
        pe.wait_ge(s_ch, 1)
        for n in range(2):
            mm = pe.transpose(bank(6 + n)[:, 0:CROWS], HC[0:CROWS, n, :], ident[0:CROWS, 0:CROWS])
        mm.then_inc(s_cht, 1)
        pe.wait_ge(s_chc, 1)
        for n in range(2):
            for kv in range(NKV):
                mm = pe.matmul(bank(6 + n)[0:NCMP, kv * DH:(kv + 1) * DH],
                               HCT[:, n, kv * 64:kv * 64 + NCMP], W2[:, n], start=True, stop=True)
        mm.then_inc(s_cout, 1)

        project("gz", xt, lambda b: pe.wait_ge(s_cend, 1) if b >= 5 else pe.wait_ge(s_z, 4))
        project("nz", xt)

        wait_chunk_read(pe, cidx["nz"])
        pe.wait_ge(s_prod, 1)
        for t in range(NT):
            for ct in range(2):
                mm = pe.matmul(bank(7)[:, t * GH + 2 * ct:t * GH + 2 * ct + 2],
                               ATT[:].rearrange("p t h q -> p (t h q)")[:, ct * SEQ + t * P:ct * SEQ + (t + 1) * P],
                               CT[:, C_HEAD:C_HEAD + 2], start=True, stop=True)
        mm.then_inc(s_diag, 1)
        for lev in range(len(LEVELS)):
            pe.wait_ge(s_dec_x, 2 * lev + 2)
            pe.wait_ge(s_dec_q, lev + 1)
            for t in range(NT):
                u = lev * NT + t
                if u >= 7:
                    pe.wait_ge(s_cp, u - 6)
                for ct in range(2):
                    mm = pe.matmul(bank(u % 7)[:, ct * P:(ct + 1) * P], XB[:, lev % 2, ct, t * P:(t + 1) * P],
                                   QP[lev % 2][:, ct, t].rearrange("p r j -> p (r j)"), start=True, stop=True)
                mm.then_inc(s_lv, 1)
        pe.wait_ge(s_cp, NT * len(LEVELS))
        pe.wait_ge(s_kdec, 1)
        for w in range(4):
            for i in range(4):
                t, ct = 2 * w + i // 2, i % 2
                mm = pe.transpose(bank(w)[:, i * P:(i + 1) * P], KTI[:, ct, t * P:(t + 1) * P], ident)
            mm.then_inc(s_kt, 1)
        pe.wait_ge(s_ktn, 4)
        for t in range(NT):
            if t < NT - 1:
                if t >= 2:
                    pe.wait_ge(s_st, t - 1)
                for ct in range(2):
                    mm = pe.matmul(bank(2 * (t % 2) + ct)[:, 0:256], KTN[:, t, ct * P:(ct + 1) * P],
                                   GV[:, t, ct * 256:ct * 256 + 256], start=True, stop=True)
                mm.then_inc(s_ds, 1)
            if t >= 2:
                pe.wait_ge(s_og, t - 1)
            if t >= 1:
                pe.wait_ge(s_qdec, 1)
                pe.wait_ge(s_st, t)
            for h in range(GH):
                ct, par = h // 2, h % 2
                r = slice(64 * par, 64 * par + 64)
                out = bank(4 + 2 * (t % 2) + par)[:, ct * P:(ct + 1) * P]
                mm = pe.matmul(out, ATT[:, t, h], GV[:, t, h * P:(h + 1) * P],
                               start=True, stop=(t == 0))
                if t:
                    mm = pe.matmul(out, QTI[r, ct, t * P:(t + 1) * P], GS[r, t % 2, ct],
                                   start=False, stop=True)
            mm.then_inc(s_o, 1)
        pe.wait_ge(s_og, NT)

        for u in range(len(stacks)):
            kind, h, half = stacks[u]
            if u >= 8:
                pe.wait_ge(s_qlo, u - 7)
            if kind == "q":
                pe.wait_ge(s_gend, NT)
            for i in range(4):
                t = 4 * half + i
                if kind == "q":
                    mm = pe.transpose(bank(u % 8)[:, i * P:(i + 1) * P],
                                      NQ[:, t, 2 * h:2 * h + 2].rearrange("p h d -> p (h d)"), ident)
                elif kind == "k":
                    for r in (slice(0, 64), slice(64, 128)):
                        mm = pe.matmul(bank(u % 8)[r, i * P:(i + 1) * P], KSW[:, t, h], ident,
                                       start=True, stop=True)
            if kind == "c":
                for kv in range(NKV):
                    for r in (slice(0, 64), slice(64, 128)):
                        mm = pe.matmul(bank(u % 8)[r, kv * 64:kv * 64 + NCMP], KCN[0:NCMP, kv],
                                       ident[0:NCMP, 0:NCMP], start=True, stop=True)
            mm.then_inc(s_qtr, 1)
        pe.wait_ge(s_qlo, len(stacks))

        def scores(n):
            s, g = divmod(n, GRP)
            kv, qt, br = steps[s]
            k0, nk = span(qt, br)
            if n >= 2:
                pe.wait_ge(s_ttr, n - 1)
            lhs = QS[:, kv * GRP + g, qt * P:(qt + 1) * P]
            for c0 in range(0, nk, 512):
                w = min(512, nk - c0) if br else NCMP + 1
                out = bank(n % 2 * 2 + c0 // 512)[:, 0:w]
                if br == 0:
                    kk = [KC1[:, kv], KC2[:, kv]]
                else:
                    ks = slice(k0 + c0, k0 + c0 + w)
                    kk = [K1[:, (br - 1) * NKV + kv, ks], K2[:, (br - 1) * NKV + kv, ks]]
                pe.matmul(out, lhs, kk[0], start=True, stop=False)
                mm = pe.matmul(out, lhs, kk[1], start=False, stop=True)
            mm.then_inc(s_qk, 1)

        def turn(u):
            s, i = units[u]
            kv, qt, br = steps[s]
            if i == 0:
                for e in sorted(set(scaler[br])):
                    pe.wait_ge(scaled[e], scaled_count(e, s))
            if u >= TRING:
                pe.wait_ge(s_plo, u - TRING + 1)
            n = min(P, span(qt, br)[1])
            for g in range(GRP):
                mm = pe.transpose(bank(4 + u % TRING)[0:n, g * P:(g + 1) * P],
                                  probs(s)[:, g, i * P:i * P + n], ident)
            mm.then_inc(s_pt, 1)

        def values(u):
            s, i = units[u]
            kv, qt, br = steps[s]
            first = br == 0
            last = u + 1 == len(units) or (units[u + 1][0] // 3 != s // 3)
            j = s // 3
            if first and j >= ORING:
                pe.wait_ge(s_oev, j - ORING + 1)
            pe.wait_ge(s_plo, u + 1)
            n = NCMP if br == 0 else P
            v = VC[0:n, kv] if br == 0 else VS[:, span(qt, br)[0] // P + i, br - 1, kv]
            pe.matmul(bank(6 + j % ORING), v, PTh[0:n, u % 4], start=first, stop=False)
            pe.matmul(bank(6 + j % ORING), v, PTl[0:n, u % 4], start=False, stop=last).then_inc(s_pv, 1)

        for kind, n in timeline:
            if kind == "score":
                scores(n)
            elif kind == "turn":
                turn(n)
            elif kind == "values":
                values(n)

        pe.wait_ge(s_ttr, GRP * len(steps))
        for u in range(8):
            if u == 6:
                pe.wait_ge(s_oev, 2 * NT)
            for i in range(4):
                t = 4 * (u % 2) + i
                mm = pe.transpose(bank(u)[:, i * P:(i + 1) * P], GZ[:, t, (u // 2) * P:(u // 2 + 1) * P], ident)
            mm.then_inc(s_mtr, 1)

        def mixed(k):
            if k < 4:
                pe.wait_ge(s_mlo, 2 * k + 2)
                return MGh[:, k], MGl[:, k]
            pe.wait_ge(s_nlo, k - 3)
            return MNh[:, k - 4], MNl[:, k - 4]

        project("woA", mixed, lambda b: pe.wait_ge(s_mlo, b + 1))
        pe.wait_ge(s_pin, 16)
        for u in range(4):
            wait_read(pe, cidx["woA"], 4 + u)
            for i in range(4):
                t = 4 * (u % 2) + i
                mm = pe.transpose(bank(4 + u)[:, i * P:(i + 1) * P], PR[:, t, (u // 2) * P:(u // 2 + 1) * P], ident)
            mm.then_inc(s_ptr, 1)
        project("woB", mixed, lambda b: pe.wait_ge(s_pplo, b - 3) if b >= 4 else wait_read(pe, cidx["woA"], b))

        def turn_h(group):
            pe.wait_ge(s_hh, 4 * group + 4)
            for k in range(KD):
                wait_read(pe, cidx["pgA" if group else "woB"], k)
                for i in range(4):
                    mm = pe.transpose(bank(k)[:, i * P:(i + 1) * P],
                                      H[:, 4 * group + i, k * P:(k + 1) * P], ident)
                mm.then_inc(s_htr, 1)

        def turned_h(group):
            def tokens(k):
                pe.wait_ge(s_hlo, KD * group + k + 1)
                return HTh[:, k], HTl[:, k]
            return tokens

        def turned_p(k):
            return pTh[:, k], pTl[:, k]

        turn_h(0)
        project("pgA", turned_h(0), lambda b: pe.wait_ge(s_hlo, b + 1))
        turn_h(1)
        project("ppA", turned_p, lambda b: pe.wait_ge(s_hlo, KD + b + 1))
        project("pgB", turned_h(1))
        project("ppB", turned_p)

    @block.scalar
    def _(act):
        chain = [0]

        def link(ins):
            chain[0] += 1
            ins.then_inc(s_a, 1)
            act.wait_ge(s_a, chain[0])

        act.wait_ge(s_const, 32)
        for t in SUM_ACT:
            act.wait_ge(s_x[t], 16)
            link(act.activation(GQK[:, 0], XN[:, t], ACT.Square, accum_out=st[:, 0, t:t + 1]))

        def split_hi(i):
            c, k = piece[i]
            w = chunks[c][4]
            act.wait_ge(s_raw[i % RAW], raw_count(i))
            if i >= SPLIT:
                wait_used(act, i - SPLIT)
            act.activation(Wh[:, i % SPLIT, 0:w], raw[:, i % RAW, 0:w], ACT.Copy).then_inc(s_whi, 1)

        for u in range(2 * KD):
            half, k = divmod(u, KD)
            if u == 6:
                for i in range(2):
                    split_hi(i)
            act.wait_ge(s_xtr, u + 1)
            act.activation(XTh[:, k, half * 512:half * 512 + 512], bank(u % 8), ACT.Copy,
                           scale=gpre[:, k:k + 1]).then_inc(s_xhi, 1)

        def read_out(c):
            name = chunks[c][0]
            for b in range(chunks[c][3]):
                ps, done = bank(b), bank0[c] + b + 1
                mine = reader(c, b) == "A"
                out = None
                if name in plain and mine:
                    act.wait_ge(s_bank, done)
                    scale = 1.0
                    if name == "gqk":
                        out = GQK[:, b // 2, b % 2 * 512:b % 2 * 512 + 512]
                        scale = GDK ** -0.5 if b < 4 else 1.0
                    elif name == "gv":
                        out = GV[:, b]
                    elif name == "nq":
                        out = NQ[:, b].rearrange("p h d -> p (h d)")
                    else:
                        t, cols = place(c, b)
                        out = MIX[:, t, cols]
                    act.activation(out, ps, ACT.Copy, scale=scale).then_inc(s_eva, 1)
                elif name == "kv3":
                    act.wait_ge(s_bank, done)
                    v = ps.rearrange("p (r w c) -> p r w c", r=2, w=2)
                    act.activation(KSW[:, b].rearrange("p (r c) d -> p r (c d)", r=2), v[:, :, 0], ACT.Copy)
                    act.activation(VS[:, b, :, :, 0:DH], v[:, :, 1].rearrange("p r (c d) -> p r c d", c=2),
                                   ACT.Copy).then_inc(s_vhi, 1)
                elif name == "ag" and mine:
                    act.wait_ge(s_bank, done)
                    if b < 2:
                        cols = slice(b * 512, b * 512 + 512)
                        act.activation(AG[0:24, cols], ps[0:24], ACT.Sigmoid)
                        act.activation(AG[32:48, cols], ps[32:48], ACT.Copy).then_inc(s_eva, 1)
                    else:
                        spread(lambda o, i_: act.activation(o, i_, ACT.Copy), b).then_inc(s_eva, 1)
                elif name in ("gz", "nz"):
                    act.wait_ge(s_bank, done)
                    if b >= 2:
                        wait_read(act, c, b - 2)
                    elif name == "nz":
                        wait_read(act, cidx["gz"], 6 + b)
                    act.activation(SG[:, b % 2], ps, ACT.Sigmoid).then_inc(s_sig, 1)
                elif name in ("pgA", "pgB"):
                    act.wait_ge(s_bank, done)
                    t, cols = place(c, b)
                    act.activation(GATE[:, t, cols], ps, ACT.Sigmoid).then_inc(s_eva, 1)

        def softplus(n):
            if n == 0:
                act.wait_ge(s_z, 4)
                act.activation(GLS[:], GLZ[:], ACT.Abs).then_inc(s_soft, 1)
                return
            act.wait_ge(s_soft, n)
            if n == 1:
                act.activation(GLS[:], GLS[:], ACT.Exp, scale=-1.0).then_inc(s_soft, 1)
            else:
                act.activation(GLS[:], GLS[:], ACT.Ln, bias=1.0).then_inc(s_sp, 1)

        def chunk_work(c, start):
            for k in range(start, chunks[c][2]):
                split_hi(piece0[c] + k)
                if k == 1 and c > 0 and chunks[c - 1][0] not in ("ag", "nz"):
                    read_out(c - 1)
                if chunks[c][0] == "gz" and k in (2, 3, 4):
                    softplus(k - 2)

        for c in range(cidx["woA"]):
            chunk_work(c, 2 if c == 0 else 0)
            if chunks[c][0] == "ag":
                read_out(c)
                act.wait_ge(s_cmp, 1)
                for n in range(2):
                    ins = act.activation(SC[0:CROWS, n], bank(6 + n)[0:CROWS, 0:P], ACT.Sigmoid)
                ins.then_inc(s_csig, 1)
                act.wait_ge(s_cout, 1)
                act.activation(VC[0:NCMP, :, 0:DH], bank(7)[0:NCMP, 0:P].rearrange("p (c d) -> p c d", c=2),
                               ACT.Copy).then_inc(s_cvh, 1)
        read_out(cidx["nz"])

        def decays_to_ends():
            act.activation(QTI[:], GB[:], ACT.Exp, scale=1.0 / 16).then_inc(s_dec_t, 1)
            act.activation(GBL[:], GB[:].rearrange("p c (t j) -> p c t j", j=P)[:, :, :, P - 1], ACT.Exp,
                           scale=1.0 / 16)
            act.wait_ge(s_ddk, 1)
            act.activation(KTI[:], KTI[:], ACT.Exp, scale=1.0 / 16).then_inc(s_dec_t, 1)

        for lev, z in enumerate(LEVELS):
            x = XB[:, lev % 2]
            act.wait_ge(s_dec_d, lev + 1)
            act.activation(halves(x, z, True), halves(x, z, True), ACT.Exp, scale=-1.0 / 16)
            act.activation(halves(x, z, False), halves(x, z, False), ACT.Exp, scale=1.0 / 16).then_inc(s_dec_e, 1)
            if lev == 1:
                decays_to_ends()
        for w in range(4):
            act.wait_ge(s_kt, w + 1)
            act.activation(KTN[:, 2 * w:2 * w + 2].rearrange("p t c -> p (t c)"), bank(w),
                           ACT.Copy).then_inc(s_ktn, 1)
        for t in range(NT):
            act.wait_ge(s_o, t + 1)
            b = 4 + 2 * (t % 2)
            link(act.activation(OG[:, t].rearrange("p (c r d) -> p r c d", c=2, r=2),
                                PSUM[:, b:b + 2, 0:256].rearrange("p r (c d) -> p r c d", c=2), ACT.Copy))
            for h in range(GH):
                ins = act.activation(GSQ[:, h], OG[:, t, h * P:(h + 1) * P], ACT.Square,
                                     accum_out=GSS[:, 0, t * GH + h:t * GH + h + 1])
            ins.then_inc(s_og, 1)

        for u, (kind, h, half) in enumerate(stacks):
            act.wait_ge(s_qtr, u + 1)
            cols, ps = slice(half * 512, half * 512 + 512), bank(u % 8)
            if kind == "q":
                for par in range(2):
                    ins = act.activation(QS[0:64, 2 * h + par, cols], ps[64 * par:64 * par + 64], ACT.Copy)
            elif kind == "k":
                ins = act.activation(K1[:, h, cols], ps, ACT.Copy)
            else:
                ins = act.activation(KC1[:, :, 0:NCMP], ps[:, 0:P].rearrange("p (c j) -> p c j", c=2)[:, :, 0:NCMP],
                                     ACT.Copy)
            ins.then_inc(s_qhi, 1)

        def exponent(n):
            s, g = divmod(n, GRP)
            kv, qt, br = steps[s]
            nk = span(qt, br)[1]
            act.wait_ge(s_ttr, n + 1)
            act.activation(probs(s)[:, g, 0:nk], probs(s)[:, g, 0:nk], ACT.Exp, bias=NM[:, n:n + 1],
                           scale=-1.0, accum_out=SU[:, n:n + 1]).then_inc(s_exp, 1)

        def tile_hi(u):
            s, i = units[u]
            n = min(P, span(*steps[s][1:])[1])
            act.wait_ge(s_pt, u + 1)
            if u >= 4:
                act.wait_ge(s_pv, u - 3)
            act.activation(PTh[0:n, u % 4], bank(4 + u % TRING)[0:n], ACT.Copy).then_inc(s_phi, 1)

        def output_half(j):
            act.wait_ge(s_pv, first_unit[3 * (j + 1)])
            if j:
                act.wait_ge(s_oev, j)
            act.activation(OB[:], bank(6 + j % ORING)[64:128], ACT.Copy).then_inc(s_ob, 1)

        def scale_act(n):
            s, g = divmod(n, GRP)
            nk = span(*steps[s][1:])[1]
            act.wait_ge(s_rg, s + 1)
            x = probs(s)[:, g, 0:nk]
            act.activation(x, x, ACT.Copy, scale=RG[:, n:n + 1]).then_inc(s_norma, 1)

        for kind, n in timeline:
            if kind == "exponent":
                exponent(n)
            elif kind == "scaleA":
                scale_act(n)
            elif kind == "high":
                tile_hi(n)
            elif kind == "half":
                output_half(n)

        for u in range(8):
            act.wait_ge(s_mtr, u + 1)
            act.activation(MGh[:, u // 2, u % 2 * 512:u % 2 * 512 + 512], bank(u), ACT.Copy).then_inc(s_mhi, 1)
            if u in (3, 5):
                split_hi(piece0[cidx["woA"]] + (u - 3) // 2)

        def squares(x, t, total, done):
            act.activation(SQ[:, t % 2], x[:, t], ACT.Square, accum_out=total[:, 0, t:t + 1]).then_inc(done, 1)
            act.wait_ge(done, t + 1)

        def output_work(name, between, start=0):
            c = cidx[name]
            for k in range(start, chunks[c][2]):
                split_hi(piece0[c] + k)
                for job in between.get(k, ()):
                    job()

        def turn_p():
            for u in range(4):
                act.wait_ge(s_ptr, u + 1)
                act.activation(pTh[:, u // 2, u % 2 * 512:u % 2 * 512 + 512], bank(4 + u),
                               ACT.Copy).then_inc(s_pphi, 1)

        def mix_squares(group):
            wait_chunk_read(act, cidx["wo" + "AB"[group]])
            for t in range(4 * group, 4 * group + 4):
                squares(MIX, t, st, s_hss)

        def turn_h(group):
            for k in range(KD):
                act.wait_ge(s_htr, KD * group + k + 1)
                act.activation(HTh[:, k, 512 * group:512 * group + 512], bank(k), ACT.Copy).then_inc(s_hhi, 1)

        def gate_squares(group):
            for t in range(4 * group, 4 * group + 4):
                wait_read(act, cidx["pp" + "AB"[group]], 4 + t % 4)
                squares(GATE, t, st2, s_ess)

        def split_nsa():
            act.wait_ge(s_nend, 2 * NT)
            for m in range(4):
                act.activation(MNh[:, m], NZ[:, m], ACT.Copy).then_inc(s_nhi, 1)

        output_work("woA", {2: [split_nsa]}, start=2)
        output_work("woB", {1: [lambda: read_out(cidx["woA"]), turn_p], 3: [lambda: mix_squares(0)]})
        output_work("pgA", {1: [lambda: read_out(cidx["woB"]), lambda: turn_h(0)], 3: [lambda: mix_squares(1)]})
        output_work("ppA", {1: [lambda: read_out(cidx["pgA"]), lambda: turn_h(1)]})
        output_work("pgB", {3: [lambda: gate_squares(0)]})
        output_work("ppB", {1: [lambda: read_out(cidx["pgB"])]})
        gate_squares(1)

    @block.gpsimd
    def _(pool):
        def inverse_rms(mean_eps, out, total, n, width, done):
            pool.tensor_scalar(mean_eps, total, 1.0 / n, EPS, ALU.mult, ALU.add).then_inc(s_mean, 1)
            mean_count[0] += 1
            pool.wait_ge(s_mean, mean_count[0])
            pool.tensor_tensor(out, mean_eps, CT[:, C_HALF:C_HALF + 1].to_broadcast([P, width]),
                               ALU.pow).then_inc(done, 1)

        mean_count = [0]
        pool.wait_ge(s_const, 32)
        for group in range(2):
            ts = slice(4 * group, 4 * group + 4)
            pool.wait_ge(s_a, sum(t < ts.stop for t in SUM_ACT))
            pool.wait_ge(s_ssq_d, sum(t < ts.stop for t in SUM_DVE))
            inverse_rms(st[:, 1, ts], st[:, 2, ts], st[:, 0, ts], DM, 4, s_rms)

        def split_lo(i):
            c, k = piece[i]
            w = chunks[c][4]
            pool.wait_ge(s_whi, i + 1)
            pool.tensor_tensor(Wl[:, i % SPLIT, 0:w], raw[:, i % RAW, 0:w],
                               Wh[:, i % SPLIT, 0:w].bitcast(F32), ALU.subtract).then_inc(s_wlo, 1)

        for i in range(piece0[cidx["nz"]] + 2):
            split_lo(i)
        pool.wait_ge(s_small, 16 * 39)
        for t in range(NT):
            wait_read(pool, cidx["gz"], t)
            pool.tensor_tensor(GZ[:, t].rearrange("p (h d) -> p h d", h=GH),
                               GZ[:, t].rearrange("p (h d) -> p h d", h=GH),
                               GGN[:].unsqueeze(1).to_broadcast([P, GH, GDV]), ALU.mult).then_inc(s_gain, 1)
            if t < 6:
                split_lo(piece0[cidx["nz"]] + 2 + t)
        wait_used(pool, piece0[cidx["woA"]] - 1)
        pool.memset(QP[1][:].rearrange("p c t r j -> p (c t r j)"), 0.0).then_inc(s_qpz1, 1)
        for lev, z in enumerate(LEVELS):
            x = XB[:, lev % 2]
            pool.wait_ge(s_dec_e, lev + 1)
            pool.tensor_tensor(halves(x, z, True), halves(x, z, True), halves(GQK[:, 2:4], z, True),
                               ALU.mult).then_inc(s_dec_x, 1)
            if lev < 2:
                pool.wait_ge(s_qpz1 if lev else s_qpz, 1)
            decay_queries(pool, lev, 0).then_inc(s_dec_x, 1)
            if lev == 4:
                pool.wait_ge(s_dec_t, 2)
                pool.tensor_tensor(KTI[:], KTI[:], GQK[:, 2:4], ALU.mult).then_inc(s_kdec, 1)
        pool.tensor_tensor(QTI[:], QTI[:], GQK[:, 0:2], ALU.mult).then_inc(s_qdec, 1)
        for t in range(NT):
            pool.wait_ge(s_og, t + 1)
            ts = slice(GH * t, GH * t + GH)
            inverse_rms(GSS[:, 1, ts], GSS[:, 2, ts], GSS[:, 0, ts], GDV, GH, s_orms)

        for n in [n for kind, n in timeline if kind == "scaleP"]:
            s, g = divmod(n, GRP)
            nk = span(*steps[s][1:])[1]
            pool.wait_ge(s_rg, s + 1)
            pool.tensor_scalar(probs(s)[:, g, 0:nk], probs(s)[:, g, 0:nk], RG[:, n:n + 1], None,
                               ALU.mult).then_inc(s_norm, 1)

        for i in range(piece0[cidx["woA"]], len(piece)):
            split_lo(i)
            for name, stats, total, n, done in (("woB", st, s_hss, 4, s_hr), ("pgA", st, s_hss, 8, s_hr),
                                                ("pgB", st2, s_ess, 4, s_er)):
                if i == piece0[cidx[name]] + 5:
                    pool.wait_ge(total, n)
                    ts = slice(n - 4, n)
                    inverse_rms(stats[:, 1, ts], stats[:, 2, ts], stats[:, 0, ts], DM, 4, done)
        for t in range(4, NT):
            pool.wait_ge(s_ess, t + 1)
            ts = slice(t, t + 1)
            inverse_rms(st2[:, 1, ts], st2[:, 2, ts], st2[:, 0, ts], DM, 1, s_er)
    @block.vector
    def _(dve):
        chain = [0]

        def link(ins):
            chain[0] += 1
            ins.then_inc(s_d, 1)
            dve.wait_ge(s_d, chain[0])

        dve.wait_ge(s_const, 32)

        def sum_squares(n):
            t = SUM_DVE[n]
            dve.wait_ge(s_x[t], 16)
            if n:
                dve.wait_ge(s_ssq_d, n)
            dve.tensor_tensor_reduce(GV[:, 0:2].rearrange("p a b -> p (a b)"), XN[:, t], XN[:, t], 1.0, 0.0,
                                     ALU.mult, ALU.add, st[:, 0, t:t + 1]).then_inc(s_ssq_d, 1)

        def scale_x(group):
            dve.wait_ge(s_rms, group + 1)
            for t in range(4 * group, 4 * group + 4):
                dve.wait_ge(s_x[t], 16)
                dve.tensor_scalar(XN[:, t], XN[:, t], st[:, 2, t:t + 1], None, ALU.mult).then_inc(s_xn, 1)

        sum_squares(0)
        sum_squares(1)
        scale_x(0)
        sum_squares(2)
        for u in range(2 * KD):
            half, k = divmod(u, KD)
            if u == 2:
                scale_x(1)
            cols = slice(half * 512, half * 512 + 512)
            dve.wait_ge(s_xhi, u + 1)
            dve.scalar_tensor_tensor(XTl[:, k, cols], bank(u % 8), gpre[:, k:k + 1],
                                     XTh[:, k, cols].bitcast(F32), ALU.mult, ALU.subtract).then_inc(s_xlo, 1)

        def read_out(c):
            name = chunks[c][0]
            for b in range(chunks[c][3]):
                ps, done = bank(b), bank0[c] + b + 1
                mine = reader(c, b) == "D"
                if not mine:
                    continue
                if name in plain:
                    dve.wait_ge(s_bank, done)
                    if name == "gqk":
                        out = GQK[:, b // 2, b % 2 * 512:b % 2 * 512 + 512]
                        if b < 4:
                            dve.tensor_scalar(out, ps, GDK ** -0.5, None, ALU.mult).then_inc(s_evd, 1)
                            continue
                    elif name == "gv":
                        out = GV[:, b]
                    elif name == "nq":
                        out = NQ[:, b].rearrange("p h d -> p (h d)")
                    else:
                        t, cols = place(c, b)
                        out = MIX[:, t, cols]
                    dve.tensor_copy(out, ps).then_inc(s_evd, 1)
                elif name == "kv3":
                    dve.wait_ge(s_vhi, b + 1)
                    v = ps.rearrange("p (r w c) -> p r w c", r=2, w=2)[:, :, 1]
                    dve.tensor_tensor(VS[:, b, :, :, DH:P], v.rearrange("p r (c d) -> p r c d", c=2),
                                      VS[:, b, :, :, 0:DH].bitcast(F32), ALU.subtract).then_inc(s_evd, 1)
                elif name == "ag":
                    dve.wait_ge(s_bank, done)
                    spread(lambda o, i_: dve.tensor_copy(o, i_), b).then_inc(s_evd, 1)
                elif name in ("gz", "nz"):
                    dve.wait_ge(s_sig, b + 1 + (8 if name == "nz" else 0))
                    out = GZ[:, b] if name == "gz" else NZ[:, b // 2, b % 2 * 512:b % 2 * 512 + 512]
                    dve.tensor_tensor(out, ps, SG[:, b % 2], ALU.mult).then_inc(s_evd, 1)
                elif name in ("ppA", "ppB"):
                    dve.wait_ge(s_bank, done)
                    t, cols = place(c, b)
                    g = GATE[:, t, cols]
                    dve.tensor_tensor(g, ps, g, ALU.mult).then_inc(s_evd, 1)

        def rotate(x, cos, sin, n):
            x1, x2 = x[..., 0:ROT], x[..., ROT:2 * ROT]
            t1, t2 = RT[0:n, 0], RT[0:n, 1]
            sh = list(x1.shape)

            def like(t):
                size = 1
                for d in sh[1:]:
                    size *= d
                t = t[:, 0:size]
                return t.rearrange("p (a b c) -> p a b c", a=sh[1], b=sh[2]) if len(sh) == 4 \
                    else t.rearrange("p (a c) -> p a c", a=sh[1])

            t1, t2 = like(t1), like(t2)
            dve.tensor_tensor(t1, x1, sin, ALU.mult)
            link(dve.tensor_tensor(t2, x2, sin, ALU.mult))
            dve.tensor_tensor(x1, x1, cos, ALU.mult)
            link(dve.tensor_tensor(x2, x2, cos, ALU.mult))
            dve.tensor_tensor(x1, x1, t2, ALU.subtract)
            link(dve.tensor_tensor(x2, x2, t1, ALU.add))

        def raise_rank(ct):
            for half in range(2):
                dve.wait_ge(s_la, 2 * ct + half + 1)
                dve.tensor_scalar(GLZ[:, ct, half * 512:half * 512 + 512], bank(2 * ct + half),
                                  GBI[:, ct:ct + 1], None, ALU.add).then_inc(s_z, 1)

        def tables(w):
            sh = [P, NT, w, ROT]
            cos = CT[:, C_COS:C_COS + NT * ROT].rearrange("p (t r) -> p t r", t=NT)
            sin = CT[:, C_SIN:C_SIN + NT * ROT].rearrange("p (t r) -> p t r", t=NT)
            return cos.unsqueeze(2).to_broadcast(sh), sin.unsqueeze(2).to_broadcast(sh)

        for c in range(cidx["woA"]):
            read_out(c)
            name = chunks[c][0]
            if name == "kv3":
                rotate(KSW[:], *tables(4), P)
            elif name == "nq":
                wait_chunk_read(dve, c)
                rotate(NQ[:], *tables(NH), P)
            elif name == "ag":
                dve.wait_ge(s_csig, 1)
                dve.wait_ge(s_cmp, 2)
                for n in range(2):
                    dve.tensor_tensor(HC[0:CROWS, n], bank(6 + n)[0:CROWS, 0:P], SC[0:CROWS, n],
                                      ALU.mult)
                link(dve.tensor_copy(GT[:].rearrange("p t h b -> p (t h b)"), bank(5)[:, 0:NT * 24]))
                dve.tensor_scalar(GT[:, 0, :, 0], GT[:, 0, :, 0], CT[:, C_V31:C_V31 + 1], None,
                                  ALU.mult).then_inc(s_ch, 1)
                raise_rank(0)
                dve.wait_ge(s_cht, 1)
                for n in range(2):
                    ins = dve.tensor_copy(HCT[:, n, 0:CROWS], bank(6 + n)[:, 0:CROWS])
                ins.then_inc(s_chc, 1)
                raise_rank(1)
                dve.wait_ge(s_cout, 1)
                link(dve.tensor_copy(KCN[0:NCMP].rearrange("p c d -> p (c d)"), bank(6)[0:NCMP, 0:P]))
                dve.wait_ge(s_cvh, 1)
                dve.tensor_tensor(VC[0:NCMP, :, DH:P], bank(7)[0:NCMP, 0:P].rearrange("p (c d) -> p c d", c=2),
                                  VC[0:NCMP, :, 0:DH].bitcast(F32), ALU.subtract).then_inc(s_cend, 1)
                sh = [NCMP, NKV, ROT]
                rotate(KCN[0:NCMP], CT[0:NCMP, C_CCOS:C_CCOS + ROT].unsqueeze(1).to_broadcast(sh),
                       CT[0:NCMP, C_CSIN:C_CSIN + ROT].unsqueeze(1).to_broadcast(sh), NCMP)
                dve.wait_ge(s_sp, 1)
                link(dve.scalar_tensor_tensor(GLZ[:], GLZ[:], 0.0, GLS[:], ALU.min, ALU.subtract))
                one = CT[:, C_ONE:C_ONE + 1].to_broadcast([P, P])
                for ct in range(2):
                    for t in range(NT):
                        ts = slice(t * P, (t + 1) * P)
                        ins = dve.tensor_tensor_scan(GB[:, ct, ts], one, GLZ[:, ct, ts], 0.0,
                                                     ALU.mult, ALU.add)
                ins.then_inc(s_b, 1)
                dve.wait_ge(s_b, 1)

        wait_used(dve, piece0[cidx["woA"]] - 1)
        def level_diff(lev):
            z = LEVELS[lev]
            if lev >= 2:
                dve.wait_ge(s_lv, NT * (lev - 1))
            b2 = GB[:].rearrange("p c (n z) -> p (c n) z", z=z)
            dve.tensor_tensor(XB[:, lev % 2].rearrange("p c (n z) -> p (c n) z", z=z), b2,
                              b2[:, :, z // 2 - 1:z // 2].to_broadcast([P, 2 * SEQ // z, z]),
                              ALU.subtract).then_inc(s_dec_d, 1)

        level_diff(0)
        dve.tensor_tensor(ATT[:].rearrange("p t h q -> p (t h q)")[:, 0:2 * SEQ],
                          GQK[:, 0:2].rearrange("p c t -> p (c t)"),
                          GQK[:, 2:4].rearrange("p c t -> p (c t)"), ALU.mult).then_inc(s_prod, 1)
        dve.memset(QP[0][:].rearrange("p c t r j -> p (c t r j)"), 0.0).then_inc(s_qpz, 1)
        level_diff(1)
        b3 = GB[:].rearrange("p c (t j) -> p (c t) j", j=P)
        dve.tensor_tensor(KTI[:].rearrange("p c (t j) -> p (c t) j", j=P),
                          b3[:, :, P - 1:P].to_broadcast([P, 2 * NT, P]), b3, ALU.subtract).then_inc(s_ddk, 1)
        dve.wait_ge(s_gm, 16)
        dve.wait_ge(s_qpz, 1)
        dve.wait_ge(s_dec_e, 1)
        decay_queries(dve, 0, 1).then_inc(s_dec_q, 1)
        dve.wait_ge(s_diag, 1)
        link(dve.tensor_copy(DG[:].rearrange("p t h -> p (t h)"), bank(7)[:, 0:NT * GH]))
        for t in range(NT):
            ins = dve.tensor_tensor(ATT[:, t], ident.unsqueeze(1).to_broadcast([P, GH, P]),
                                   DG[:, t].unsqueeze(2).to_broadcast([P, GH, P]), ALU.mult)
        link(ins)
        dve.wait_ge(s_qpz1, 1)
        for lev, z in enumerate(LEVELS):
            mask = GM[:, lev].bitcast(U32).rearrange("p (n z) -> p n z", z=z)[:, :, z // 2:z]
            for t in range(NT):
                u = lev * NT + t
                if t == 4 and lev + 1 < len(LEVELS):
                    dve.wait_ge(s_dec_e, lev + 2)
                    if lev:
                        dve.wait_ge(s_lv, NT * lev)
                    decay_queries(dve, lev + 1, 1).then_inc(s_dec_q, 1)
                dve.wait_ge(s_lv, u + 1)
                dve.copy_predicated(
                    ATT[:, t].rearrange("p h (n z) -> p h n z", z=z)[:, :, :, z // 2:z],
                    mask.unsqueeze(1).to_broadcast([P, GH, P // z, z // 2]),
                    bank(u % 7)[:, 0:GH * P // 2].rearrange("p (h n z) -> p h n z", h=GH, z=z // 2)
                ).then_inc(s_cp, 1)
            if lev + 2 < len(LEVELS):
                level_diff(lev + 2)
        def scale_output(t):
            dve.wait_ge(s_orms, t + 1)
            dve.wait_ge(s_gain, t + 1)
            for h in range(GH):
                hs = slice(h * P, (h + 1) * P)
                i = t * GH + h
                ins = dve.scalar_tensor_tensor(GZ[:, t, hs], OG[:, t, hs], GSS[:, 2, i:i + 1], GZ[:, t, hs],
                                               ALU.mult, ALU.mult)
            ins.then_inc(s_gend, 1)

        for t in range(NT - 1):
            dve.wait_ge(s_ds, t + 1)
            if t:
                dve.wait_ge(s_o, t)
                dve.wait_ge(s_st, t)
            for ct in range(2):
                for par in range(2):
                    r = slice(64 * par, 64 * par + 64)
                    new, add = GS[r, (t + 1) % 2, ct], bank(2 * (t % 2) + ct)[r, par * P:(par + 1) * P]
                    if t == 0:
                        ins = dve.tensor_copy(new, add)
                    else:
                        ins = dve.scalar_tensor_tensor(new, GS[r, t % 2, ct], GBL[r, ct, t:t + 1], add,
                                                       ALU.mult, ALU.add)
            ins.then_inc(s_st, 1)
            if t >= 1:
                scale_output(t - 1)
        scale_output(NT - 2)
        scale_output(NT - 1)

        for kc in (KC1, KC2):
            dve.memset(kc[:, :, NCMP:NCMP + 1].bitcast(F32), 0.0)
        for u, (kind, h, half) in enumerate(stacks):
            dve.wait_ge(s_qhi, u + 1)
            cols, ps = slice(half * 512, half * 512 + 512), bank(u % 8)
            if kind == "q":
                for par in range(2):
                    ins = dve.tensor_tensor(QS[64:128, 2 * h + par, cols], ps[64 * par:64 * par + 64],
                                            QS[0:64, 2 * h + par, cols].bitcast(F32), ALU.subtract)
            elif kind == "k":
                ins = dve.tensor_tensor(K2[:, h, cols], ps, K1[:, h, cols].bitcast(F32), ALU.subtract)
            else:
                ins = dve.tensor_tensor(KC2[:, :, 0:NCMP],
                                        ps[:, 0:P].rearrange("p (c j) -> p c j", c=2)[:, :, 0:NCMP],
                                        KC1[:, :, 0:NCMP].bitcast(F32), ALU.subtract)
            ins.then_inc(s_qlo, 1)
        dve.wait_ge(s_mk, 16)

        def mask_max(n):
            s, g = divmod(n, GRP)
            kv, qt, br = steps[s]
            nk = span(qt, br)[1]
            m0 = {0: M_CMP + 7 * 8 - 8 * qt, 1: SEQ - nk, 2: M_WIN + WT * P - nk}[br]
            dve.wait_ge(s_qk, n + 1)
            if g == 0 and s >= 6:
                dve.wait_ge(s_pt, first_unit[s - 5])
            ps = PSUM[:, n % 2 * 2:n % 2 * 2 + 2].rearrange("p a b -> p (a b)")[:, 0:nk]
            dve.tensor_tensor_reduce(probs(s)[:, g, 0:nk], ps, MK[:, m0:m0 + nk].bitcast(BF16),
                                     -(DH ** -0.5), 3.0e38, ALU.add, ALU.min,
                                     NM[:, n:n + 1]).then_inc(s_ttr, 1)

        def gate_over_sum(s):
            kv, qt, br = steps[s]
            n = slice(GRP * s, GRP * s + GRP)
            dve.wait_ge(s_exp, GRP * (s + 1))
            link(dve.reciprocal(RG[:, n], SU[:, n]))
            dve.tensor_tensor(RG[:, n], RG[:, n], GT[:, qt, kv * GRP:(kv + 1) * GRP, br],
                              ALU.mult).then_inc(s_rg, 1)

        def scale_dve(n):
            s, g = divmod(n, GRP)
            nk = span(*steps[s][1:])[1]
            dve.wait_ge(s_rg, s + 1)
            x = probs(s)[:, g, 0:nk]
            dve.tensor_scalar(x, x, RG[:, n:n + 1], None, ALU.mult).then_inc(s_normd, 1)

        def tile_lo(u):
            s, i = units[u]
            n = min(P, span(*steps[s][1:])[1])
            dve.wait_ge(s_phi, u + 1)
            dve.tensor_tensor(PTl[0:n, u % 4], bank(4 + u % TRING)[0:n], PTh[0:n, u % 4].bitcast(F32),
                              ALU.subtract).then_inc(s_plo, 1)

        def output_tile(j):
            kv, qt, _ = steps[3 * j]
            dve.wait_ge(s_ob, j + 1)
            o = bank(6 + j % ORING)[0:64].rearrange("p (a r q) -> p a r q", a=2, r=2)
            ob = OB[:].rearrange("p (a r q) -> p a r q", a=2, r=2)
            for par in range(2):
                ins = dve.tensor_tensor(OT[64 * par:64 * par + 64], o[:, :, par], ob[:, :, par], ALU.add)
            ins.then_inc(s_oev, 1)
            dve.wait_ge(s_oev, j + 1)
            z = NZ[:, 2 * kv:2 * kv + 2, qt * P:(qt + 1) * P]
            dve.tensor_tensor(z, z, OT[:], ALU.mult).then_inc(s_nend, 1)

        for kind, n in timeline:
            if kind == "mask_max":
                mask_max(n)
            elif kind == "gate":
                gate_over_sum(n)
            elif kind == "scaleV":
                scale_dve(n)
            elif kind == "low":
                tile_lo(n)
            elif kind == "output":
                output_tile(n)

        for u in range(8):
            cols = slice(u % 2 * 512, u % 2 * 512 + 512)
            dve.wait_ge(s_mhi, u + 1)
            dve.tensor_tensor(MGl[:, u // 2, cols], bank(u), MGh[:, u // 2, cols].bitcast(F32),
                              ALU.subtract).then_inc(s_mlo, 1)
        for m in range(4):
            dve.wait_ge(s_nhi, m + 1)
            dve.tensor_tensor(MNl[:, m], NZ[:, m], MNh[:, m].bitcast(F32), ALU.subtract).then_inc(s_nlo, 1)

        def add_normed(x, t, stats, gain, done):
            link(dve.scalar_tensor_tensor(TMP[:, t % 3], x[:, t], stats[:, 2, t:t + 1], gain[:],
                                          ALU.mult, ALU.mult))
            dve.tensor_tensor(H[:, t], H[:, t], TMP[:, t % 3], ALU.add).then_inc(done, 1)

        def make_h(group):
            dve.wait_ge(s_hr, group + 1)
            for t in range(4 * group, 4 * group + 4):
                add_normed(MIX, t, st, GPO, s_hh)

        def turn_h(group):
            for k in range(KD):
                cols = slice(group * 512, group * 512 + 512)
                dve.wait_ge(s_hhi, KD * group + k + 1)
                dve.tensor_tensor(HTl[:, k, cols], bank(k), HTh[:, k, cols].bitcast(F32),
                                  ALU.subtract).then_inc(s_hlo, 1)

        read_out(cidx["woA"])
        for u in range(4):
            cols = slice(u % 2 * 512, u % 2 * 512 + 512)
            dve.wait_ge(s_pphi, u + 1)
            dve.tensor_tensor(pTl[:, u // 2, cols], bank(4 + u), pTh[:, u // 2, cols].bitcast(F32),
                              ALU.subtract).then_inc(s_pplo, 1)
        dve.wait_ge(s_gn, 32)
        dve.wait_ge(s_h, 16 * NT)
        make_h(0)
        read_out(cidx["woB"])
        turn_h(0)
        make_h(1)
        turn_h(1)
        read_out(cidx["ppA"])
        dve.wait_ge(s_er, 1)
        for t in range(4):
            add_normed(GATE, t, st2, GPL, s_eo)
        read_out(cidx["ppB"])
        for t in range(4, NT):
            dve.wait_ge(s_er, t - 2)
            add_normed(GATE, t, st2, GPL, s_eo)

    ctx.close()


_INS = ["x", "p", "pre_norm", "w_in", "gla_a_up", "gla_a_bias", "gla_out_norm", "cmp_pos_k", "cmp_w1_k",
        "cmp_w2_k", "cmp_pos_v", "cmp_w1_v", "cmp_w2_v", "w_out", "post_norm", "ple_proj", "ple_gate",
        "ple_norm"]


def kernel(**inputs):
    import numpy as _np
    import concourse.bacc as _bacc
    from concourse import mybir as _mybir
    from concourse.bass_utils import run_bass_kernel_spmd as _run

    nc = _bacc.Bacc("TRN2", target_bir_lowering=False, num_devices=1)
    arrays, aps = {}, {}
    named = {n: _np.ascontiguousarray(inputs[n]) for n in _INS}
    named["consts"], named["masks"], named["gla_masks"] = shape_constants()
    for n, v in named.items():
        arrays[f"in_{n}"] = v
        aps[n] = nc.dram_tensor(f"in_{n}", v.shape, _mybir.dt.from_np(v.dtype), kind="ExternalInput").ap()
    aps["out"] = nc.dram_tensor("out_0", (1, SEQ, DM), _mybir.dt.float32, kind="ExternalOutput").ap()
    build_program(nc, aps)
    r = _run(nc, [arrays], core_ids=[0])
    return r.results[0]["out_0"]
```
